# Optimizing a Trainium2 kernel written in Bass

```python
import jax
import jax.numpy as jnp
from jax import lax
import numpy as np

D_MODEL = 1024
BATCH = 1
SEQ = 512
DEPTH = 1

CHUNK = 64
EPS = 1e-6
FFN_DIM = 2816
GLA_HEADS = 4
GLA_DK = D_MODEL // 2
GLA_DV = D_MODEL
GLA_HK = GLA_DK // GLA_HEADS
GLA_HV = GLA_DV // GLA_HEADS
GLA_GK_RANK = 16
GLA_GATE_NORM = 16.0
SSM_D_INNER = 2 * D_MODEL
SSM_HEADDIM = 64
SSM_HEADS = SSM_D_INNER // SSM_HEADDIM
SSM_GROUPS = 8
SSM_HPG = SSM_HEADS // SSM_GROUPS
SSM_DSTATE = 128
SSM_CONV = 4
SSM_CONV_DIM = SSM_D_INNER + 2 * SSM_GROUPS * SSM_DSTATE
ATT_HEADS = 16
ATT_HD = D_MODEL // ATT_HEADS
ATT_W = ATT_HEADS * ATT_HD
ATT_LEFT_CHUNKS = 8
ATT_MAX_REL = 256
N_BRANCH = 3
IN_SIZES = (GLA_DK, GLA_DK, GLA_DV, GLA_DV, GLA_GK_RANK, SSM_D_INNER, SSM_CONV_DIM, SSM_HEADS, ATT_W, ATT_W, ATT_W, N_BRANCH * D_MODEL)
N_IN = sum(IN_SIZES)

kernel_name = 'hybrid_gla_ssd_chunkattn_macaron'

F32 = jnp.float32

def _rmsnorm(x, w):
    xf = x.astype(F32)
    y = xf * lax.rsqrt(jnp.mean(xf * xf, axis=-1, keepdims=True) + EPS)
    return (y * w.astype(F32)).astype(x.dtype)

def _swiglu(x, w_gate, w_up, w_down):
    return (jax.nn.silu(x @ w_gate) * (x @ w_up)) @ w_down

def _in_cols(u, w_in, i):
    start = sum(IN_SIZES[:i])
    return u @ w_in[:, start:start + IN_SIZES[i]]

def _to_chunks(t, n_chunks):
    t = t.reshape((t.shape[0], n_chunks, CHUNK) + t.shape[2:])
    return jnp.moveaxis(t, 1, 0)

def _from_chunks(t):
    t = jnp.moveaxis(t, 0, 1)
    return t.reshape((t.shape[0], t.shape[1] * t.shape[2]) + t.shape[3:])

def _gla(q, k, v, gk):
    bsz, seq = q.shape[:2]
    n_chunks = seq // CHUNK
    xs = tuple(_to_chunks(t, n_chunks) for t in (q, k, v, gk))
    mask = jnp.tril(jnp.ones((CHUNK, CHUNK), bool))

    def step(state, inp):
        qc, kc, vc, gc = inp
        b = jnp.cumsum(gc, axis=1)
        b_last = b[:, -1:]
        b_mid = b[:, CHUNK // 2:CHUNK // 2 + 1]
        a = jnp.einsum('bthd,bshd->bhts', qc * jnp.exp(b - b_mid), kc * jnp.exp(b_mid - b))
        a = jnp.where(mask, a, 0.0)
        o = jnp.einsum('bhts,bshv->bthv', a, vc) + jnp.einsum('bthd,bhdv->bthv', qc * jnp.exp(b), state)
        state = jnp.exp(b_last[:, 0])[..., None] * state + jnp.einsum('bshd,bshv->bhdv', kc * jnp.exp(b_last - b), vc)
        return state, o

    s0 = jnp.zeros((bsz, GLA_HEADS, GLA_HK, GLA_HV), F32)
    _, o = lax.scan(step, s0, xs)
    return _from_chunks(o)

def _ssd(xh, bm, cm, dt, a):
    bsz, seq = xh.shape[:2]
    n_chunks = seq // CHUNK
    xs = tuple(_to_chunks(t, n_chunks) for t in (xh, bm, cm, dt, dt * a))
    mask = jnp.tril(jnp.ones((CHUNK, CHUNK), bool))[None, :, :, None, None]

    def step(state, inp):
        xc, bc, cc, dtc, dac = inp
        cum = jnp.cumsum(dac, axis=1)
        seg = cum[:, :, None] - cum[:, None, :]
        decay = jnp.exp(jnp.where(mask, seg, -jnp.inf))
        cb = jnp.einsum('btgn,bsgn->btsg', cc, bc)
        xdt = xc * dtc[..., None]
        y = jnp.einsum('btsg,btsgr,bsgrp->btgrp', cb, decay, xdt)
        y = y + jnp.einsum('btgn,bgrpn->btgrp', cc, state) * jnp.exp(cum)[..., None]
        to_end = jnp.exp(cum[:, -1:] - cum)
        state = jnp.exp(cum[:, -1])[..., None, None] * state + jnp.einsum('bsgn,bsgrp->bgrpn', bc, xdt * to_end[..., None])
        return state, y

    s0 = jnp.zeros((bsz, SSM_GROUPS, SSM_HPG, SSM_HEADDIM, SSM_DSTATE), F32)
    _, y = lax.scan(step, s0, xs)
    return _from_chunks(y)

def _causal_conv(x, w, b):
    out = lax.conv_general_dilated(x, w.astype(x.dtype)[:, None, :], window_strides=(1,),
                                   padding=[(SSM_CONV - 1, 0)],
                                   dimension_numbers=('NWC', 'WIO', 'NWC'),
                                   feature_group_count=x.shape[-1])
    return out + b.astype(x.dtype)

def _chunk_attention(q, k, v, rel_table):
    seq = q.shape[1]
    n_chunks = seq // CHUNK
    pad = ATT_LEFT_CHUNKS * CHUNK
    band = (ATT_LEFT_CHUNKS + 1) * CHUNK
    kp = jnp.pad(k, ((0, 0), (pad, 0), (0, 0), (0, 0)))
    vp = jnp.pad(v, ((0, 0), (pad, 0), (0, 0), (0, 0)))
    qc = _to_chunks(q, n_chunks)
    rel = jnp.arange(CHUNK)[:, None] + pad - jnp.arange(band)[None, :]
    idx = jnp.clip(rel, -ATT_MAX_REL, ATT_MAX_REL) + ATT_MAX_REL
    bias = jnp.transpose(rel_table[idx], (2, 0, 1)).astype(F32)
    scale = ATT_HD ** -0.5

    def one_chunk(inp):
        c, qb = inp
        start = c * CHUNK
        kb = lax.dynamic_slice_in_dim(kp, start, band, axis=1)
        vb = lax.dynamic_slice_in_dim(vp, start, band, axis=1)
        valid = (start - pad + jnp.arange(band)) >= 0
        s = jnp.einsum('bthd,bshd->bhts', qb, kb).astype(F32) * scale + bias
        s = jnp.where(valid, s, -jnp.inf)
        p = jax.nn.softmax(s, axis=-1).astype(vb.dtype)
        return jnp.einsum('bhts,bshd->bthd', p, vb)

    o = lax.map(one_chunk, (jnp.arange(n_chunks), qc))
    return _from_chunks(o)

def _mixer(u, w_in, gla_w_gk, gla_b_gk, gla_norm, ssm_conv_w, ssm_conv_b, ssm_dt_bias, ssm_A_log, ssm_D,
           ssm_norm, attn_rel_bias, gate_bias, w_branch_gla, w_branch_ssm, w_branch_attn, w_out):
    bsz, seq, _ = u.shape
    q = _in_cols(u, w_in, 0).reshape(bsz, seq, GLA_HEADS, GLA_HK).astype(F32) * GLA_HK ** -0.5
    k = _in_cols(u, w_in, 1).reshape(bsz, seq, GLA_HEADS, GLA_HK).astype(F32)
    v = _in_cols(u, w_in, 2).reshape(bsz, seq, GLA_HEADS, GLA_HV).astype(F32)
    r = _in_cols(u, w_in, 3).reshape(bsz, seq, GLA_HEADS, GLA_HV)
    gk = jax.nn.log_sigmoid((_in_cols(u, w_in, 4) @ gla_w_gk + gla_b_gk).astype(F32)) / GLA_GATE_NORM
    gk = gk.reshape(bsz, seq, GLA_HEADS, GLA_HK)
    o_gla = _gla(q, k, v, gk)
    o_gla = (_rmsnorm(o_gla, gla_norm) * jax.nn.silu(r.astype(F32))).reshape(bsz, seq, GLA_DV).astype(u.dtype)
    y_gla = o_gla @ w_branch_gla
    z = _in_cols(u, w_in, 5)
    xbc = jax.nn.silu(_causal_conv(_in_cols(u, w_in, 6), ssm_conv_w, ssm_conv_b))
    xs_, bm, cm = jnp.split(xbc, [SSM_D_INNER, SSM_D_INNER + SSM_GROUPS * SSM_DSTATE], axis=-1)
    dt = jax.nn.softplus(_in_cols(u, w_in, 7).astype(F32) + ssm_dt_bias.astype(F32))
    dt = dt.reshape(bsz, seq, SSM_GROUPS, SSM_HPG)
    a = -jnp.exp(ssm_A_log.astype(F32)).reshape(SSM_GROUPS, SSM_HPG)
    xh = xs_.reshape(bsz, seq, SSM_GROUPS, SSM_HPG, SSM_HEADDIM).astype(F32)
    bm = bm.reshape(bsz, seq, SSM_GROUPS, SSM_DSTATE).astype(F32)
    cm = cm.reshape(bsz, seq, SSM_GROUPS, SSM_DSTATE).astype(F32)
    y = _ssd(xh, bm, cm, dt, a) + ssm_D.astype(F32).reshape(SSM_GROUPS, SSM_HPG)[..., None] * xh
    y = y.reshape(bsz, seq, SSM_D_INNER) * jax.nn.silu(z.astype(F32))
    y = _rmsnorm(y.reshape(bsz, seq, SSM_GROUPS, SSM_D_INNER // SSM_GROUPS),
                 ssm_norm.reshape(SSM_GROUPS, SSM_D_INNER // SSM_GROUPS))
    y_ssm = y.reshape(bsz, seq, SSM_D_INNER).astype(u.dtype) @ w_branch_ssm
    aq = _in_cols(u, w_in, 8).reshape(bsz, seq, ATT_HEADS, ATT_HD)
    ak = _in_cols(u, w_in, 9).reshape(bsz, seq, ATT_HEADS, ATT_HD)
    av = _in_cols(u, w_in, 10).reshape(bsz, seq, ATT_HEADS, ATT_HD)
    o_att = _chunk_attention(aq, ak, av, attn_rel_bias).reshape(bsz, seq, ATT_W)
    y_att = o_att @ w_branch_attn
    g = jax.nn.sigmoid(_in_cols(u, w_in, 11) + gate_bias).reshape(bsz, seq, N_BRANCH, D_MODEL)
    merged = g[:, :, 0] * y_gla + g[:, :, 1] * y_ssm + g[:, :, 2] * y_att
    return merged.astype(u.dtype) @ w_out

def setup_inputs(seed: int = 0) -> dict:
    key = jax.random.key(seed)
    ks = jax.random.split(key, 32)

    def nrm(k, shape, scale):
        return jax.random.normal(k, shape, F32) * scale

    def gain(k, shape):
        return 1.0 + 0.05 * jax.random.normal(k, shape, F32)

    dt = jnp.exp(jax.random.uniform(ks[10], (DEPTH, SSM_HEADS), F32) * (np.log(0.1) - np.log(0.001)) + np.log(0.001))
    return {
        'x': jax.random.normal(ks[0], (BATCH, SEQ, D_MODEL), F32),
        'ffn1_norm': gain(ks[1], (DEPTH, D_MODEL)),
        'ffn1_w_gate': nrm(ks[2], (DEPTH, D_MODEL, FFN_DIM), D_MODEL ** -0.5),
        'ffn1_w_up': nrm(ks[3], (DEPTH, D_MODEL, FFN_DIM), D_MODEL ** -0.5),
        'ffn1_w_down': nrm(ks[4], (DEPTH, FFN_DIM, D_MODEL), FFN_DIM ** -0.5),
        'mix_norm': gain(ks[5], (DEPTH, D_MODEL)),
        'w_in': nrm(ks[6], (DEPTH, D_MODEL, N_IN), D_MODEL ** -0.5),
        'gla_w_gk': nrm(ks[7], (DEPTH, GLA_GK_RANK, GLA_DK), GLA_GK_RANK ** -0.5),
        'gla_b_gk': nrm(ks[8], (DEPTH, GLA_DK), 0.1),
        'gla_norm': gain(ks[9], (DEPTH, GLA_HV)),
        'ssm_conv_w': nrm(ks[11], (DEPTH, SSM_CONV, SSM_CONV_DIM), SSM_CONV ** -0.5),
        'ssm_conv_b': nrm(ks[12], (DEPTH, SSM_CONV_DIM), 0.02),
        'ssm_dt_bias': dt + jnp.log(-jnp.expm1(-dt)),
        'ssm_A_log': jnp.log(jax.random.uniform(ks[13], (DEPTH, SSM_HEADS), F32, 1.0, 16.0)),
        'ssm_D': gain(ks[14], (DEPTH, SSM_HEADS)),
        'ssm_norm': gain(ks[15], (DEPTH, SSM_D_INNER)),
        'attn_rel_bias': nrm(ks[16], (DEPTH, 2 * ATT_MAX_REL + 1, ATT_HEADS), 0.2),
        'gate_bias': nrm(ks[17], (DEPTH, N_BRANCH * D_MODEL), 0.02),
        'w_branch_gla': nrm(ks[18], (DEPTH, GLA_DV, D_MODEL), GLA_DV ** -0.5),
        'w_branch_ssm': nrm(ks[19], (DEPTH, SSM_D_INNER, D_MODEL), SSM_D_INNER ** -0.5),
        'w_branch_attn': nrm(ks[20], (DEPTH, ATT_W, D_MODEL), ATT_W ** -0.5),
        'w_out': nrm(ks[21], (DEPTH, D_MODEL, D_MODEL), D_MODEL ** -0.5),
        'ffn2_norm': gain(ks[22], (DEPTH, D_MODEL)),
        'ffn2_w_gate': nrm(ks[23], (DEPTH, D_MODEL, FFN_DIM), D_MODEL ** -0.5),
        'ffn2_w_up': nrm(ks[24], (DEPTH, D_MODEL, FFN_DIM), D_MODEL ** -0.5),
        'ffn2_w_down': nrm(ks[25], (DEPTH, FFN_DIM, D_MODEL), FFN_DIM ** -0.5),
        'final_norm': gain(ks[26], (D_MODEL,)),
    }

def reference(x, ffn1_norm, ffn1_w_gate, ffn1_w_up, ffn1_w_down, mix_norm, w_in, gla_w_gk, gla_b_gk, gla_norm,
              ssm_conv_w, ssm_conv_b, ssm_dt_bias, ssm_A_log, ssm_D, ssm_norm, attn_rel_bias, gate_bias,
              w_branch_gla, w_branch_ssm, w_branch_attn, w_out, ffn2_norm, ffn2_w_gate, ffn2_w_up, ffn2_w_down,
              final_norm):
    h = x
    for l in range(DEPTH):
        h = h + 0.5 * _swiglu(_rmsnorm(h, ffn1_norm[l]), ffn1_w_gate[l], ffn1_w_up[l], ffn1_w_down[l])
        h = h + _mixer(_rmsnorm(h, mix_norm[l]), w_in[l], gla_w_gk[l], gla_b_gk[l], gla_norm[l],
                       ssm_conv_w[l], ssm_conv_b[l], ssm_dt_bias[l], ssm_A_log[l], ssm_D[l], ssm_norm[l],
                       attn_rel_bias[l], gate_bias[l], w_branch_gla[l], w_branch_ssm[l], w_branch_attn[l], w_out[l])
        h = h + 0.5 * _swiglu(_rmsnorm(h, ffn2_norm[l]), ffn2_w_gate[l], ffn2_w_up[l], ffn2_w_down[l])
    return _rmsnorm(h, final_norm)


_drawn_inputs = setup_inputs


def setup_inputs(seed=0):
    import zlib

    import numpy as np

    out = dict(_drawn_inputs(seed))
    spreads = {}
    factors = {'gla_b_gk': 4.935,
     'gla_norm': 3.981,
     'ssm_conv_b': 4.513,
     'ssm_D': 4.498,
     'attn_rel_bias': 5.547,
     'gate_bias': 8.0,
     'ffn2_norm': 3.284}
    for name, (base, spread) in spreads.items():
        noise = np.random.default_rng([zlib.crc32(name.encode()), seed]).standard_normal(out[name].shape)
        drawn = base * np.exp(spread * noise) if base else spread * noise
        out[name] = jnp.asarray(drawn.astype(out[name].dtype))
    for name, factor in factors.items():
        out[name] = (out[name] * factor).astype(out[name].dtype)
    return out
```

```python
from contextlib import ExitStack

import numpy as np
import concourse.bass as bass
from concourse import mybir

F32 = mybir.dt.float32
F32R = mybir.dt.float32r
ALU = mybir.AluOpType
ACT = mybir.ActivationFunctionType

P = 128
T = 512
D = 1024
KT = D // P
FFN = 2816
FT = FFN // P
TT = T // P
CH = 64
NCH = T // CH
HG = 4
NG = 8
HPG = 4
HS = NG * HPG
NQ = 4
EPS = 1e-6
GLA_SCALE = 128 ** -0.5
GATE_NORM = 16.0
ATT_SCALE = 64 ** -0.5
MASKED = -1.0e30
SLAB = 1024
RING = 3

N_FFN1 = 0
N_DOWN1 = N_FFN1 + 2 * FT
N_SMALL = N_DOWN1 + 3 * KT
N_SSM = N_SMALL + 1
N_MERGE1 = N_SSM + 6 * NG
N_GLA = N_MERGE1 + 3 * KT
N_ATT = N_GLA + 6 * HG
N_MERGE2 = N_ATT + 6 * NQ
N_OUT = N_MERGE2 + 4 * KT
N_FFN2 = N_OUT + KT
N_DOWN2 = N_FFN2 + 2 * FT
N_SLABS = N_DOWN2 + 3 * KT
DOWN_K = ((0, 8), (8, 15), (15, 22))

W_SSM, W_GLA, W_ATT = 3, 3 + 6 * NG, 3 + 6 * NG + 6 * HG

C_N1, C_NM, C_N2, C_NF, C_GN, C_GB, C_GATE, C_DTB, C_CONV, C_GRP = 0, 8, 16, 24, 32, 34, 38, 62, 64, 224
C_ALOG = C_GRP + 6 * NG
NCST = C_ALOG + HS


class At:

    def __init__(self, k, i=0, per=0):
        self.k, self.i, self.per = k, i, per

    def __add__(self, d):
        return At(self.k + d, self.i, self.per)

    @property
    def value(self):
        return self.k + self.per * self.i if self.per else self.k

    @property
    def slot(self):
        return self.k % RING

    @property
    def turn(self):
        return self.k // RING + ((self.per // RING) * self.i if self.per else 0)


ROUND = {
    "scalar": {
        "conv_begun": 4, "conv_tanh": 4, "x_copied": 1, "b_copied": 1, "decay_exp": 1, "z_tanh": 2,
        "ssm_squares": 4, "ssm_hi": 2,
        "gla_exp": 1, "gla_kt_copied": 1, "gla_r_tanh": 2, "gla_squares": 4, "gla_hi": 2,
        "att_p": 4, "att_pt_a": 4, "att_hi": 2,
    },
    "vector": {
        "conv_const": 1, "group_const": 1, "da_masked": 1, "xdt_ready": 1, "xte_ready": 1, "cb_masked": 1,
        "m_ready": 1, "conv_done": 4, "ssm_chain": 13, "ssm_y": 4, "ssm_var": 1, "ssm_scaled": 4, "ssm_lo": 2,
        "gla_t": 2, "gla_qh": 1, "gla_qt": 1, "gla_kh": 1, "gla_a_masked": 1, "gla_chain": 7, "gla_var": 1,
        "gla_o_ready": 4, "gla_lo": 2,
        "att_scored": 16, "att_neg": 4, "att_recip": 4, "att_pt_b": 8, "att_o": 4, "att_lo": 2,
    },
    "gpsimd": {"xd_ready": 1, "ssm_rstd": 1, "gla_rstd": 1},
    "tensor": {
        "xb_turned": 1, "seg_done": 1, "cb_done": 1, "u_done": 2, "intra_done": 1, "inter_done": 1,
        "ssm_turned": 1,
        "gla_a_done": 1, "gla_kt_turned": 1, "gla_u_done": 2, "gla_o_done": 1, "gla_turned": 1,
        "att_s": 4, "att_turned": 4, "att_pv": 4, "att_o_turned": 1,
    },
}
PER = {name: k for sems in ROUND.values() for name, k in sems.items()}


def after(name, r, j=0):
    return PER[name] * (r + 1) + j + 1


def last(name, r):
    return PER[name] * (r + 1) + PER[name] if not isinstance(r, int) or r >= 0 else PER[name]


def build(nc, a, out):
    ctx = ExitStack()
    with ctx:
        def sb(name, shape, dt=F32, stack=None):
            return (stack or ctx).enter_context(nc.sbuf_tensor(name, shape, dt))

        h = sb("h", [P, KT, T])
        UH = sb("UH", [P, KT, T], F32R)
        UL = sb("UL", [P, KT, T], F32R)
        RAW = sb("RAW", [P, RING, SLAB])
        WH = sb("WH", [P, RING, SLAB], F32R)
        WL = sb("WL", [P, RING, SLAB], F32R)
        cst = sb("cst", [P, NCST])
        half_gate_bias = sb("half_gate_bias", [P, 3 * KT])
        ident = sb("ident", [P, P])
        ones = sb("ones", [P, P])
        after_s = sb("after_s", [P, P])
        upto_t = sb("upto_t", [P, P])
        causal = sb("causal", [P, CH])
        minus_half = sb("minus_half", [P, TT])
        LR = sb("LR", [16, T])
        var4 = sb("var4", [P, TT])
        rstd4 = sb("rstd4", [P, TT])
        SC = sb("SC", [P, 24, HS])
        gconv = sb("gconv", [P, 20])
        ggrp = sb("ggrp", [P, 6])
        gsc = sb("gsc", [P, 24, HPG])
        minus_a = sb("minus_a", [P, HS])
        ut = sb("ut", [P, 2, T])
        gate_th = ut
        WGK = sb("WGK", [16, 512])
        dump = sb("dump", [P, 256])

        r = ExitStack()
        acc = sb("acc", [P, T], F32, r)
        sq = sb("sq", [P, 2, T], F32, r)
        diag = sb("diag", [P, TT, P], F32, r)
        HH = sb("HH", [P, FT, T], F32R, r)
        HL = sb("HL", [P, FT, T], F32R, r)
        gate_act = sb("gate_act", [P, RING, T], F32, r)
        hid = gate_act
        r.close()

        r = ExitStack()
        SH = sb("SH", [P, 2 * NG, T], F32R, r)
        SL = sb("SL", [P, 2 * NG, T], F32R, r)
        w = ExitStack()
        XT = sb("XT", [P, 2, T], F32, w)
        BT = sb("BT", [P, T], F32, w)
        CT = sb("CT", [P, T], F32, w)
        CV = sb("CV", [P, 2, T], F32, w)
        TH = sb("TH", [P, 2, T], F32, w)
        ZS = sb("ZS", [P, TT, 256], F32, w)
        XDT = sb("XDT", [P, TT, 256], F32, w)
        XTE = sb("XTE", [P, TT, 256], F32, w)
        XD = sb("XD", [P, TT, 256], F32, w)
        BK = sb("BK", [P, TT, P], F32, w)
        M = sb("M", [P, TT, HPG, CH], F32, w)
        CBM = sb("CBM", [P, TT, CH], F32, w)
        SS = sb("SS", [P, NCH, 256], F32, w)
        ST = sb("ST", [P, 256], F32, w)
        Y = sb("Y", [P, TT, 256], F32, w)
        ss4 = sb("ss4", [P, TT], F32, w)
        w.close()
        w = ExitStack()
        dtv = sb("dtv", [P, 7, T], F32, w)
        w.close()
        r.close()

        r = ExitStack()
        GH = sb("GH", [P, KT, T], F32R, r)
        GL = sb("GL", [P, KT, T], F32R, r)
        w = ExitStack()
        BB = sb("BB", [P, HG, T], F32, w)
        EX = sb("EX", [P, 4, T], F32, w)
        TB = sb("TB", [P, 2, T], F32, w)
        QR = sb("QR", [P, T], F32, w)
        QH = sb("QH", [P, T], F32, w)
        QT = sb("QT", [P, T], F32, w)
        KH = sb("KH", [P, T], F32, w)
        KT_ = sb("KT_", [P, T], F32, w)
        RM = sb("RM", [P, T], F32, w)
        w.close()
        AH = sb("AH", [P, KT, T], F32R, r)
        AL = sb("AL", [P, KT, T], F32R, r)
        merged = sb("merged", [P, KT, T], F32, r)
        w = ExitStack()
        KK = sb("KK", [P, TT, P], F32, w)
        GV = sb("GV", [P, TT, 256], F32, w)
        GR = sb("GR", [P, TT, 256], F32, w)
        GTH = sb("GTH", [P, 2, T], F32, w)
        GA = sb("GA", [P, TT, CH], F32, w)
        GS = sb("GS", [P, NCH, 256], F32, w)
        GO = sb("GO", [P, TT, 256], F32, w)
        EL = sb("EL", [P, NCH], F32, w)
        gss4 = sb("gss4", [P, TT], F32, w)
        w.close()
        w = ExitStack()
        AQ = sb("AQ", [P, 2, 2, T], F32, w)
        AK = sb("AK", [P, 2, 2, T], F32, w)
        AV = sb("AV", [P, TT, 256], F32, w)
        bias = sb("bias", [P, 2, T], F32, w)
        PR = sb("PR", [P, 1280], F32, w)
        PT = sb("PT", [P, 1280], F32, w)
        AO = sb("AO", [P, TT, 256], F32, w)
        mx = sb("mx", [P, TT], F32, w)
        ngm = sb("ngm", [P, TT], F32, w)
        rs = sb("rs", [P, TT], F32, w)
        rc = sb("rc", [P, TT], F32, w)
        w.close()
        w = ExitStack()
        MH = sb("MH", [P, KT, T], F32R, w)
        ML = sb("ML", [P, KT, T], F32R, w)
        MT = sb("MT", [P, 2, T], F32, w)
        w.close()
        r.close()
        G = ctx.enter_context(nc.psum_tensor("G", [P, 3, T], F32))
        I01 = ctx.enter_context(nc.psum_tensor("I01", [P, 2 * T], F32))
        I2 = ctx.enter_context(nc.psum_tensor("I2", [P, T], F32))
        I34 = ctx.enter_context(nc.psum_tensor("I34", [P, 2 * T], F32))

        sems = {}

        def sem(name):
            sems[name] = ctx.enter_context(nc.semaphore(name))
            return sems[name]

        slab_landed = [sem(f"slab_landed{s}") for s in range(RING)]
        split_hi, split_lo, slab_done = sem("split_hi"), sem("split_lo"), sem("slab_done")
        g_free = [sem(f"g_free{s}") for s in range(3)]
        gate_ready, hid_ready, hh_ready, hl_ready = sem("gate_ready"), sem("hid_ready"), sem("hh_ready"), sem("hl_ready")
        h_updated, squared, acc_updated = sem("h_updated"), sem("squared"), sem("acc_updated")
        acc_clear = sem("acc_clear")
        norm_sums, norm_var, norm_rstd, norm_diag, norm_bc = (
            sem("norm_sums"), sem("norm_var"), sem("norm_rstd"), sem("norm_diag"), sem("norm_bc"))
        ut_ready, uh_ready, ul_ready = sem("ut_ready"), sem("uh_ready"), sem("ul_ready")
        x_landed, cst_landed, wgk_landed = sem("x_landed"), sem("cst_landed"), sem("wgk_landed")
        consts, half_bias = sem("consts"), sem("half_bias")
        m_gate, m_y, m_sum, m_final, mh_ready, ml_ready = (
            sem("m_gate"), sem("m_y"), sem("m_sum"), sem("m_final"), sem("mh_ready"), sem("ml_ready"))
        out_ready, stored = sem("out_ready"), sem("stored")
        dt_act, dt_dve, dt_pe = sem("dt_act"), sem("dt_dve"), sem("dt_pe")
        gk_act, gk_dve, gk_pe, gk_pool = sem("gk_act"), sem("gk_dve"), sem("gk_pe"), sem("gk_pool")
        bias_landed = [sem(f"bias_landed{s}") for s in range(2)]
        bias_masked = sem("bias_masked")
        taps = sem("taps")
        for group in ROUND.values():
            for name in group:
                sem(name)

        def inc(ins, name):
            return ins.then_inc(sems[name], 1)

        HID0, GATE0, RES0, PAIR0 = 2, 1, 2, 1

        def update(c):
            bank, k = c % 2, c // 2 % 2
            return (I01, I34)[c // 4][:, bank * T + k * 256:bank * T + (k + 1) * 256]

        def bc(ap, n):
            return ap.unsqueeze(len(ap.shape)).to_broadcast(list(ap.shape) + [n])

        block = ctx.enter_context(nc.Block())

        @block.sync
        def _(sp):
            sp.dma_start(cst[:], a["cst"]).then_inc(cst_landed, 16)
            sp.dma_start(WGK[:], a["wgk"]).then_inc(wgk_landed, 16)
            slabs = a["slabs"]

            def load(n):
                sp.dma_start(RAW[:, n.slot:n.slot + 1, :],
                             slabs[bass.ds(n.value, 1)].rearrange("s p c -> p s c")
                             ).then_inc(slab_landed[n.slot], 16)

            for n in range(RING):
                load(At(n))
                if n == 0:
                    sp.dma_start(h[:, 0:4, :], a["x"][:, 0:4, :]).then_inc(x_landed, 16)
                    sp.dma_start(h[:, 4:8, :], a["x"][:, 4:8, :]).then_inc(x_landed, 16)
            with sp.Fori(1, N_SLABS // RING) as i:
                for j in range(RING):
                    n = At(j, i, RING)
                    sp.wait_ge(split_lo, n.value - (RING - 1))
                    load(n)
            for n in range(N_SLABS // RING * RING, N_SLABS):
                sp.wait_ge(split_lo, n - (RING - 1))
                load(At(n))

        @block.gpsimd
        def _(pool):
            for name, k in ROUND["gpsimd"].items():
                pool.sem_inc(sems[name], k)
            step = [0]

            def link(ins):
                step[0] += 1
                ins.then_inc(consts, 1)
                pool.wait_ge(consts, step[0])

            link(nc.gpsimd.memset(ones[:], 1.0))
            link(nc.gpsimd.memset(minus_half[:], -0.5))
            link(nc.gpsimd.memset(ident[:], 0.0))
            link(nc.gpsimd.affine_select(out=ident[:], in_=ident[:], compare_op=ALU.not_equal, fill=1.0, base=0,
                                         pattern=[[-1, P]], channel_multiplier=1))
            link(nc.gpsimd.affine_select(out=after_s[:], in_=ones[:], compare_op=ALU.is_gt, fill=0.0, base=0,
                                         pattern=[[-1, P]], channel_multiplier=1))
            link(nc.gpsimd.memset(after_s[CH:P, 0:CH], 0.0))
            link(nc.gpsimd.affine_select(out=upto_t[:], in_=ones[:], compare_op=ALU.is_ge, fill=0.0, base=0,
                                         pattern=[[1, P]], channel_multiplier=-1))
            link(nc.gpsimd.memset(upto_t[0:CH, CH:P], 0.0))
            link(nc.gpsimd.tensor_copy(causal[0:CH, :], upto_t[0:CH, 0:CH]))
            link(nc.gpsimd.tensor_copy(causal[CH:P, :], upto_t[CH:P, CH:P]))
            assert step[0] == N_CONSTS

            def norm(k):
                pool.wait_ge(norm_var, k + 1)
                nc.gpsimd.tensor_tensor(rstd4[:], var4[:], minus_half[:], ALU.pow).then_inc(norm_rstd, 1)

            def ssm(g):
                pool.wait_ge(sems["xte_ready"], after("xte_ready", g))
                pool.wait_ge(sems["group_const"], after("group_const", g))
                d = ggrp[:, 2:6].unsqueeze(1).unsqueeze(3).to_broadcast([P, TT, HPG, CH])
                x4 = XD[:].rearrange("p j (r c) -> p j r c", r=HPG)
                inc(nc.gpsimd.tensor_tensor(x4, x4, d, ALU.mult), "xd_ready")
                pool.wait_ge(sems["ssm_var"], after("ssm_var", g))
                inc(nc.gpsimd.tensor_tensor(rstd4[:], var4[:], minus_half[:], ALU.pow), "ssm_rstd")

            def gla(hd):
                pool.wait_ge(sems["gla_var"], after("gla_var", hd))
                inc(nc.gpsimd.tensor_tensor(rstd4[:], var4[:], minus_half[:], ALU.pow), "gla_rstd")

            norm(0)
            norm(1)
            with pool.Fori(0, NG) as i:
                ssm(i)
            pool.wait_ge(m_y, PAIR0 + KT)
            nc.gpsimd.memset(RM[:], 1.0).then_inc(gk_pool, 1)
            pool.wait_ge(gk_pool, 1)
            nc.gpsimd.memset(RM[:].rearrange("p (c t) -> p c t", t=CH)[:, :, 0:1], 0.0).then_inc(gk_pool, 1)
            for hd in range(HG):
                gla(hd)
            pool.wait_ge(sems["gla_turned"], last("gla_turned", HG - 1))
            for s in range(2):
                nc.gpsimd.memset(bias[0:CH, s, T - CH:T], MASKED).then_inc(bias_masked, 1)
            norm(2)
            norm(3)

        @block.tensor
        def _(pe):
            for name, k in ROUND["tensor"].items():
                pe.sem_inc(sems[name], k)
            mm = nc.tensor.matmul

            def need_slab(n):
                pe.wait_ge(split_lo, n.value + 1)

            def blocks(dst, n, k0, k1, RH, RL, begin, end):
                last_ins = None
                for which, (W, R) in enumerate(((WH, RH), (WH, RL), (WL, RH))):
                    for k in range(k0, k1):
                        last_ins = mm(dst, W[:, n.slot, (k - k0) * P:(k - k0 + 1) * P], R[:, k, :],
                                      start=begin and which == 0 and k == k0,
                                      stop=end and which == 2 and k == k1 - 1)
                return last_ins

            def fm(dst, n, RH, RL):
                need_slab(n)
                blocks(dst, n, 0, KT, RH, RL, True, True).then_inc(slab_done, 1)

            def fm_pass(dst, n, which):
                if which == 0:
                    need_slab(n)
                W, R = ((WH, UH), (WH, UL), (WL, UH))[which]
                for k in range(KT):
                    ins = mm(dst, W[:, n.slot, k * P:(k + 1) * P], R[:, k, :],
                             start=which == 0 and k == 0, stop=which == 2 and k == KT - 1)
                if which == 2:
                    ins.then_inc(slab_done, 1)

            def tm_tile(n, j):
                if j == 0:
                    need_slab(n)
                    need_slab(n + 1)
                dst = G[:, (n + j // 2).slot, (j % 2) * 256:(j % 2 + 1) * 256]
                for which, (U, W) in enumerate(((UH, WH), (UL, WH), (UH, WL))):
                    for k in range(KT):
                        ins = mm(dst, U[:, k, j * P:(j + 1) * P],
                                 W[:, (n + k // 4).slot, (k % 4) * 256:(k % 4 + 1) * 256],
                                 start=which == 0 and k == 0, stop=which == 2 and k == KT - 1)
                if j == TT - 1:
                    ins.then_inc(slab_done, 2)

            def bank_free(wn):
                pe.wait_ge(g_free[wn.slot], wn.turn)

            def bank_read(wn):
                pe.wait_ge(g_free[wn.slot], wn.turn + 1)

            def norm(k):
                pe.wait_ge(acc_updated, RES0 + 8 * k + 8)
                if k == 0:
                    pe.wait_ge(consts, N_CONSTS)
                for j in range(TT):
                    ins = mm(I2[:, j:j + 1], acc[:, j * P:(j + 1) * P], ones[:, 0:1], start=True, stop=True)
                ins.then_inc(norm_sums, 1)
                pe.wait_ge(norm_diag, k + 1)
                mm(I34[:, 0:T], ones[:], diag[:].rearrange("p j t -> p (j t)"), start=True,
                   stop=True).then_inc(norm_bc, 1)

            def ffn(f):
                n0, nd = (N_FFN1, N_DOWN1) if f == 0 else (N_FFN2, N_DOWN2)
                pe.wait_ge(ul_ready, 8 * (2 * f + 1))

                def tile(ft, n):
                    pe.wait_ge(hid_ready, FT * f + ft + 1)
                    fm(G[:, n.slot, :], n, UH, UL)
                    pe.wait_ge(gate_ready, FT * f + ft + 1)
                    fm(G[:, (n + 1).slot, :], n + 1, UH, UL)

                with pe.Fori(0, FT // 3) as i:
                    for t in range(3):
                        tile(3 * i + t, At(n0 + 2 * t, i, 6))
                tile(FT - 1, At(n0 + 2 * (FT - 1)))

                with pe.Fori(0, KT // 2) as i:
                    for t in range(2):
                        pe.wait_ge(h_updated, 8 * (0, 2)[f] + 2 * i + t + 1)
                        for c, (k0, k1) in enumerate(DOWN_K):
                            n = At(nd + 3 * t + c, i, 6)
                            need_slab(n)
                            pe.wait_ge(hl_ready, FT * f + k1)
                            blocks(I01[:, t * T:(t + 1) * T], n, k0, k1, HH, HL, c == 0,
                                   c == 2).then_inc(slab_done, 1)

            def half(c):
                return slice(CH * (c % 2), CH * (c % 2) + CH)

            def dt_prep():
                pe.wait_ge(dt_dve, DT_READY)
                for j in range(TT):
                    ins = nc.tensor.transpose(I01[:, j * 32:(j + 1) * 32], dtv[32:64, 6, j * P:(j + 1) * P],
                                              ident[32:64, 32:64])
                ins.then_inc(dt_pe, 1)
                pe.wait_ge(dt_dve, DA_READY)
                da = SC[:, 0:4, :].rearrange("p j h -> p (j h)")
                mm(I01[:, T:T + 128], upto_t[:], da, start=True, stop=True)
                mm(I01[:, T + 128:T + 256], after_s[:], da, start=True, stop=True)
                for c in range(NCH):
                    dst = I2[:, 32 * (c // 2):32 * (c // 2) + 32] if c % 2 else \
                        I01[:, T + 256 + 16 * c:T + 288 + 16 * c]
                    ins = mm(dst, ones[half(c), :], SC[half(c), c // 2, :], start=True, stop=True)
                ins.then_inc(dt_pe, 1)

            def ssm_turn(g):
                pe.wait_ge(sems["conv_done"], last("conv_done", g))
                pe.wait_ge(sems["ssm_lo"], last("ssm_lo", g - 1))
                pe.wait_ge(sems["cb_masked"], last("cb_masked", g - 1))
                for j in range(TT):
                    for f in range(2):
                        nc.tensor.transpose(I01[:, j * 256 + f * P:j * 256 + (f + 1) * P],
                                            XT[:, f, j * P:(j + 1) * P], ident[:])
                for j in range(TT):
                    ins = nc.tensor.transpose(I2[:, j * P:(j + 1) * P], BT[:, j * P:(j + 1) * P], ident[:])
                inc(ins, "xb_turned")
                pe.wait_ge(sems["da_masked"], after("da_masked", g))
                pe.wait_ge(sems["ssm_y"], last("ssm_y", g - 1))
                rhs = M[:].rearrange("p j r t -> p (j r t)")
                for s in range(2):
                    ins = mm(I34[:, s * T:(s + 1) * T], after_s[:], rhs[:, s * T:(s + 1) * T], start=True, stop=True)
                inc(ins, "seg_done")

            def ssm_cb_u(g):
                pe.wait_ge(sems["b_copied"], after("b_copied", g))
                for c in range(NCH):
                    ins = mm(I2[half(c), (c // 2) * CH:(c // 2 + 1) * CH], BT[:, c * CH:(c + 1) * CH],
                             CT[:, c * CH:(c + 1) * CH], start=True, stop=True)
                inc(ins, "cb_done")
                pe.wait_ge(sems["xte_ready"], after("xte_ready", g))
                pe.wait_ge(sems["x_copied"], after("x_copied", g))
                for c in range(4):
                    ins = mm(update(c), BK[half(c), c // 2, :], XTE[half(c), c // 2, :],
                             start=True, stop=True)
                inc(ins, "u_done")
                pe.wait_ge(sems["decay_exp"], after("decay_exp", g))
                for c in range(4, 7):
                    ins = mm(update(c), BK[half(c), c // 2, :], XTE[half(c), c // 2, :],
                             start=True, stop=True)
                inc(ins, "u_done")

            def ssm_intra():
                for c in range(NCH):
                    j, s = c // 2, half(c)
                    for rr in range(HPG):
                        ins = mm(I01[s, j * 256 + rr * CH:j * 256 + (rr + 1) * CH], M[s, j, rr, :],
                                 XDT[s, j, rr * CH:(rr + 1) * CH], start=True, stop=True)
                inc(ins, "intra_done")

            def ssm_inter(g):
                pe.wait_ge(sems["m_ready"], after("m_ready", g))
                pe.wait_ge(sems["ssm_chain"], last("ssm_chain", g))
                for c in range(NCH):
                    ins = mm(I34[half(c), (c // 2) * 256:(c // 2 + 1) * 256], CT[:, c * CH:(c + 1) * CH],
                             SS[:, c, :], start=True, stop=True)
                inc(ins, "inter_done")

            def turn_back(src, dst, ready, g, done):
                pe.wait_ge(sems[ready], last(ready, g))
                for f in range(2):
                    for j in range(TT):
                        ins = nc.tensor.transpose(dst[:, f * T + j * P:f * T + (j + 1) * P],
                                                  src[:, j, f * P:(f + 1) * P], ident[:])
                inc(ins, done)

            def project(n, wn, kinds, between):
                t = 0
                for kind in kinds:
                    if kind == "fm":
                        bank_free(wn + t)
                        fm(G[:, (wn + t).slot, :], n + t, UH, UL)
                        t += 1
                    else:
                        bank_free(wn + t)
                        bank_free(wn + t + 1)
                        for j in range(TT):
                            tm_tile(n + t, j)
                        t += 2
                    if t in between:
                        between[t]()

            def merge(b_slabs, n, q, RH, RL, k_slabs):
                pe.wait_ge(m_gate, PAIR0 + q)
                fm(I01[:, 0:T], n, UH, UL)
                pe.wait_ge(m_y, PAIR0 + q)
                for s in range(k_slabs):
                    need_slab(n + 1 + s)
                    m_dst = I01[:, T:2 * T]
                    nn = n + 1 + s
                    blocks_off(m_dst, nn, s * KT, RH, RL, s == 0, s == k_slabs - 1).then_inc(slab_done, 1)

            def blocks_off(dst, n, k0, RH, RL, begin, end):
                return blocks(dst, n, k0, k0 + KT, RH, RL, begin, end)

            norm(0)
            ffn(0)
            norm(1)
            pe.wait_ge(ul_ready, 16)
            fm(G[:, 0, :], At(N_SMALL), UH, UL)
            dt_prep()

            SSM_KINDS = ("fm", "fm", "fm", "fm", "tm")
            project(At(N_SSM), At(W_SSM), SSM_KINDS, {})
            with pe.Fori(0, NG - 1) as i:
                project(At(N_SSM + 6, i, 6), At(W_SSM + 6, i, 6), SSM_KINDS, {
                    1: lambda: ssm_turn(i), 2: lambda: ssm_cb_u(i), 4: lambda: (ssm_inter(i), ssm_intra()),
                    6: lambda: turn_back(Y, I01, "ssm_scaled", i, "ssm_turned")})
            g = NG - 1
            ssm_turn(g)
            ssm_cb_u(g)
            ssm_inter(g)
            ssm_intra()
            turn_back(Y, I01, "ssm_scaled", g, "ssm_turned")

            pe.wait_ge(sems["ssm_lo"], last("ssm_lo", NG - 1))
            with pe.Fori(0, KT // 2) as i:
                for t in range(2):
                    merge(1, At(N_MERGE1 + 3 * t, i, 6), 2 * i + t, SH, SL, 2)

            def gla_a_u(hd):
                pe.wait_ge(sems["gla_qh"], after("gla_qh", hd))
                bank_read(At(W_GLA + 6 * hd + 3))
                for c in range(NCH):
                    ins = mm(I2[half(c), (c // 2) * CH:(c // 2 + 1) * CH], KH[:, c * CH:(c + 1) * CH],
                             QH[:, c * CH:(c + 1) * CH], start=True, stop=True)
                inc(ins, "gla_a_done")
                pe.wait_ge(sems["gla_lo"], last("gla_lo", hd - 1))
                for j in range(TT):
                    ins = nc.tensor.transpose(I34[:, j * P:(j + 1) * P], KT_[:, j * P:(j + 1) * P], ident[:])
                inc(ins, "gla_kt_turned")
                pe.wait_ge(sems["gla_kt_copied"], after("gla_kt_copied", hd))
                for s in range(2):
                    bank_read(At(W_GLA + 6 * hd + 1 + s))
                pe.wait_ge(sems["gla_o_ready"], last("gla_o_ready", hd - 1))
                for c in range(4):
                    ins = mm(update(c), KK[half(c), c // 2, :], GV[half(c), c // 2, :],
                             start=True, stop=True)
                inc(ins, "gla_u_done")
                for c in range(4, 7):
                    ins = mm(update(c), KK[half(c), c // 2, :], GV[half(c), c // 2, :],
                             start=True, stop=True)
                inc(ins, "gla_u_done")

            def gla_o(hd):
                pe.wait_ge(sems["gla_a_masked"], after("gla_a_masked", hd))
                pe.wait_ge(sems["gla_chain"], last("gla_chain", hd))
                pe.wait_ge(sems["gla_qt"], after("gla_qt", hd))
                for c in range(NCH):
                    j, s = c // 2, half(c)
                    dst = I01[s, j * 256:(j + 1) * 256]
                    mm(dst, GA[s, j, :], GV[s, j, :], start=True, stop=False)
                    ins = mm(dst, QT[:, c * CH:(c + 1) * CH], GS[:, c, :], start=False, stop=True)
                inc(ins, "gla_o_done")

            pe.wait_ge(m_y, PAIR0 + KT)
            pe.wait_ge(wgk_landed, 16)
            for hd in range(HG):
                dst = (I01[:, 0:T], I01[:, T:], I34[:, 0:T], I34[:, T:])[hd]
                ins = mm(dst, WGK[:, hd * P:(hd + 1) * P], LR[:], start=True, stop=True)
            ins.then_inc(gk_pe, 1)
            GLA_KINDS = ("fm", "tm", "fm", "tm")
            project(At(N_GLA), At(W_GLA), GLA_KINDS, {})
            pe.wait_ge(gk_dve, GK_EVICTED)
            for hd in range(HG - 1):
                project(At(N_GLA + 6 * (hd + 1)), At(W_GLA + 6 * (hd + 1)), GLA_KINDS, {
                    1: lambda: gla_a_u(hd), 3: lambda: gla_o(hd),
                    6: lambda: turn_back(GO, I34, "gla_o_ready", hd, "gla_turned")})
            hd = HG - 1
            gla_a_u(hd)
            gla_o(hd)
            turn_back(GO, I34, "gla_o_ready", hd, "gla_turned")

            def att_s(q, e):
                f, s, par = e // 2, slice(CH * (e % 2), CH * (e % 2) + CH), q % 2
                if e == 0:
                    for t in range(4):
                        bank_read(At(W_ATT + 6 * q + t))
                    if q == 0:
                        pe.wait_ge(sems["gla_lo"], last("gla_lo", HG - 1))
                pe.wait_ge(sems["att_o"], after("att_o", q, e - 1))
                for i in (3, 2, 0, 1):
                    dst = {3: I01[:, 0:512], 2: I01[:, 512:896], 0: I01[:, 896:1024], 1: I2[:, 0:256]}[i]
                    ins = mm(dst, AQ[s, par, f, i * P:(i + 1) * P], AK[s, par, f, 0:(i + 1) * P],
                             start=True, stop=True)
                inc(ins, "att_s")

            def att_turn(q, e):
                pe.wait_ge(sems["att_p"], after("att_p", q, e))
                if q == 0 and e == 0:
                    pass
                elif e == 0:
                    pe.wait_ge(sems["att_lo"], last("att_lo", q - 1))
                else:
                    pe.wait_ge(sems["att_pt_b"], after("att_pt_b", q, 2 * (e - 1) + 1))
                    pe.wait_ge(sems["att_pt_a"], after("att_pt_a", q, e - 1))
                for i in range(TT):
                    for b in range(i + 1):
                        col = PT_OFF[b] + (i - b) * P
                        dst = I34[:, col:col + P] if b != 2 else I2[:, 256 + (i - b) * P:256 + (i - b + 1) * P]
                        ins = nc.tensor.transpose(dst, PR[:, P_OFF[i] + b * P:P_OFF[i] + (b + 1) * P], ident[:])
                inc(ins, "att_turned")

            def att_pv(q, e):
                if e == 0:
                    for t in (4, 5):
                        bank_read(At(W_ATT + 6 * q + t))
                pe.wait_ge(sems["att_pt_a"], after("att_pt_a", q, e))
                pe.wait_ge(sems["att_pt_b"], after("att_pt_b", q, 2 * e + 1))
                for i in range(TT):
                    for b in range(i + 1):
                        col = PT_OFF[b] + (i - b) * P
                        ins = mm(I01[:, i * CH:(i + 1) * CH], PT[:, col:col + P], AV[:, b, e * CH:(e + 1) * CH],
                                 start=b == 0, stop=b == i)
                inc(ins, "att_pv")

            def att_part(q, k):
                n, wn = At(N_ATT + 6 * q), At(W_ATT + 6 * q)
                if k < 12:
                    t, which = k // 3, k % 3
                    if which == 0:
                        bank_free(wn + t)
                    fm_pass(G[:, (wn + t).slot, :], n + t, which)
                else:
                    if k == 12:
                        bank_free(wn + 4)
                        bank_free(wn + 5)
                    tm_tile(n + 4, k - 12)

            for k in range(16):
                att_part(0, k)
            for q in range(NQ):
                for e in range(4):
                    att_s(q, e)
                    if q + 1 < NQ:
                        att_part(q + 1, 4 * e)
                        att_part(q + 1, 4 * e + 1)
                    att_turn(q, e)
                    if q + 1 < NQ:
                        att_part(q + 1, 4 * e + 2)
                    att_pv(q, e)
                    if q + 1 < NQ:
                        att_part(q + 1, 4 * e + 3)
                turn_back(AO, I34, "att_o", q, "att_o_turned")

            pe.wait_ge(sems["att_lo"], last("att_lo", NQ - 1))

            def merge2(nt, n):
                merge(0, n, KT + 2 * nt, GH, GL, 1)
                merge(2, n + 2, KT + 2 * nt + 1, AH, AL, 1)

            with pe.Fori(0, 2) as i:
                for t in range(3):
                    merge2(3 * i + t, At(N_MERGE2 + 4 * t, i, 12))
            for nt in (6, 7):
                merge2(nt, At(N_MERGE2 + 4 * nt))

            pe.wait_ge(m_y, PAIR0 + 3 * KT)
            pe.wait_ge(m_gate, PAIR0 + 3 * KT)
            pe.wait_ge(ml_ready, KT)
            for m in range(KT):
                pe.wait_ge(h_updated, 8 + m + 1)
                fm(I01[:, (m % 2) * T:(m % 2 + 1) * T], At(N_OUT + m), MH, ML)
            norm(2)
            ffn(1)
            norm(3)

        @block.scalar
        def _(act):
            for name, k in ROUND["scalar"].items():
                act.sem_inc(sems[name], k)
            act.sem_inc(gate_ready, GATE0)
            act.sem_inc(g_free[1], 1)
            act.sem_inc(g_free[2], 1)
            act.sem_inc(m_gate, PAIR0)
            act.wait_ge(cst_landed, 16)
            A = nc.scalar.activation

            def hi(n):
                if isinstance(n.value, int) and n.value >= N_SLABS:
                    return
                act.wait_ge(slab_landed[n.slot], 16 * n.turn + 16)
                if n.k >= RING:
                    act.wait_ge(slab_done, n.value - RING + 1)
                nc.scalar.copy(WH[:, n.slot, :], RAW[:, n.slot, :]).then_inc(split_hi, 1)

            def square(m, k, slot):
                if k == 0:
                    act.wait_ge(x_landed, 32)
                else:
                    act.wait_ge(h_updated, RES0 + 8 * (k - 1) + m + 1)
                act.wait_ge(acc_updated, 8 * k + m + 1)
                A(sq[:, slot, :], h[:, bass.ds(m, 1), :].rearrange("p a t -> p (a t)"), ACT.Square).then_inc(squared, 1)

            def norm(k):
                if k == 3:
                    for m in range(KT):
                        act.wait_ge(out_ready, m + 1)
                        act.dma_start(out[:, m, :], h[:, m, :]).then_inc(stored, 16)
                    act.wait_ge(stored, 16 * KT)
                    return
                for m in range(KT):
                    act.wait_ge(ut_ready, 8 * k + m + 1)
                    nc.scalar.copy(UH[:, m, :], ut[:, m % 2, :]).then_inc(uh_ready, 1)

            def ffn(f):
                n0, nd = (N_FFN1, N_DOWN1) if f == 0 else (N_FFN2, N_DOWN2)
                act.preload_act_table_set("silu_and_others")

                def tile(ft, n, t):
                    act.wait_ge(slab_done, n.value + 1)
                    A(gate_act[:, t, :], G[:, n.slot, :], ACT.Silu).then_inc(gate_ready, 1)
                    hi(n + 3)
                    act.wait_ge(hid_ready, HID0 + FT * f + ft + 1)
                    nc.scalar.copy(HH[:, bass.ds(ft, 1), :].rearrange("p a t -> p (a t)"),
                                   hid[:, t, :]).then_inc(hh_ready, 1)
                    hi(n + 4)

                with act.Fori(0, FT // 3) as i:
                    for t in range(3):
                        tile(3 * i + t, At(n0 + 2 * t, i, 6), t)
                tile(FT - 1, At(n0 + 2 * (FT - 1)), 0)

                def down(m, n, t):
                    for c in range(3):
                        hi(n + 3 + c)
                    square(m, 1 if f == 0 else 3, t)

                with act.Fori(0, KT // 2 - 1) as i:
                    for t in range(2):
                        down(2 * i + t, At(nd + 3 * t, i, 6), t)
                for m in (KT - 2, KT - 1):
                    down(m, At(nd + 3 * m), m % 2)

            def dt_prep():
                n = N_SMALL
                act.wait_ge(slab_done, n + 1)
                nc.scalar.copy(LR[:], G[0:16, 0, :]).then_inc(dt_act, 1)
                A(dtv[32:64, 0, :], G[32:64, 0, :], ACT.Identity,
                  bias=cst[32:64, C_DTB:C_DTB + 1]).then_inc(g_free[0], 1)
                hi(At(n + 3))
                act.wait_ge(dt_dve, DT_ABS)
                A(dtv[32:64, 2, :], dtv[32:64, 1, :], ACT.Exp, scale=-1.0).then_inc(dt_act, 1)
                A(minus_a[:], cst[:, C_ALOG:C_ALOG + HS], ACT.Exp).then_inc(dt_act, 1)
                act.wait_ge(dt_pe, 2)
                flat = SC[:].rearrange("p r h -> p (r h)")
                A(flat[:, 12 * HS:16 * HS], I01[:, T:T + 128], ACT.Exp).then_inc(dt_act, 1)
                A(flat[:, 8 * HS:12 * HS], I01[:, T + 128:T + 256], ACT.Exp).then_inc(dt_act, 1)
                for odd, src in enumerate((I01[:, T + 256:T + 384], I2[:, 0:128])):
                    A(SC[:, 16 + odd:24:2, :], src.rearrange("p (c h) -> p c h", h=HS), ACT.Exp).then_inc(dt_act, 1)

            def conv_begin(p, t, n):
                act.wait_ge(slab_done, n.value + 1)
                act.wait_ge(sems["conv_const"], after("conv_const", p))
                act.wait_ge(sems["conv_done"], after("conv_done", p, t - 2))
                inc(A(CV[:, t % 2, :], G[:, n.slot, :], ACT.Identity, bias=gconv[:, 5 * t + 4:5 * t + 5],
                      scale=gconv[:, 5 * t + 3:5 * t + 4]), "conv_begun")
                hi(n + 3)

            def conv_tanh(p, t, wn):
                act.wait_ge(g_free[wn.slot], wn.turn + 1)
                inc(A(TH[:, t % 2, :], CV[:, t % 2, :], ACT.Tanh), "conv_tanh")

            def z_tanh(p, n):
                act.wait_ge(slab_done, n.value + 2)
                act.wait_ge(sems["conv_done"], last("conv_done", p))
                for s in range(2):
                    inc(A(TH[:, s, :], G[:, (n + s).slot, :], ACT.Tanh, scale=0.5), "z_tanh")
                hi(n + 3)
                hi(n + 4)

            def ssm_copy_exp(g):
                act.wait_ge(sems["xb_turned"], after("xb_turned", g))
                act.wait_ge(sems["ssm_y"], last("ssm_y", g - 1))
                inc(nc.scalar.copy(XD[:].rearrange("p j c -> p (j c)"), I01[:]), "x_copied")
                act.wait_ge(sems["u_done"], last("u_done", g - 1))
                inc(nc.scalar.copy(BK[:].rearrange("p j c -> p (j c)"), I2[:]), "b_copied")
                act.wait_ge(sems["seg_done"], after("seg_done", g))
                inc(A(M[:].rearrange("p j r t -> p (j r t)"), I34[:], ACT.Exp), "decay_exp")

            def squares(src, dst, name, g):
                for j in range(TT):
                    act.wait_ge(sems[name], after(name, g, j - 1))
                    inc(A(dump[:], src(j), ACT.Square, accum_out=dst[:, j:j + 1]), name)

            def ssm_squares(g):
                act.wait_ge(sems["ssm_y"], last("ssm_y", g))
                act.wait_ge(sems["ssm_chain"], last("ssm_chain", g))
                squares(lambda j: Y[:, j, :], ss4, "ssm_squares", g)

            def evict_hi(src, dstH, k0, scale, turned, g, name):
                act.wait_ge(sems[turned], last(turned, g))
                for f in range(2):
                    inc(A(dstH[:, bass.ds(k0 + f, 1), :].rearrange("p a t -> p (a t)"), src[:, f * T:(f + 1) * T],
                          ACT.Copy, scale=scale[f]), name)

            ssm_norm_cols = [ggrp[:, f:f + 1] for f in range(2)]
            gla_norm_cols = [cst[:, C_GN + f:C_GN + f + 1] for f in range(2)]

            def merge_gate(q, slot, n, gate_col, n_ahead):
                act.wait_ge(slab_done, n.value + 1)
                A(gate_th[:, slot, :], I01[:, 0:T], ACT.Tanh, bias=half_gate_bias[:, bass.ds(gate_col, 1)],
                  scale=0.5).then_inc(m_gate, 1)
                for s in range(n_ahead):
                    hi(n + 3 + s)

            for n in range(RING):
                hi(At(n))
            for m in range(KT):
                square(m, 0, m % 2)
            norm(0)
            ffn(0)
            act.preload_act_table_set("exp_and_others")
            norm(1)
            dt_prep()
            act.wait_ge(half_bias, 1)

            def ssm_proj(p, n, wn, inner):
                for t in range(4):
                    conv_begin(p, t, n + t)
                    if t == 0 and inner is not None:
                        ssm_copy_exp(inner)
                    conv_tanh(p, t, wn + t)
                if inner is not None:
                    ssm_squares(inner)
                z_tanh(p, n + 4)
                if inner is not None:
                    evict_hi(I01, SH, 2 * inner, ssm_norm_cols, "ssm_turned", inner, "ssm_hi")

            ssm_proj(0, At(N_SSM), At(W_SSM), None)
            with act.Fori(0, NG - 1) as i:
                ssm_proj(i + 1, At(N_SSM + 6, i, 6), At(W_SSM + 6, i, 6), i)
            g = NG - 1
            ssm_copy_exp(g)
            ssm_squares(g)
            evict_hi(I01, SH, 2 * g, ssm_norm_cols, "ssm_turned", g, "ssm_hi")

            with act.Fori(0, KT // 2) as i:
                for t in range(2):
                    merge_gate(2 * i + t, t, At(N_MERGE1 + 3 * t, i, 6), KT + 2 * i + t, 3)

            act.preload_act_table_set("natural_log_exp_and_others")
            for hd in range(HG):
                act.wait_ge(gk_dve, 1 + 2 * (hd + 1))
                A(EX[:, hd, :], EX[:, hd, :], ACT.Exp, scale=-1.0).then_inc(gk_act, 1)
                act.wait_ge(gk_act, 2 * hd + 1)
                A(EX[:, hd, :], EX[:, hd, :], ACT.Ln, bias=1.0).then_inc(gk_act, 1)
            act.preload_act_table_set("exp_and_others")

            def gla_exps(p):
                act.wait_ge(sems["gla_t"], last("gla_t", p))
                A(EX[:, 0, :], TB[:, 0, :], ACT.Exp, scale=1 / GATE_NORM)
                A(EX[:, 1, :], TB[:, 0, :], ACT.Exp, scale=-1 / GATE_NORM)
                A(EX[:, 2, :], BB[:, p, :], ACT.Exp, scale=1 / GATE_NORM)
                A(EX[:, 3, :], TB[:, 1, :], ACT.Exp, scale=1 / GATE_NORM)
                act.wait_ge(sems["gla_chain"], last("gla_chain", p - 1))
                b_last = BB[:, p, :].rearrange("p (c t) -> p c t", t=CH)[:, :, CH - 1]
                inc(A(EL[:], b_last, ACT.Exp, scale=1 / GATE_NORM), "gla_exp")

            def gla_proj(p, n, wn, inner):
                act.wait_ge(slab_done, n.value + 1)
                act.wait_ge(sems["gla_qt"], last("gla_qt", p - 1))
                nc.scalar.copy(QR[:], G[:, wn.slot, :]).then_inc(g_free[wn.slot], 1)
                hi(n + 3)
                if inner is not None:
                    act.wait_ge(sems["gla_kt_turned"], after("gla_kt_turned", inner))
                    inc(nc.scalar.copy(KK[:].rearrange("p j c -> p (j c)"), I34[:, 0:T]), "gla_kt_copied")
                gla_exps(p)
                act.wait_ge(slab_done, n.value + 3)
                act.wait_ge(sems["gla_o_done"], last("gla_o_done", p - 1))
                for s in range(2):
                    nc.scalar.copy(GV[:, 2 * s:2 * s + 2, :].rearrange("p j c -> p (j c)"),
                                   G[:, (wn + 1 + s).slot, :]).then_inc(g_free[(wn + 1 + s).slot], 1)
                hi(n + 4)
                hi(n + 5)
                if inner is not None:
                    gla_squares(inner)
                act.wait_ge(slab_done, n.value + 4)
                hi(n + 6)
                act.wait_ge(slab_done, n.value + 6)
                for s in range(2):
                    inc(A(GTH[:, s, :], G[:, (wn + 4 + s).slot, :], ACT.Tanh, scale=0.5), "gla_r_tanh")
                hi(n + 7)
                hi(n + 8)
                if inner is not None:
                    evict_hi(I34, GH, 2 * inner, gla_norm_cols, "gla_turned", inner, "gla_hi")

            def gla_squares(hd):
                act.wait_ge(sems["gla_o_done"], after("gla_o_done", hd))
                squares(lambda j: I01[:, j * 256:(j + 1) * 256], gss4, "gla_squares", hd)

            for p in range(HG):
                gla_proj(p, At(N_GLA + 6 * p), At(W_GLA + 6 * p), p - 1 if p else None)
            hd = HG - 1
            act.wait_ge(sems["gla_kt_turned"], after("gla_kt_turned", hd))
            inc(nc.scalar.copy(KK[:].rearrange("p j c -> p (j c)"), I34[:, 0:T]), "gla_kt_copied")
            gla_squares(hd)
            evict_hi(I34, GH, 2 * hd, gla_norm_cols, "gla_turned", hd, "gla_hi")

            def load_bias(hd):
                s = hd % 2
                if hd >= 2:
                    act.wait_ge(sems["att_scored"], 16 * ((hd - 2) // 4 + 1) + 4 * ((hd - 2) % 4) + 4)
                else:
                    act.wait_ge(bias_masked, s + 1)
                act.dma_start(bias[0:CH, s, 0:T - CH], a["rel"][hd, 0:CH, 0:T - CH]).then_inc(bias_landed[s], 16)
                act.dma_start(bias[CH:P, s, :], a["rel"][hd, CH:P, :]).then_inc(bias_landed[s], 16)

            def att_out(q, t, n, wn):
                act.wait_ge(slab_done, n.value + t + 1)
                par, kind, f = q % 2, t % 2, t // 2
                act.wait_ge(sems["att_pv"], last("att_pv", q - 2) if q >= 2 else PER["att_pv"])
                dst = (AQ, AK)[kind][:, par, f, :]
                if kind == 0:
                    ins = nc.scalar.mul(dst, G[:, (wn + t).slot, :], ATT_SCALE)
                else:
                    ins = nc.scalar.copy(dst, G[:, (wn + t).slot, :])
                ins.then_inc(g_free[(wn + t).slot], 1)
                hi(n + t + 3)

            def att_v(q, n, wn):
                act.wait_ge(slab_done, n.value + 6)
                act.wait_ge(sems["att_pv"], last("att_pv", q - 1))
                for s in range(2):
                    nc.scalar.copy(AV[:, 2 * s:2 * s + 2, :].rearrange("p j c -> p (j c)"),
                                   G[:, (wn + 4 + s).slot, :]).then_inc(g_free[(wn + 4 + s).slot], 1)
                hi(n + 7)
                hi(n + 8)

            def att_exp(q, e):
                act.wait_ge(sems["att_neg"], after("att_neg", q, e))
                for i in range(TT):
                    o = P_OFF[i]
                    ins = A(PR[:, o:o + (i + 1) * P], PR[:, o:o + (i + 1) * P], ACT.Exp, bias=ngm[:, i:i + 1],
                            accum_out=rs[:, i:i + 1])
                inc(ins, "att_p")

            def att_pt(q, e):
                act.wait_ge(sems["att_turned"], after("att_turned", q, e))
                act.wait_ge(sems["att_pv"], after("att_pv", q, e - 1))
                inc(nc.scalar.copy(PT[:, 0:T], I34[:, 0:T]), "att_pt_a")

            load_bias(0)
            load_bias(1)
            n, wn = At(N_ATT), At(W_ATT)
            for t in range(4):
                att_out(0, t, n, wn)
            att_v(0, n, wn)
            for q in range(NQ):
                n, wn = At(N_ATT + 6 * (q + 1)), At(W_ATT + 6 * (q + 1))
                for e in range(4):
                    att_exp(q, e)
                    if 4 * q + e + 2 < 16:
                        load_bias(4 * q + e + 2)
                    if q + 1 < NQ:
                        att_out(q + 1, e, n, wn)
                    att_pt(q, e)
                if q + 1 < NQ:
                    att_v(q + 1, n, wn)
                evict_hi(I34, AH, 2 * q, (1.0, 1.0), "att_o_turned", q, "att_hi")

            def merge2(nt, n):
                for b, o in ((0, 0), (2, 2)):
                    merge_gate(None, o // 2, n + o, b * KT + nt, 2)
                act.wait_ge(m_final, nt + 1)
                A(MH[:, bass.ds(nt, 1), :].rearrange("p a t -> p (a t)"),
                  merged[:, bass.ds(nt, 1), :].rearrange("p a t -> p (a t)"), ACT.Copy, scale=0.5).then_inc(mh_ready, 1)

            with act.Fori(0, 2) as i:
                for t in range(3):
                    merge2(3 * i + t, At(N_MERGE2 + 4 * t, i, 12))
            for nt in (6, 7):
                merge2(nt, At(N_MERGE2 + 4 * nt))
            for m in range(KT):
                hi(At(N_OUT + m + 3))
                square(m, 2, m % 2)
            norm(2)
            ffn(1)
            norm(3)

        @block.vector
        def _(dve):
            for name, k in ROUND["vector"].items():
                dve.sem_inc(sems[name], k)
            dve.sem_inc(hid_ready, HID0)
            dve.sem_inc(h_updated, RES0)
            dve.sem_inc(acc_updated, RES0)
            dve.sem_inc(m_y, PAIR0)
            V = nc.vector

            def tile_of(ap, k):
                return ap[:, bass.ds(k, 1), :].rearrange("p a t -> p (a t)")

            def lo(n):
                if isinstance(n.value, int) and n.value >= N_SLABS:
                    return
                dve.wait_ge(split_hi, n.value + 1)
                V.tensor_tensor(WL[:, n.slot, :], RAW[:, n.slot, :], WH[:, n.slot, :].bitcast(F32),
                                ALU.subtract).then_inc(split_lo, 1)

            def accumulate(m, k, slot):
                dve.wait_ge(squared, 8 * k + m + 1)
                dve.wait_ge(acc_updated, RES0 + 8 * k + m)
                V.tensor_tensor(acc[:], acc[:], sq[:, slot, :], ALU.add).then_inc(acc_updated, 1)

            def clear_acc(k):
                V.memset(acc[:], 0.0).then_inc(acc_clear, 1)
                dve.wait_ge(acc_clear, k + 1)

            def norm(k):
                dve.wait_ge(norm_sums, k + 1)
                V.tensor_scalar(var4[:], I2[:, 0:TT], 1.0 / D, EPS, ALU.mult, ALU.add).then_inc(norm_var, 1)
                dve.wait_ge(norm_rstd, k + 1)
                V.tensor_tensor(diag[:], ident[:].unsqueeze(1).to_broadcast([P, TT, P]), bc(rstd4[:], P),
                                ALU.mult).then_inc(norm_diag, 1)
                dve.wait_ge(norm_bc, k + 1)
                col = (C_N1, C_NM, C_N2, C_NF)[k]

                def scaled(m):
                    if k != 3 and m >= 2:
                        dve.wait_ge(ul_ready, 8 * k + m - 1)
                    dst = h[:, m, :] if k == 3 else ut[:, m % 2, :]
                    V.scalar_tensor_tensor(dst, h[:, m, :], cst[:, col + m:col + m + 1], I34[:, 0:T],
                                           ALU.mult, ALU.mult).then_inc(out_ready if k == 3 else ut_ready, 1)

                def rest(m):
                    dve.wait_ge(uh_ready, 8 * k + m + 1)
                    V.tensor_tensor(UL[:, m, :], ut[:, m % 2, :], UH[:, m, :].bitcast(F32),
                                    ALU.subtract).then_inc(ul_ready, 1)

                for m in range(KT):
                    if k != 3 and m >= 2:
                        rest(m - 2)
                    scaled(m)
                if k != 3:
                    rest(KT - 2)
                    rest(KT - 1)

            def residual(m, k, n, bank, scale):
                dve.wait_ge(slab_done, n.value + 1)
                V.scalar_tensor_tensor(tile_of(h, m), I01[:, bank * T:(bank + 1) * T], scale, tile_of(h, m),
                                       ALU.mult, ALU.add).then_inc(h_updated, 1)

            def ffn(f):
                n0, nd = (N_FFN1, N_DOWN1) if f == 0 else (N_FFN2, N_DOWN2)

                def tile(ft, n, t):
                    lo(n + 3)
                    dve.wait_ge(gate_ready, GATE0 + FT * f + ft + 1)
                    dve.wait_ge(slab_done, n.value + 2)
                    V.tensor_tensor(hid[:, t, :], G[:, (n + 1).slot, :], gate_act[:, t, :],
                                    ALU.mult).then_inc(hid_ready, 1)
                    dve.wait_ge(hh_ready, FT * f + ft + 1)
                    V.tensor_tensor(tile_of(HL, ft), hid[:, t, :], tile_of(HH, ft).bitcast(F32),
                                    ALU.subtract).then_inc(hl_ready, 1)
                    lo(n + 4)

                with dve.Fori(0, FT // 3) as i:
                    for t in range(3):
                        tile(3 * i + t, At(n0 + 2 * t, i, 6), t)
                tile(FT - 1, At(n0 + 2 * (FT - 1)), 0)
                k = 1 if f == 0 else 3
                clear_acc(k)

                def down(m, n, t):
                    for c in range(3):
                        lo(n + 3 + c)
                    residual(m, k, n + 2, t, 0.5)
                    accumulate(m, k, t)

                with dve.Fori(0, KT // 2 - 1) as i:
                    for t in range(2):
                        down(2 * i + t, At(nd + 3 * t, i, 6), t)
                for m in (KT - 2, KT - 1):
                    down(m, At(nd + 3 * m), m % 2)

            def dt_prep():
                step = [0]

                def link(ins):
                    step[0] += 1
                    ins.then_inc(dt_dve, 1)
                    dve.wait_ge(dt_dve, step[0])

                r0, r1, r2, r3, r4, r5, r6 = (dtv[32:64, s, :] for s in range(7))
                dve.wait_ge(g_free[0], 1)
                link(V.scalar_tensor_tensor(r1, r0, -1.0, r0, ALU.mult, ALU.max))
                assert step[0] == DT_ABS
                lo(At(N_SMALL + 3))
                dve.wait_ge(dt_act, 2)
                link(V.tensor_scalar(r3, r2, 2.0, None, ALU.add))
                link(V.reciprocal(r4, r3))
                link(V.tensor_tensor(r5, r2, r4, ALU.mult))
                link(V.tensor_tensor(r4, r5, r5, ALU.mult))
                link(V.tensor_scalar(r3, r4, 1.0 / 17, None, ALU.mult))
                for odd in (15, 13, 11, 9, 7, 5, 3):
                    link(V.scalar_tensor_tensor(r3, r3, 1.0 / odd, r4, ALU.add, ALU.mult))
                link(V.scalar_tensor_tensor(r3, r3, 1.0, r5, ALU.add, ALU.mult))
                link(V.tensor_scalar(r1, r0, 0.0, None, ALU.max))
                link(V.scalar_tensor_tensor(r6, r3, 2.0, r1, ALU.mult, ALU.add))
                assert step[0] == DT_READY, step
                dve.wait_ge(dt_pe, 1)
                dt_rows = SC[:, 4:8, :].rearrange("p j h -> p (j h)")
                link(V.tensor_copy(dt_rows, I01[:, 0:128]))
                dve.wait_ge(dt_act, 3)
                link(V.scalar_tensor_tensor(SC[:, 0:4, :], SC[:, 4:8, :], -1.0,
                                            minus_a[:].unsqueeze(1).to_broadcast([P, 4, HS]), ALU.mult, ALU.mult))
                assert step[0] == DA_READY, step
                dve.wait_ge(dt_act, 7)
                te = SC[:, 8:12, :].rearrange("p j h -> p (j h)")
                link(V.tensor_tensor(te, te, dt_rows, ALU.mult))
                link(V.memset(SS[:, 0, :], 0.0))

            def conv_consts(p):
                dve.wait_ge(sems["conv_begun"], last("conv_begun", p - 1))
                inc(V.tensor_scalar(gconv[:], cst[:, bass.ds(C_CONV + 20 * p, 20)], 0.5, None, ALU.mult), "conv_const")
                dve.wait_ge(sems["conv_const"], after("conv_const", p))

            def group_consts(g):
                dve.wait_ge(sems["ssm_hi"], last("ssm_hi", g - 1))
                dve.wait_ge(sems["ssm_lo"], last("ssm_lo", g - 1))
                V.tensor_copy(ggrp[:], cst[:, bass.ds(C_GRP + 6 * g, 6)])
                inc(V.tensor_copy(gsc[:], SC[:, :, bass.ds(HPG * g, HPG)]), "group_const")
                dve.wait_ge(sems["group_const"], after("group_const", g))
                dve.wait_ge(sems["intra_done"], last("intra_done", g - 1))
                da = gsc[:, 0:4, :].rearrange("p j r -> p (j r)")
                inc(V.tensor_tensor(M[:].rearrange("p j r t -> p (j r) t"), bc(da, CH),
                                    causal[:].unsqueeze(1).to_broadcast([P, TT * HPG, CH]), ALU.mult), "da_masked")

            def conv_taps(p, t, n, wn):
                cv, src = CV[:, t % 2, :], G[:, n.slot, :]
                dve.wait_ge(sems["conv_begun"], after("conv_begun", p, t))
                for back in (1, 2, 3):
                    ins = V.scalar_tensor_tensor(cv[:, back:T], src[:, 0:T - back],
                                                 gconv[:, 5 * t + 3 - back:5 * t + 4 - back], cv[:, back:T],
                                                 ALU.mult, ALU.add)
                    if back < 3:
                        ins.then_inc(taps, 1)
                        taps_n[0] += 1
                        dve.wait_ge(taps, taps_at(taps_n[0]))
                ins.then_inc(g_free[wn.slot], 1)

            taps_n = [0]
            taps_base = [lambda k: k]

            def taps_at(k):
                return taps_base[0](k)

            def conv_silu(p, t):
                dve.wait_ge(sems["conv_tanh"], after("conv_tanh", p, t))
                if t < 3:
                    dve.wait_ge(sems["cb_done" if t == 2 else "xb_turned"],
                                last("cb_done" if t == 2 else "xb_turned", p - 1))
                else:
                    dve.wait_ge(sems["inter_done"], last("inter_done", p - 1))
                dst = (XT[:, 0, :], XT[:, 1, :], BT[:], CT[:])[t]
                inc(V.scalar_tensor_tensor(dst, TH[:, t % 2, :], 1.0, CV[:, t % 2, :], ALU.add, ALU.mult), "conv_done")

            def z_silu(p, wn):
                for s in range(2):
                    dve.wait_ge(sems["z_tanh"], after("z_tanh", p, s))
                    V.scalar_tensor_tensor(ZS[:, 2 * s:2 * s + 2, :].rearrange("p j c -> p (j c)"), TH[:, s, :], 1.0,
                                           G[:, (wn + s).slot, :], ALU.add,
                                           ALU.mult).then_inc(g_free[(wn + s).slot], 1)

            def rows(k):
                return bc(gsc[:, 4 * k:4 * k + 4, :].rearrange("p j r -> p (j r)"), CH)

            def heads(ap):
                return ap.rearrange("p (q c) -> p q c", c=CH)

            def ssm_x(g):
                dve.wait_ge(sems["x_copied"], after("x_copied", g))
                dve.wait_ge(sems["intra_done"], last("intra_done", g - 1))
                inc(V.tensor_tensor(XDT[:].rearrange("p j (r c) -> p (j r) c", c=CH), heads(XD[:].rearrange("p j c -> p (j c)")), rows(1),
                                    ALU.mult), "xdt_ready")
                dve.wait_ge(sems["u_done"], last("u_done", g - 1))
                inc(V.tensor_tensor(XTE[:].rearrange("p j (r c) -> p (j r) c", c=CH), heads(XD[:].rearrange("p j c -> p (j c)")), rows(2),
                                    ALU.mult), "xte_ready")

            def ssm_m(g):
                dve.wait_ge(sems["cb_done"], after("cb_done", g))
                inc(V.tensor_tensor(CBM[:], I2[:, 0:256].rearrange("p (j t) -> p j t", t=CH),
                                    causal[:].unsqueeze(1).to_broadcast([P, TT, CH]), ALU.mult), "cb_masked")
                dve.wait_ge(sems["cb_masked"], after("cb_masked", g))
                dve.wait_ge(sems["decay_exp"], after("decay_exp", g))
                inc(V.tensor_tensor(M[:], M[:], CBM[:].unsqueeze(2).to_broadcast([P, TT, HPG, CH]), ALU.mult),
                    "m_ready")

            def ssm_chain(g):
                dve.wait_ge(sems["inter_done"], last("inter_done", g - 1))
                dve.wait_ge(sems["ssm_squares"], last("ssm_squares", g - 1))
                k = 0
                for c in range(7):
                    u = update(c)
                    dve.wait_ge(sems["u_done"], after("u_done", g, 0 if c < 4 else 1))
                    if c == 0:
                        inc(V.tensor_copy(SS[:, 1, :], u), "ssm_chain")
                        k += 1
                    else:
                        dve.wait_ge(sems["ssm_chain"], after("ssm_chain", g, k - 1))
                        inc(V.tensor_tensor(heads(ST[:]), heads(SS[:, c, :]), bc(gsc[:, 16 + c, :], CH), ALU.mult),
                            "ssm_chain")
                        k += 1
                        dve.wait_ge(sems["ssm_chain"], after("ssm_chain", g, k - 1))
                        inc(V.tensor_tensor(SS[:, c + 1, :], ST[:], u, ALU.add), "ssm_chain")
                        k += 1
                assert k == PER["ssm_chain"]

            def ssm_y(g):
                dve.wait_ge(sems["inter_done"], after("inter_done", g))
                dve.wait_ge(sems["ssm_turned"], last("ssm_turned", g - 1))
                yf = Y[:].rearrange("p j c -> p (j c)")
                inc(V.tensor_tensor(heads(yf), heads(I34[:]), rows(3), ALU.mult), "ssm_y")
                dve.wait_ge(sems["ssm_y"], after("ssm_y", g, 0))
                dve.wait_ge(sems["intra_done"], after("intra_done", g))
                inc(V.tensor_tensor(yf, yf, I01[:], ALU.add), "ssm_y")
                dve.wait_ge(sems["ssm_y"], after("ssm_y", g, 1))
                dve.wait_ge(sems["xd_ready"], after("xd_ready", g))
                inc(V.tensor_tensor(yf, yf, XD[:].rearrange("p j c -> p (j c)"), ALU.add), "ssm_y")
                dve.wait_ge(sems["ssm_y"], after("ssm_y", g, 2))
                inc(V.tensor_tensor(yf, yf, ZS[:].rearrange("p j c -> p (j c)"), ALU.mult), "ssm_y")

            def ssm_scale(g):
                dve.wait_ge(sems["ssm_squares"], last("ssm_squares", g))
                inc(V.tensor_scalar(var4[:], ss4[:], 1.0 / 256, 4 * EPS, ALU.mult, ALU.add), "ssm_var")
                dve.wait_ge(sems["ssm_rstd"], last("ssm_rstd", g))
                for j in range(TT):
                    inc(V.tensor_scalar(Y[:, j, :], Y[:, j, :], rstd4[:, j:j + 1], None, ALU.mult), "ssm_scaled")

            def evict_lo(src, dH, dL, k0, scale, hi_name, g, name):
                for f in range(2):
                    dve.wait_ge(sems[hi_name], after(hi_name, g, f))
                    inc(V.scalar_tensor_tensor(tile_of(dL, k0 + f), src[:, f * T:(f + 1) * T], scale[f],
                                               tile_of(dH, k0 + f).bitcast(F32), ALU.mult, ALU.subtract), name)

            def merge_y(q, slot, n, nt, first_branch, last_branch, b):
                dve.wait_ge(m_gate, PAIR0 + q + 1)
                dve.wait_ge(slab_done, n.value + 1)
                if b == 1:
                    V.scalar_tensor_tensor(tile_of(merged, nt), gate_th[:, slot, :], 1.0, I01[:, T:2 * T],
                                           ALU.add, ALU.mult).then_inc(m_y, 1)
                    return
                V.scalar_tensor_tensor(MT[:, slot, :], gate_th[:, slot, :], 1.0, I01[:, T:2 * T],
                                       ALU.add, ALU.mult).then_inc(m_y, 1)
                dve.wait_ge(m_y, PAIR0 + q + 1)
                if last_branch:
                    dve.wait_ge(m_sum, nt + 1)
                V.tensor_tensor(tile_of(merged, nt), tile_of(merged, nt), MT[:, slot, :],
                                ALU.add).then_inc(m_final if last_branch else m_sum, 1)

            for n in range(RING):
                lo(At(n))
            clear_acc(0)
            dve.wait_ge(cst_landed, 16)
            V.tensor_scalar(half_gate_bias[:], cst[:, C_GATE:C_GATE + 3 * KT], 0.5, None,
                            ALU.mult).then_inc(half_bias, 1)
            for m in range(KT):
                accumulate(m, 0, m % 2)
            dve.wait_ge(consts, N_CONSTS)
            norm(0)
            ffn(0)
            norm(1)
            dt_prep()

            def ssm_proj(p, n, wn, inner):
                conv_consts(p)
                if inner is not None:
                    group_consts(inner)
                for t in range(4):
                    conv_taps(p, t, n + t, wn + t)
                    lo(n + t + 3)
                    if inner is not None:
                        if t == 0:
                            ssm_x(inner)
                        if t == 1:
                            ssm_m(inner)
                            ssm_chain(inner)
                        if t == 3:
                            ssm_y(inner)
                    conv_silu(p, t)
                if inner is not None:
                    ssm_scale(inner)
                z_silu(p, wn + 4)
                lo(n + 7)
                lo(n + 8)
                if inner is not None:
                    evict_lo(I01, SH, SL, 2 * inner, ssm_norm_cols, "ssm_hi", inner, "ssm_lo")

            ssm_norm_cols = [ggrp[:, f:f + 1] for f in range(2)]
            gla_norm_cols = [cst[:, C_GN + f:C_GN + f + 1] for f in range(2)]
            ssm_proj(0, At(N_SSM), At(W_SSM), None)
            with dve.Fori(0, NG - 1) as i:
                taps_n[0] = 0
                taps_base[0] = lambda k: 8 * i + 8 + k
                ssm_proj(i + 1, At(N_SSM + 6, i, 6), At(W_SSM + 6, i, 6), i)
            g = NG - 1
            group_consts(g)
            ssm_x(g)
            ssm_m(g)
            ssm_chain(g)
            ssm_y(g)
            ssm_scale(g)
            evict_lo(I01, SH, SL, 2 * g, ssm_norm_cols, "ssm_hi", g, "ssm_lo")

            with dve.Fori(0, KT // 2) as i:
                for t in range(2):
                    n = At(N_MERGE1 + 3 * t, i, 6)
                    lo(n + 3)
                    lo(n + 4)
                    merge_y(2 * i + t, t, n + 2, 2 * i + t, True, True, 1)
                    lo(n + 5)

            dve.wait_ge(gk_pe, 1)
            dve.wait_ge(gk_pool, 2)
            V.memset(GS[:, 0, :], 0.0).then_inc(gk_dve, 1)
            for hd in range(HG):
                src = (I01[:, 0:T], I01[:, T:], I34[:, 0:T], I34[:, T:])[hd]
                V.tensor_scalar(BB[:, hd, :], src, cst[:, C_GB + hd:C_GB + hd + 1], None, ALU.add).then_inc(gk_dve, 1)
                dve.wait_ge(gk_dve, 1 + 2 * hd + 1)
                V.scalar_tensor_tensor(EX[:, hd, :], BB[:, hd, :], -1.0, BB[:, hd, :], ALU.mult,
                                       ALU.max).then_inc(gk_dve, 1)
            k = 1 + 2 * HG
            assert k == GK_EVICTED
            for hd in range(HG):
                dve.wait_ge(gk_act, 2 * hd + 2)
                V.scalar_tensor_tensor(TB[:, hd % 2, :], BB[:, hd, :], 0.0, EX[:, hd, :], ALU.min,
                                       ALU.subtract).then_inc(gk_dve, 1)
                k += 1
                dve.wait_ge(gk_dve, k)
                V.tensor_tensor_scan(BB[:, hd, :], RM[:], TB[:, hd % 2, :], 0.0, ALU.mult, ALU.add).then_inc(gk_dve, 1)
                k += 1
                dve.wait_ge(gk_dve, k)

            def chunks(ap):
                return ap.rearrange("p (c t) -> p c t", t=CH)

            def gla_proj(p, n, wn, inner):
                dve.wait_ge(sems["gla_exp"], last("gla_exp", p - 1))
                b3 = chunks(BB[:, p, :])
                inc(V.tensor_tensor(chunks(TB[:, 0, :]), b3, bc(b3[:, :, CH // 2], CH), ALU.subtract), "gla_t")
                inc(V.tensor_tensor(chunks(TB[:, 1, :]), bc(b3[:, :, CH - 1], CH), b3, ALU.subtract), "gla_t")
                lo(n + 3)
                if inner is not None:
                    gla_a_chain(inner)
                dve.wait_ge(sems["gla_exp"], after("gla_exp", p))
                dve.wait_ge(g_free[wn.slot], wn.turn + 1)
                dve.wait_ge(sems["gla_a_done"], last("gla_a_done", p - 1))
                inc(V.scalar_tensor_tensor(QH[:], QR[:], GLA_SCALE, EX[:, 0, :], ALU.mult, ALU.mult), "gla_qh")
                dve.wait_ge(sems["gla_o_done"], last("gla_o_done", p - 1))
                inc(V.scalar_tensor_tensor(QT[:], QR[:], GLA_SCALE, EX[:, 2, :], ALU.mult, ALU.mult), "gla_qt")
                lo(n + 4)
                lo(n + 5)
                if inner is not None:
                    gla_out(inner)
                dve.wait_ge(slab_done, n.value + 4)
                dve.wait_ge(sems["gla_kt_turned"], last("gla_kt_turned", p - 1))
                inc(V.tensor_tensor(KH[:], G[:, (wn + 3).slot, :], EX[:, 1, :], ALU.mult), "gla_kh")
                V.tensor_tensor(KT_[:], G[:, (wn + 3).slot, :], EX[:, 3, :], ALU.mult).then_inc(g_free[(wn + 3).slot], 1)
                lo(n + 6)
                dve.wait_ge(sems["gla_o_ready"], last("gla_o_ready", p - 1))
                for s in range(2):
                    dve.wait_ge(sems["gla_r_tanh"], after("gla_r_tanh", p, s))
                    V.scalar_tensor_tensor(GR[:, 2 * s:2 * s + 2, :].rearrange("p j c -> p (j c)"), GTH[:, s, :], 1.0,
                                           G[:, (wn + 4 + s).slot, :], ALU.add,
                                           ALU.mult).then_inc(g_free[(wn + 4 + s).slot], 1)
                lo(n + 7)
                lo(n + 8)
                if inner is not None:
                    evict_lo(I34, GH, GL, 2 * inner, gla_norm_cols, "gla_hi", inner, "gla_lo")

            def gla_a_chain(hd):
                dve.wait_ge(sems["gla_a_done"], after("gla_a_done", hd))
                inc(V.tensor_tensor(GA[:], I2[:, 0:256].rearrange("p (j t) -> p j t", t=CH),
                                    causal[:].unsqueeze(1).to_broadcast([P, TT, CH]), ALU.mult), "gla_a_masked")
                for c in range(7):
                    u = update(c)
                    dve.wait_ge(sems["gla_u_done"], after("gla_u_done", hd, 0 if c < 4 else 1))
                    if c:
                        dve.wait_ge(sems["gla_chain"], after("gla_chain", hd, c - 1))
                    inc(V.scalar_tensor_tensor(GS[:, c + 1, :], GS[:, c, :], EL[:, c:c + 1], u, ALU.mult, ALU.add),
                        "gla_chain")

            def gla_out(hd):
                dve.wait_ge(sems["gla_squares"], last("gla_squares", hd))
                inc(V.tensor_scalar(var4[:], gss4[:], 4.0 / 256, 4 * EPS, ALU.mult, ALU.add), "gla_var")
                dve.wait_ge(sems["gla_rstd"], last("gla_rstd", hd))
                dve.wait_ge(sems["gla_turned"], last("gla_turned", hd - 1))
                for j in range(TT):
                    inc(V.scalar_tensor_tensor(GO[:, j, :], I01[:, j * 256:(j + 1) * 256], rstd4[:, j:j + 1],
                                               GR[:, j, :], ALU.mult, ALU.mult), "gla_o_ready")

            for p in range(HG):
                gla_proj(p, At(N_GLA + 6 * p), At(W_GLA + 6 * p), p - 1 if p else None)
            hd = HG - 1
            gla_a_chain(hd)
            gla_out(hd)
            evict_lo(I34, GH, GL, 2 * hd, gla_norm_cols, "gla_hi", hd, "gla_lo")

            def att_score(q, e):
                hd = 4 * q + e
                s = hd % 2
                dve.wait_ge(sems["att_s"], after("att_s", q, e))
                dve.wait_ge(bias_landed[s], 32 * (hd // 2 + 1))
                dve.wait_ge(bias_masked, s + 1)
                dve.wait_ge(sems["att_turned"], after("att_turned", q, e - 1))
                for k, i in enumerate((3, 2, 0, 1)):
                    src = {3: I01[:, 0:512], 2: I01[:, 512:896], 0: I01[:, 896:1024], 1: I2[:, 0:256]}[i]
                    o, wd = P_OFF[i], (i + 1) * P
                    inc(V.tensor_tensor_reduce(out=PR[:, o:o + wd], in0=src, in1=bias[:, s, T - wd:T], scale=1.0,
                                               scalar=-3.0e38, op0=ALU.add, op1=ALU.max,
                                               accum_out=mx[:, i:i + 1]), "att_scored")
                dve.wait_ge(sems["att_scored"], 16 * (q + 1) + 4 * e + 4)
                dve.wait_ge(sems["att_p"], after("att_p", q, e - 1))
                inc(V.tensor_scalar(ngm[:], mx[:], -1.0, None, ALU.mult), "att_neg")

            def att_rest(q, e):
                dve.wait_ge(sems["att_p"], after("att_p", q, e))
                dve.wait_ge(sems["att_o"], after("att_o", q, e - 1))
                inc(V.reciprocal(rc[:], rs[:]), "att_recip")
                dve.wait_ge(sems["att_turned"], after("att_turned", q, e))
                dve.wait_ge(sems["att_pv"], after("att_pv", q, e - 1))
                inc(V.tensor_copy(PT[:, T:2 * T], I34[:, T:2 * T]), "att_pt_b")
                inc(V.tensor_copy(PT[:, 2 * T:2 * T + 256], I2[:, 256:512]), "att_pt_b")
                dve.wait_ge(sems["att_recip"], after("att_recip", q, e))
                if e == 0:
                    dve.wait_ge(sems["att_o_turned"], last("att_o_turned", q - 1))
                dve.wait_ge(sems["att_pv"], after("att_pv", q, e))
                inc(V.tensor_tensor(AO[:, :, e * CH:(e + 1) * CH],
                                    I01[:, 0:256].rearrange("p (j c) -> p j c", c=CH), bc(rc[:], CH), ALU.mult),
                    "att_o")

            for s in range(6):
                lo(At(N_ATT + 3 + s))
            for q in range(NQ):
                n = At(N_ATT + 6 * (q + 1))
                for e in range(4):
                    att_score(q, e)
                    if q + 1 < NQ:
                        lo(n + e + 3)
                    att_rest(q, e)
                if q + 1 < NQ:
                    lo(n + 7)
                    lo(n + 8)
                evict_lo(I34, AH, AL, 2 * q, (1.0, 1.0), "att_hi", q, "att_lo")

            def merge2(nt, n):
                for b, o in ((0, 0), (2, 2)):
                    lo(n + o + 3)
                    merge_y(KT + 2 * nt + o // 2, o // 2, n + o + 1, nt, None, b == 2, b)
                    lo(n + o + 4)
                dve.wait_ge(mh_ready, nt + 1)
                V.scalar_tensor_tensor(tile_of(ML, nt), tile_of(merged, nt), 0.5, tile_of(MH, nt).bitcast(F32),
                                       ALU.mult, ALU.subtract).then_inc(ml_ready, 1)

            with dve.Fori(0, 2) as i:
                for t in range(3):
                    merge2(3 * i + t, At(N_MERGE2 + 4 * t, i, 12))
            for nt in (6, 7):
                merge2(nt, At(N_MERGE2 + 4 * nt))
            clear_acc(2)
            for m in range(KT):
                lo(At(N_OUT + m + 3))
                residual(m, 2, At(N_OUT + m), m % 2, 1.0)
                accumulate(m, 2, m % 2)
            norm(2)
            ffn(1)
            norm(3)


N_CONSTS = 10
DT_ABS, DT_READY, DA_READY = 1, 16, 18
GK_EVICTED = 9
P_OFF = {3: 0, 2: 512, 0: 896, 1: 1024}
PT_OFF = {0: 0, 1: 512, 3: 896, 2: 1024}
MAX_REL = 256


def fm_slabs(w):
    k = w.shape[0] // P
    return np.ascontiguousarray(w.reshape(k, P, -1, P).transpose(2, 1, 0, 3)).reshape(-1, P, k * P)


def tm_slabs(w):
    t = w.reshape(2, 4, P, -1, 256).transpose(3, 0, 2, 1, 4)
    return np.ascontiguousarray(t).reshape(-1, P, SLAB)


def down_slabs(w):
    t = fm_slabs(w)
    out = np.zeros((t.shape[0], 3, P, SLAB), np.float32)
    for c, (k0, k1) in enumerate(DOWN_K):
        out[:, c, :, 0:(k1 - k0) * P] = t[:, :, k0 * P:k1 * P]
    return out.reshape(-1, P, SLAB)


def interleave(*parts):
    return np.concatenate(parts, axis=1).reshape(-1, P, SLAB)


def lay_out(i):
    sizes = (512, 512, 1024, 1024, 16, 2048, 4096, 32, 1024, 1024, 1024, 3072)
    ends = np.cumsum(sizes)
    win = i["w_in"][0]
    q, k, v, r, lr, z, xbc, dt, aq, ak, av, gates = (win[:, e - s:e] for s, e in zip(sizes, ends))
    small = np.zeros((D, P), np.float32)
    small[:, 0:16] = lr
    small[:, 32:64] = dt
    gate = fm_slabs(gates).reshape(3, KT, 1, P, SLAB)

    def rounds(s, n):
        return s.reshape(n, -1, P, SLAB)

    xb = fm_slabs(xbc)
    aq_s, ak_s = rounds(fm_slabs(aq), NQ), rounds(fm_slabs(ak), NQ)
    ws = fm_slabs(i["w_branch_ssm"][0]).reshape(KT, P, 2, SLAB).transpose(0, 2, 1, 3)
    stream = [
        interleave(rounds(fm_slabs(i["ffn1_w_gate"][0]), FT), rounds(fm_slabs(i["ffn1_w_up"][0]), FT)),
        down_slabs(i["ffn1_w_down"][0]),
        fm_slabs(small),
        interleave(rounds(xb[0:16], NG), rounds(xb[16:24], NG), rounds(xb[24:32], NG), rounds(tm_slabs(z), NG)),
        interleave(gate[1], ws),
        interleave(rounds(fm_slabs(q), HG), rounds(tm_slabs(v), HG), rounds(fm_slabs(k), HG), rounds(tm_slabs(r), HG)),
        interleave(aq_s[:, 0:1], ak_s[:, 0:1], aq_s[:, 1:2], ak_s[:, 1:2], rounds(tm_slabs(av), NQ)),
        interleave(gate[0], rounds(fm_slabs(i["w_branch_gla"][0]), KT), gate[2],
                   rounds(fm_slabs(i["w_branch_attn"][0]), KT)),
        fm_slabs(i["w_out"][0]),
        interleave(rounds(fm_slabs(i["ffn2_w_gate"][0]), FT), rounds(fm_slabs(i["ffn2_w_up"][0]), FT)),
        down_slabs(i["ffn2_w_down"][0]),
    ]
    slabs = np.concatenate(stream)
    assert slabs.shape[0] == N_SLABS, slabs.shape

    cst = np.zeros((P, NCST), np.float32)

    def cols(at, vec):
        cst[:, at:at + vec.size // P] = vec.reshape(-1, P).T

    cols(C_N1, i["ffn1_norm"][0])
    cols(C_NM, i["mix_norm"][0])
    cols(C_N2, i["ffn2_norm"][0])
    cols(C_NF, i["final_norm"])
    cols(C_GN, i["gla_norm"][0])
    cols(C_GB, i["gla_b_gk"][0])
    cols(C_GATE, i["gate_bias"][0])
    cst[32:64, C_DTB] = i["ssm_dt_bias"][0]
    taps = np.concatenate([i["ssm_conv_w"][0], i["ssm_conv_b"][0][None]])
    taps = taps.reshape(5, 32, P).transpose(2, 1, 0)
    sn = i["ssm_norm"][0].reshape(NG, 2, P)
    for g in range(NG):
        for t, tile in enumerate((2 * g, 2 * g + 1, 16 + g, 24 + g)):
            cst[:, C_CONV + 20 * g + 5 * t:C_CONV + 20 * g + 5 * t + 5] = taps[:, tile]
        cst[:, C_GRP + 6 * g:C_GRP + 6 * g + 2] = sn[g].T
        cst[:, C_GRP + 6 * g + 2:C_GRP + 6 * g + 6] = i["ssm_D"][0][None, HPG * g:HPG * g + HPG]
    cst[:, C_ALOG:] = i["ssm_A_log"][0][None]

    distance = np.arange(P)[:, None] + T - P - np.arange(T)[None, :]
    rel = np.ascontiguousarray(i["attn_rel_bias"][0][np.minimum(distance, MAX_REL) + MAX_REL].transpose(2, 0, 1))
    x = np.ascontiguousarray(i["x"][0].reshape(T, KT, P).transpose(2, 1, 0))
    return {"slabs": slabs, "cst": cst, "rel": rel, "x": x, "wgk": np.ascontiguousarray(i["gla_w_gk"][0])}


def kernel(**inputs):
    from concourse import bacc
    from concourse.bass_utils import run_bass_kernel_spmd

    arrays = lay_out({k: np.asarray(v) for k, v in inputs.items()})
    nc = bacc.Bacc("TRN2", target_bir_lowering=False, num_devices=1, dynamic_dma_scratch_size=1024)
    aps = {n: nc.dram_tensor(f"in_{n}", v.shape, mybir.dt.from_np(v.dtype), kind="ExternalInput").ap()
           for n, v in arrays.items()}
    out = nc.dram_tensor("out_y", (P, KT, T), F32, kind="ExternalOutput").ap()
    build(nc, aps, out)
    r = run_bass_kernel_spmd(nc, [{f"in_{n}": v for n, v in arrays.items()}], core_ids=[0])
    y = r.results[0]["out_y"]
    return np.ascontiguousarray(y.transpose(2, 1, 0)).reshape(1, T, D)
```

```python
from contextlib import ExitStack

import numpy as np
import concourse.bass as bass
from concourse import mybir

F32 = mybir.dt.float32
F32R = mybir.dt.float32r
ALU = mybir.AluOpType
ACT = mybir.ActivationFunctionType

P = 128
T = 512
D = 1024
KT = D // P
FFN = 2816
FT = FFN // P
TT = T // P
CH = 64
NCH = T // CH
HG = 4
NG = 8
HPG = 4
HS = NG * HPG
NQ = 4
EPS = 1e-6
GLA_SCALE = 128 ** -0.5
GATE_NORM = 16.0
ATT_SCALE = 64 ** -0.5
MASKED = -1.0e30
SLAB = 1024
RING = 3

N_FFN1 = 0
N_DOWN1 = N_FFN1 + 2 * FT
N_SMALL = N_DOWN1 + 3 * KT
N_SSM = N_SMALL + 1
N_MERGE1 = N_SSM + 6 * NG
N_GLA = N_MERGE1 + 3 * KT
N_ATT = N_GLA + 6 * HG
N_MERGE2 = N_ATT + 6 * NQ
N_OUT = N_MERGE2 + 4 * KT
N_FFN2 = N_OUT + KT
N_DOWN2 = N_FFN2 + 2 * FT
N_SLABS = N_DOWN2 + 3 * KT
DOWN_K = ((0, 8), (8, 15), (15, 22))

W_SSM = 1
W_MERGE1 = W_SSM + 6 * NG
W_GLA = W_MERGE1 + 2 * KT
W_ATT = W_GLA + 6 * HG
W_MERGE2 = W_ATT + 6 * NQ
MERGE2_HEAD = ((0, 0), (0, 1), (0, 2), (1, 0), (1, 1), (0, 3), (1, 2), (1, 3))

C_N1, C_NM, C_N2, C_NF, C_GN, C_GB, C_GATE, C_CONV, C_GRP = 0, 8, 16, 24, 32, 34, 38, 64, 224
C_ALOG = C_GRP + 6 * NG
C_DTB = C_ALOG + HS
NCST = C_DTB + HS


class At:

    def __init__(self, k, i=0, per=0):
        self.k, self.i, self.per = k, i, per

    def __add__(self, d):
        return At(self.k + d, self.i, self.per)

    @property
    def value(self):
        return self.k + self.per * self.i if self.per else self.k

    @property
    def slot(self):
        return self.k % RING

    @property
    def turn(self):
        return self.k // RING + ((self.per // RING) * self.i if self.per else 0)

    @property
    def free(self):
        return self.turn + 1

    @property
    def read(self):
        return self.turn + 2


ROUND = {
    "scalar": {
        "conv_begun": 4, "conv_tanh": 4, "x_copied": 1, "b_copied": 1, "decay_exp": 1, "z_tanh": 2,
        "ssm_squares": 4, "ssm_hi": 2,
        "gla_exp": 1, "gla_kt_copied": 1, "gla_r_tanh": 2, "gla_squares": 4, "gla_hi": 2,
        "att_p": 4, "att_pt_a": 4, "att_hi": 2,
    },
    "vector": {
        "conv_const": 1, "group_const": 1, "da_masked": 1, "xdt_ready": 1, "xte_ready": 1, "cb_masked": 1,
        "m_ready": 1, "conv_done": 4, "ssm_chain": 13, "ssm_y": 4, "ssm_var": 1, "ssm_scaled": 4, "ssm_lo": 2,
        "gla_t": 2, "gla_qh": 1, "gla_qt": 1, "gla_kh": 1, "gla_a_masked": 1, "gla_chain": 7, "gla_var": 1,
        "gla_o_ready": 4, "gla_lo": 2,
        "att_scored": 16, "att_neg": 4, "att_recip": 4, "att_pt_b": 8, "att_o": 4, "att_lo": 2,
    },
    "gpsimd": {"xd_ready": 1, "ssm_rstd": 1, "gla_rstd": 1},
    "tensor": {
        "xb_turned": 1, "seg_done": 1, "cb_done": 1, "u_done": 2, "intra_done": 1, "inter_done": 1,
        "ssm_turned": 1,
        "gla_a_done": 1, "gla_kt_turned": 1, "gla_u_done": 2, "gla_o_done": 1, "gla_turned": 1,
        "att_s": 4, "att_turned": 4, "att_pv": 4, "att_o_turned": 1,
    },
}
PER = {name: k for sems in ROUND.values() for name, k in sems.items()}


def after(name, r, j=0):
    return PER[name] * (r + 1) + j + 1


def last(name, r):
    return PER[name] * (r + 1) + PER[name] if not isinstance(r, int) or r >= 0 else PER[name]


def build(nc, a, out):
    ctx = ExitStack()
    with ctx:
        def sb(name, shape, dt=F32, stack=None):
            return (stack or ctx).enter_context(nc.sbuf_tensor(name, shape, dt))

        h = sb("h", [P, KT, T])
        UH = sb("UH", [P, KT, T], F32R)
        UL = sb("UL", [P, KT, T], F32R)
        RAW = sb("RAW", [P, RING, SLAB])
        WH = sb("WH", [P, RING, SLAB], F32R)
        WL = sb("WL", [P, RING, SLAB], F32R)
        cst = sb("cst", [P, NCST])
        half_gate_bias = sb("half_gate_bias", [P, 3 * KT])
        ident = sb("ident", [P, P])
        ones = sb("ones", [P, P])
        after_s = sb("after_s", [P, P])
        upto_t = sb("upto_t", [P, P])
        causal = sb("causal", [P, CH])
        minus_half = sb("minus_half", [P, TT])
        LR = sb("LR", [16, T])
        var4 = sb("var4", [P, TT])
        rstd4 = sb("rstd4", [P, TT])
        SC = sb("SC", [P, 24, HS])
        gconv = sb("gconv", [P, 20])
        ggrp = sb("ggrp", [P, 6])
        gsc = sb("gsc", [P, 24, HPG])
        minus_a = sb("minus_a", [P, HS])
        ut = sb("ut", [P, 3, T])
        gate_th = ut
        WGK = sb("WGK", [16, 512])
        rms = sb("rms", [P, T])
        dump = sb("dump", [P, 256])

        r = ExitStack()
        acc = sb("acc", [P, T], F32, r)
        sq = sb("sq", [P, 2, T], F32, r)
        diag = sb("diag", [P, TT, P], F32, r)
        HH = sb("HH", [P, FT, T], F32R, r)
        HL = sb("HL", [P, FT, T], F32R, r)
        hid = sb("hid", [P, RING, T], F32, r)
        r.close()

        r = ExitStack()
        SH = sb("SH", [P, 2 * NG, T], F32R, r)
        SL = sb("SL", [P, 2 * NG, T], F32R, r)
        w = ExitStack()
        XT = sb("XT", [P, 2, T], F32, w)
        BT = sb("BT", [P, T], F32, w)
        CT = sb("CT", [P, T], F32, w)
        CV = sb("CV", [P, 2, T], F32, w)
        TH = sb("TH", [P, 2, T], F32, w)
        ZS = sb("ZS", [P, TT, 256], F32, w)
        prep = ExitStack()
        dtv = sb("dtv", [P, T], F32, prep)
        dtw = sb("dtw", [P, 6, P], F32, prep)
        prep.close()
        XDT = sb("XDT", [P, TT, 256], F32, w)
        XTE = sb("XTE", [P, TT, 256], F32, w)
        XD = sb("XD", [P, TT, 256], F32, w)
        BK = sb("BK", [P, TT, P], F32, w)
        M = sb("M", [P, TT, HPG, CH], F32, w)
        CBM = sb("CBM", [P, TT, CH], F32, w)
        SS = sb("SS", [P, NCH, 256], F32, w)
        ST = sb("ST", [P, 256], F32, w)
        Y = sb("Y", [P, TT, 256], F32, w)
        ss4 = sb("ss4", [P, TT], F32, w)
        w.close()
        r.close()

        r = ExitStack()
        GH = sb("GH", [P, KT, T], F32R, r)
        GL = sb("GL", [P, KT, T], F32R, r)
        w = ExitStack()
        KK = sb("KK", [P, TT, P], F32, w)
        GV = sb("GV", [P, TT, 256], F32, w)
        GR = sb("GR", [P, TT, 256], F32, w)
        GTH = sb("GTH", [P, 2, T], F32, w)
        GA = sb("GA", [P, TT, CH], F32, w)
        GS = sb("GS", [P, NCH, 256], F32, w)
        GO = sb("GO", [P, TT, 256], F32, w)
        EL = sb("EL", [P, NCH], F32, w)
        gss4 = sb("gss4", [P, TT], F32, w)
        w.close()
        AH = sb("AH", [P, KT, T], F32R, r)
        AL = sb("AL", [P, KT, T], F32R, r)
        merged = sb("merged", [P, KT, T], F32, r)
        w = ExitStack()
        BB = sb("BB", [P, HG, T], F32, w)
        EX = sb("EX", [P, 4, T], F32, w)
        TB = sb("TB", [P, 2, T], F32, w)
        RM = sb("RM", [P, T], F32, w)
        QR = sb("QR", [P, T], F32, w)
        QT = sb("QT", [P, T], F32, w)
        QH = sb("QH", [P, T], F32, w)
        KH = sb("KH", [P, T], F32, w)
        KT_ = sb("KT_", [P, T], F32, w)
        w.close()
        w = ExitStack()
        AQ, AK = [None, None], [None, None]
        AQ[0] = sb("AQ0", [P, 2, T], F32, w)
        AK[0] = sb("AK0", [P, 2, T], F32, w)
        AV = sb("AV", [P, TT, 256], F32, w)
        bias = sb("bias", [P, 2, T], F32, w)
        AQ[1] = sb("AQ1", [P, 2, T], F32, w)
        AK[1] = sb("AK1", [P, 2, T], F32, w)
        PR = sb("PR", [P, 1280], F32, w)
        PT = sb("PT", [P, 1280], F32, w)
        AO = sb("AO", [P, TT, 256], F32, w)
        mx = sb("mx", [P, TT], F32, w)
        ngm = sb("ngm", [P, TT], F32, w)
        rs = sb("rs", [P, TT], F32, w)
        rc = sb("rc", [P, TT], F32, w)
        w.close()
        w = ExitStack()
        MH = sb("MH", [P, KT, T], F32R, w)
        ML = sb("ML", [P, KT, T], F32R, w)
        w.close()
        r.close()
        G = ctx.enter_context(nc.psum_tensor("G", [P, 3, T], F32))
        I01 = ctx.enter_context(nc.psum_tensor("I01", [P, 2 * T], F32))
        I2 = ctx.enter_context(nc.psum_tensor("I2", [P, T], F32))
        I34 = ctx.enter_context(nc.psum_tensor("I34", [P, 2 * T], F32))

        sems = {}

        def sem(name):
            sems[name] = ctx.enter_context(nc.semaphore(name))
            return sems[name]

        slab_landed = [sem(f"slab_landed{s}") for s in range(RING)]
        split_hi, split_lo, slab_done = sem("split_hi"), sem("split_lo"), sem("slab_done")
        g_free = [sem(f"g_free{s}") for s in range(3)]
        gate_scaled, gate_ready, gate_rms, hid_ready, hh_ready, hl_ready = (
            sem("gate_scaled"), sem("gate_ready"), sem("gate_rms"), sem("hid_ready"), sem("hh_ready"), sem("hl_ready"))
        h_updated, squared, acc_updated = sem("h_updated"), sem("squared"), sem("acc_updated")
        acc_clear = sem("acc_clear")
        norm_sums, norm_var, norm_rstd, norm_diag, norm_bc = (
            sem("norm_sums"), sem("norm_var"), sem("norm_rstd"), sem("norm_diag"), sem("norm_bc"))
        ut_ready, uh_ready, ul_ready = sem("ut_ready"), sem("uh_ready"), sem("ul_ready")
        rms_ready, raw_read, raw_taps = sem("rms_ready"), sem("raw_read"), sem("raw_taps")
        x_landed = [sem(f"x_landed{s}") for s in range(KT // 2)]
        cst_landed, wgk_landed = sem("cst_landed"), sem("wgk_landed")
        consts, half_bias, lr_ready = sem("consts"), sem("half_bias"), sem("lr_ready")
        m_sum, m_final, mh_ready, ml_ready = sem("m_sum"), sem("m_final"), sem("mh_ready"), sem("ml_ready")
        out_ready, stored = sem("out_ready"), sem("stored")
        dt_act, dt_dve, dt_pe = sem("dt_act"), sem("dt_dve"), sem("dt_pe")
        gk_act, gk_dve, gk_pe, gk_pool = sem("gk_act"), sem("gk_dve"), sem("gk_pe"), sem("gk_pool")
        bias_landed = [sem(f"bias_landed{s}") for s in range(2)]
        bias_masked = sem("bias_masked")
        taps = sem("taps")
        for group in ROUND.values():
            for name in group:
                sem(name)

        def inc(ins, name):
            return ins.then_inc(sems[name], 1)

        HID0, GATE0, RES0 = 2, 1, 2

        def update(c):
            bank, k = c % 2, c // 2 % 2
            return (I01, I34)[c // 4][:, bank * T + k * 256:bank * T + (k + 1) * 256]

        def bc(ap, n):
            return ap.unsqueeze(len(ap.shape)).to_broadcast(list(ap.shape) + [n])

        block = ctx.enter_context(nc.Block())

        @block.sync
        def _(sp):
            sp.dma_start(cst[:], a["cst"]).then_inc(cst_landed, 16)
            slabs = a["slabs"]

            def load(n):
                sp.dma_start(RAW[:, n.slot:n.slot + 1, :],
                             slabs[bass.ds(n.value, 1)].rearrange("s p c -> p s c")
                             ).then_inc(slab_landed[n.slot], 16)

            load(At(0))
            for s in range(KT // 2):
                sp.dma_start(h[:, 2 * s:2 * s + 2, :], a["x"][:, 2 * s:2 * s + 2, :]).then_inc(x_landed[s], 16)
            load(At(1))
            load(At(2))
            sp.dma_start(WGK[:], a["wgk"]).then_inc(wgk_landed, 16)
            with sp.Fori(1, N_SLABS // RING) as i:
                for j in range(RING):
                    n = At(j, i, RING)
                    sp.wait_ge(split_lo, n.value - (RING - 1))
                    load(n)
            for n in range(N_SLABS // RING * RING, N_SLABS):
                sp.wait_ge(split_lo, n - (RING - 1))
                load(At(n))

        @block.gpsimd
        def _(pool):
            for name, k in ROUND["gpsimd"].items():
                pool.sem_inc(sems[name], k)
            step = [0]

            def link(ins):
                step[0] += 1
                ins.then_inc(consts, 1)
                pool.wait_ge(consts, step[0])

            link(nc.gpsimd.memset(ones[:], 1.0))
            link(nc.gpsimd.memset(minus_half[:], -0.5))
            link(nc.gpsimd.memset(ident[:], 0.0))
            link(nc.gpsimd.affine_select(out=ident[:], in_=ident[:], compare_op=ALU.not_equal, fill=1.0, base=0,
                                         pattern=[[-1, P]], channel_multiplier=1))
            link(nc.gpsimd.affine_select(out=after_s[:], in_=ones[:], compare_op=ALU.is_gt, fill=0.0, base=0,
                                         pattern=[[-1, P]], channel_multiplier=1))
            link(nc.gpsimd.memset(after_s[CH:P, 0:CH], 0.0))
            link(nc.gpsimd.affine_select(out=upto_t[:], in_=ones[:], compare_op=ALU.is_ge, fill=0.0, base=0,
                                         pattern=[[1, P]], channel_multiplier=-1))
            link(nc.gpsimd.memset(upto_t[0:CH, CH:P], 0.0))
            link(nc.gpsimd.tensor_copy(causal[0:CH, :], upto_t[0:CH, 0:CH]))
            link(nc.gpsimd.tensor_copy(causal[CH:P, :], upto_t[CH:P, CH:P]))
            assert step[0] == N_CONSTS

            def norm(k):
                pool.wait_ge(norm_var, k + 1)
                nc.gpsimd.tensor_tensor(rstd4[:], var4[:], minus_half[:], ALU.pow).then_inc(norm_rstd, 1)

            def ssm(g):
                pool.wait_ge(sems["xte_ready"], after("xte_ready", g))
                pool.wait_ge(sems["group_const"], after("group_const", g))
                d = ggrp[:, 2:6].unsqueeze(1).unsqueeze(3).to_broadcast([P, TT, HPG, CH])
                x4 = XD[:].rearrange("p j (r c) -> p j r c", r=HPG)
                inc(nc.gpsimd.tensor_tensor(x4, x4, d, ALU.mult), "xd_ready")
                pool.wait_ge(sems["ssm_var"], after("ssm_var", g))
                inc(nc.gpsimd.tensor_tensor(rstd4[:], var4[:], minus_half[:], ALU.pow), "ssm_rstd")

            def gla(hd):
                pool.wait_ge(sems["gla_var"], after("gla_var", hd))
                inc(nc.gpsimd.tensor_tensor(rstd4[:], var4[:], minus_half[:], ALU.pow), "gla_rstd")

            def ffn(f):
                def tile(ft, t):
                    pool.wait_ge(gate_ready, FT * f + ft + 1)
                    nc.gpsimd.tensor_tensor(hid[:, t, :], hid[:, t, :], rms[:], ALU.mult).then_inc(gate_rms, 1)

                tile(0, 0)
                with pool.Fori(0, FT // 3) as i:
                    for t in range(3):
                        tile(3 * i + t + 1, (t + 1) % 3)

            norm(0)
            ffn(0)
            norm(1)
            for m in range(KT):
                pool.wait_ge(uh_ready, 16 + m + 1)
                nc.gpsimd.tensor_tensor(UL[:, m, :], ut[:, m % 2, :], UH[:, m, :].bitcast(F32),
                                        ALU.subtract).then_inc(ul_ready, 1)
            with pool.Fori(0, NG) as i:
                ssm(i)
            pool.wait_ge(sems["ssm_lo"], last("ssm_lo", NG - 1))
            nc.gpsimd.memset(RM[:], 1.0).then_inc(gk_pool, 1)
            pool.wait_ge(gk_pool, 1)
            nc.gpsimd.memset(RM[:].rearrange("p (c t) -> p c t", t=CH)[:, :, 0:1], 0.0).then_inc(gk_pool, 1)
            for hd in range(HG - 1):
                gla(hd)
            k_last = At(W_GLA + 6 * (HG - 1) + 3)
            pool.wait_ge(g_free[k_last.slot], k_last.read)
            for s in range(2):
                nc.gpsimd.memset(bias[0:CH, s, T - CH:T], MASKED).then_inc(bias_masked, 1)
            gla(HG - 1)
            norm(2)
            ffn(1)
            norm(3)

        @block.tensor
        def _(pe):
            for name, k in ROUND["tensor"].items():
                pe.sem_inc(sems[name], k)
            mm = nc.tensor.matmul

            def need_slab(n):
                pe.wait_ge(split_lo, n.value + 1)

            def blocks(dst, n, k0, k1, RH, RL, begin, end):
                last_ins = None
                for which, (W, R) in enumerate(((WH, RH), (WH, RL), (WL, RH))):
                    for k in range(k0, k1):
                        last_ins = mm(dst, W[:, n.slot, (k - k0) * P:(k - k0 + 1) * P], R[:, k, :],
                                      start=begin and which == 0 and k == k0,
                                      stop=end and which == 2 and k == k1 - 1)
                return last_ins

            def fm(dst, n, RH, RL):
                need_slab(n)
                blocks(dst, n, 0, KT, RH, RL, True, True).then_inc(slab_done, 1)

            def fm_pass(dst, n, which):
                if which == 0:
                    need_slab(n)
                W, R = ((WH, UH), (WH, UL), (WL, UH))[which]
                for k in range(KT):
                    ins = mm(dst, W[:, n.slot, k * P:(k + 1) * P], R[:, k, :],
                             start=which == 0 and k == 0, stop=which == 2 and k == KT - 1)
                if which == 2:
                    ins.then_inc(slab_done, 1)

            def fm_fresh(dst, n, stage):
                pe.wait_ge(split_hi, n.value + 1)
                for which, (W, R, ready) in enumerate(((WH, UH, uh_ready), (WH, UL, ul_ready), (WL, UH, None))):
                    if which == 2:
                        need_slab(n)
                    for k in range(KT):
                        if ready is not None:
                            pe.wait_ge(ready, 8 * stage + k + 1)
                        ins = mm(dst, W[:, n.slot, k * P:(k + 1) * P], R[:, k, :],
                                 start=which == 0 and k == 0, stop=which == 2 and k == KT - 1)
                ins.then_inc(slab_done, 1)

            def fm_by_tile(dst, n, stage=None):
                need_slab(n)
                for k in range(KT):
                    if stage is not None:
                        pe.wait_ge(ul_ready, 8 * stage + k + 1)
                    for which, (W, R) in enumerate(((WH, UH), (WH, UL), (WL, UH))):
                        ins = mm(dst, W[:, n.slot, k * P:(k + 1) * P], R[:, k, :],
                                 start=which == 0 and k == 0, stop=which == 2 and k == KT - 1)
                    if stage is None and k < KT - 1:
                        ins.then_inc(raw_read, 1)
                ins.then_inc(slab_done, 1)

            def tm_tile(n, wn, j):
                if j == 0:
                    need_slab(n)
                    need_slab(n + 1)
                dst = G[:, (wn + j // 2).slot, (j % 2) * 256:(j % 2 + 1) * 256]
                for which, (U, W) in enumerate(((UH, WH), (UL, WH), (UH, WL))):
                    for k in range(KT):
                        ins = mm(dst, U[:, k, j * P:(j + 1) * P],
                                 W[:, (n + k // 4).slot, (k % 4) * 256:(k % 4 + 1) * 256],
                                 start=which == 0 and k == 0, stop=which == 2 and k == KT - 1)
                if j == TT - 1:
                    ins.then_inc(slab_done, 2)

            def bank_free(wn):
                pe.wait_ge(g_free[wn.slot], wn.free)

            def bank_read(wn):
                pe.wait_ge(g_free[wn.slot], wn.read)

            def norm_total(k):
                pe.wait_ge(acc_updated, RES0 + 8 * k + 8)
                if k == 0:
                    pe.wait_ge(consts, N_CONSTS)
                for j in range(TT):
                    ins = mm(I2[:, j:j + 1], acc[:, j * P:(j + 1) * P], ones[:, 0:1], start=True, stop=True)
                ins.then_inc(norm_sums, 1)

            def norm_spread(k):
                pe.wait_ge(norm_diag, k + 1)
                mm(I34[:, 0:T], ones[:], diag[:].rearrange("p j t -> p (j t)"), start=True,
                   stop=True).then_inc(norm_bc, 1)

            def ffn(f):
                n0, nd = (N_FFN1, N_DOWN1) if f == 0 else (N_FFN2, N_DOWN2)

                def tile(ft, n):
                    pe.wait_ge(hid_ready, FT * f + ft + 1)
                    if isinstance(ft, int):
                        fm_fresh(G[:, n.slot, :], n, 3 * f)
                        norm_total(2 * f)
                    else:
                        fm(G[:, n.slot, :], n, UH, UL)
                    pe.wait_ge(gate_scaled, FT * f + ft + 1)
                    fm(G[:, (n + 1).slot, :], n + 1, UH, UL)

                tile(0, At(n0))
                norm_spread(2 * f)
                with pe.Fori(0, FT // 3) as i:
                    for t in range(3):
                        tile(3 * i + t + 1, At(n0 + 2 * t + 2, i, 6))

                with pe.Fori(0, KT // 2) as i:
                    for t in range(2):
                        pe.wait_ge(h_updated, 8 * (0, 2)[f] + 2 * i + t + 1)
                        for c, (k0, k1) in enumerate(DOWN_K):
                            n = At(nd + 3 * t + c, i, 6)
                            need_slab(n)
                            pe.wait_ge(hl_ready, FT * f + k1)
                            blocks(I01[:, t * T:(t + 1) * T], n, k0, k1, HH, HL, c == 0,
                                   c == 2).then_inc(slab_done, 1)

            def half(c):
                return slice(CH * (c % 2), CH * (c % 2) + CH)

            def dt_turn():
                bank_read(At(0))
                for j in range(TT):
                    ins = nc.tensor.transpose(I01[:, j * 32:(j + 1) * 32], dtv[32:64, j * P:(j + 1) * P],
                                              ident[32:64, 32:64])
                ins.then_inc(dt_pe, 1)

            def dt_sums():
                pe.wait_ge(dt_dve, DA_READY)
                da = SC[:, 0:4, :].rearrange("p j h -> p (j h)")
                mm(I01[:, T:T + 128], upto_t[:], da, start=True, stop=True)
                mm(I01[:, T + 128:T + 256], after_s[:], da, start=True, stop=True)
                for c in range(NCH):
                    dst = I2[:, 32 * (c // 2):32 * (c // 2) + 32] if c % 2 else \
                        I01[:, T + 256 + 16 * c:T + 288 + 16 * c]
                    ins = mm(dst, ones[half(c), :], SC[half(c), c // 2, :], start=True, stop=True)
                ins.then_inc(dt_pe, 1)

            def ssm_turn(g):
                pe.wait_ge(sems["conv_done"], last("conv_done", g))
                pe.wait_ge(sems["ssm_lo"], last("ssm_lo", g - 1))
                pe.wait_ge(sems["cb_masked"], last("cb_masked", g - 1))
                for j in range(TT):
                    for f in range(2):
                        nc.tensor.transpose(I01[:, j * 256 + f * P:j * 256 + (f + 1) * P],
                                            XT[:, f, j * P:(j + 1) * P], ident[:])
                for j in range(TT):
                    ins = nc.tensor.transpose(I2[:, j * P:(j + 1) * P], BT[:, j * P:(j + 1) * P], ident[:])
                inc(ins, "xb_turned")
                pe.wait_ge(sems["da_masked"], after("da_masked", g))
                pe.wait_ge(sems["ssm_y"], last("ssm_y", g - 1))
                rhs = M[:].rearrange("p j r t -> p (j r t)")
                for s in range(2):
                    ins = mm(I34[:, s * T:(s + 1) * T], after_s[:], rhs[:, s * T:(s + 1) * T], start=True, stop=True)
                inc(ins, "seg_done")

            def ssm_cb_u(g):
                pe.wait_ge(sems["b_copied"], after("b_copied", g))
                for c in range(NCH):
                    ins = mm(I2[half(c), (c // 2) * CH:(c // 2 + 1) * CH], BT[:, c * CH:(c + 1) * CH],
                             CT[:, c * CH:(c + 1) * CH], start=True, stop=True)
                inc(ins, "cb_done")
                pe.wait_ge(sems["xte_ready"], after("xte_ready", g))
                pe.wait_ge(sems["x_copied"], after("x_copied", g))
                for c in range(4):
                    ins = mm(update(c), BK[half(c), c // 2, :], XTE[half(c), c // 2, :],
                             start=True, stop=True)
                inc(ins, "u_done")
                pe.wait_ge(sems["decay_exp"], after("decay_exp", g))
                for c in range(4, 7):
                    ins = mm(update(c), BK[half(c), c // 2, :], XTE[half(c), c // 2, :],
                             start=True, stop=True)
                inc(ins, "u_done")

            def ssm_intra():
                for c in range(NCH):
                    j, s = c // 2, half(c)
                    for rr in range(HPG):
                        ins = mm(I01[s, j * 256 + rr * CH:j * 256 + (rr + 1) * CH], M[s, j, rr, :],
                                 XDT[s, j, rr * CH:(rr + 1) * CH], start=True, stop=True)
                inc(ins, "intra_done")

            def ssm_inter(g):
                pe.wait_ge(sems["m_ready"], after("m_ready", g))
                pe.wait_ge(sems["ssm_chain"], last("ssm_chain", g))
                for c in range(NCH):
                    ins = mm(I34[half(c), (c // 2) * 256:(c // 2 + 1) * 256], CT[:, c * CH:(c + 1) * CH],
                             SS[:, c, :], start=True, stop=True)
                inc(ins, "inter_done")

            def turn_back(src, dst, ready, g, done):
                pe.wait_ge(sems[ready], last(ready, g))
                for f in range(2):
                    for j in range(TT):
                        ins = nc.tensor.transpose(dst[:, f * T + j * P:f * T + (j + 1) * P],
                                                  src[:, j, f * P:(f + 1) * P], ident[:])
                inc(ins, done)

            def project(n, wn, kinds, between):
                t = u = 0
                for kind in kinds:
                    if kind == "fm":
                        bank_free(wn + t)
                        fm(G[:, (wn + t).slot, :], n + t, UH, UL)
                        between.get(u, lambda: None)()
                        t, u = t + 1, u + 1
                    else:
                        bank_free(wn + t)
                        bank_free(wn + t + 1)
                        for j in range(TT):
                            tm_tile(n + t, wn + t, j)
                            between.get(u + j, lambda: None)()
                        t, u = t + 2, u + 4

            def output(n, wn, RH, RL):
                bank_free(wn)
                fm(G[:, wn.slot, :], n, RH, RL)

            def output_half(n, wn, half_no):
                if half_no == 0:
                    bank_free(wn)
                need_slab(n)
                blocks(G[:, wn.slot, :], n, half_no * KT, half_no * KT + KT, SH, SL, half_no == 0,
                       half_no == 1).then_inc(slab_done, 1)

            ffn(0)

            fm_fresh(G[:, 0, :], At(N_SMALL), 1)
            norm_total(1)
            n, wn = At(N_SSM), At(W_SSM)
            bank_free(wn)
            fm(G[:, wn.slot, :], n, UH, UL)
            norm_spread(1)
            bank_free(wn + 1)
            fm_by_tile(G[:, (wn + 1).slot, :], n + 1)
            bank_free(wn + 2)
            fm_by_tile(G[:, (wn + 2).slot, :], n + 2, 2)
            dt_turn()
            bank_free(wn + 3)
            fm(G[:, (wn + 3).slot, :], n + 3, UH, UL)
            bank_free(wn + 4)
            bank_free(wn + 5)
            for j in range(TT):
                tm_tile(n + 4, wn + 4, j)
                if j == 2:
                    dt_sums()
            pe.wait_ge(dt_act, 6)

            SSM_KINDS = ("fm", "fm", "fm", "fm", "tm")
            with pe.Fori(0, NG - 1) as i:
                project(At(N_SSM + 6, i, 6), At(W_SSM + 6, i, 6), SSM_KINDS, {
                    0: lambda: ssm_turn(i), 1: lambda: ssm_cb_u(i), 3: lambda: (ssm_inter(i), ssm_intra()),
                    7: lambda: turn_back(Y, I01, "ssm_scaled", i, "ssm_turned")})
            g = NG - 1
            n, wn = At(N_MERGE1), At(W_MERGE1)
            output(n, wn, UH, UL)
            ssm_turn(g)
            ssm_cb_u(g)
            output_half(n + 1, wn + 1, 0)
            ssm_inter(g)
            ssm_intra()
            output(n + 2, wn + 2, UH, UL)
            output_half(n + 3, wn + 3, 0)
            turn_back(Y, I01, "ssm_scaled", g, "ssm_turned")

            pe.wait_ge(sems["ssm_lo"], last("ssm_lo", NG - 1))
            pe.wait_ge(lr_ready, 1)
            pe.wait_ge(wgk_landed, 16)
            for hd in range(HG):
                dst = (I01[:, 0:T], I01[:, T:], I34[:, 0:T], I34[:, T:])[hd]
                ins = mm(dst, WGK[:, hd * P:(hd + 1) * P], LR[:], start=True, stop=True)
            ins.then_inc(gk_pe, 1)

            output_half(n + 4, wn + 1, 1)
            output_half(n + 5, wn + 3, 1)
            with pe.Fori(0, 2) as i:
                for t in range(3):
                    n, wn = At(N_MERGE1 + 6 + 3 * t, i, 9), At(W_MERGE1 + 4 + 2 * t, i, 6)
                    output(n, wn, UH, UL)
                    output_half(n + 1, wn + 1, 0)
                    output_half(n + 2, wn + 1, 1)

            def gla_a(hd):
                pe.wait_ge(sems["gla_qh"], after("gla_qh", hd))
                bank_read(At(W_GLA + 6 * hd + 3))
                for c in range(NCH):
                    ins = mm(I2[half(c), (c // 2) * CH:(c // 2 + 1) * CH], KH[:, c * CH:(c + 1) * CH],
                             QH[:, c * CH:(c + 1) * CH], start=True, stop=True)
                inc(ins, "gla_a_done")
                pe.wait_ge(sems["gla_lo"], last("gla_lo", hd - 1))
                for j in range(TT):
                    ins = nc.tensor.transpose(I34[:, j * P:(j + 1) * P], KT_[:, j * P:(j + 1) * P], ident[:])
                inc(ins, "gla_kt_turned")

            def gla_u(hd):
                pe.wait_ge(sems["gla_kt_copied"], after("gla_kt_copied", hd))
                for s in range(2):
                    bank_read(At(W_GLA + 6 * hd + 1 + s))
                pe.wait_ge(sems["gla_o_ready"], last("gla_o_ready", hd - 1))
                for c in range(4):
                    ins = mm(update(c), KK[half(c), c // 2, :], GV[half(c), c // 2, :],
                             start=True, stop=True)
                inc(ins, "gla_u_done")
                for c in range(4, 7):
                    ins = mm(update(c), KK[half(c), c // 2, :], GV[half(c), c // 2, :],
                             start=True, stop=True)
                inc(ins, "gla_u_done")

            def gla_o(hd):
                pe.wait_ge(sems["gla_a_masked"], after("gla_a_masked", hd))
                pe.wait_ge(sems["gla_chain"], last("gla_chain", hd))
                pe.wait_ge(sems["gla_qt"], after("gla_qt", hd))
                for c in range(NCH):
                    j, s = c // 2, half(c)
                    dst = I01[s, j * 256:(j + 1) * 256]
                    mm(dst, GA[s, j, :], GV[s, j, :], start=True, stop=False)
                    ins = mm(dst, QT[:, c * CH:(c + 1) * CH], GS[:, c, :], start=False, stop=True)
                inc(ins, "gla_o_done")

            GLA_KINDS = ("fm", "tm", "fm", "tm")
            project(At(N_GLA), At(W_GLA), GLA_KINDS, {})
            pe.wait_ge(gk_dve, GK_EVICTED)
            for hd in range(HG - 1):
                project(At(N_GLA + 6 * (hd + 1)), At(W_GLA + 6 * (hd + 1)), GLA_KINDS, {
                    0: lambda: gla_a(hd), 1: lambda: gla_u(hd), 4: lambda: gla_o(hd),
                    8: lambda: turn_back(GO, I34, "gla_o_ready", hd, "gla_turned")})

            def att_s(q, e):
                f, s, par = e // 2, slice(CH * (e % 2), CH * (e % 2) + CH), q % 2
                if e == 0:
                    for t in range(4):
                        bank_read(At(W_ATT + 6 * q + t))
                    if q == 0:
                        pe.wait_ge(sems["gla_lo"], last("gla_lo", HG - 1))
                pe.wait_ge(sems["att_o"], after("att_o", q, e - 1))
                for i in (3, 2, 0, 1):
                    dst = {3: I01[:, 0:512], 2: I01[:, 512:896], 0: I01[:, 896:1024], 1: I2[:, 0:256]}[i]
                    ins = mm(dst, AQ[par][s, f, i * P:(i + 1) * P], AK[par][s, f, 0:(i + 1) * P],
                             start=True, stop=True)
                inc(ins, "att_s")

            def att_turn(q, e):
                pe.wait_ge(sems["att_p"], after("att_p", q, e))
                if q == 0 and e == 0:
                    pass
                elif e == 0:
                    pe.wait_ge(sems["att_lo"], last("att_lo", q - 1))
                else:
                    pe.wait_ge(sems["att_pt_b"], after("att_pt_b", q, 2 * (e - 1) + 1))
                    pe.wait_ge(sems["att_pt_a"], after("att_pt_a", q, e - 1))
                for i in range(TT):
                    for b in range(i + 1):
                        col = PT_OFF[b] + (i - b) * P
                        dst = I34[:, col:col + P] if b != 2 else I2[:, 256 + (i - b) * P:256 + (i - b + 1) * P]
                        ins = nc.tensor.transpose(dst, PR[:, P_OFF[i] + b * P:P_OFF[i] + (b + 1) * P], ident[:])
                inc(ins, "att_turned")

            def att_pv(q, e):
                if e == 0:
                    for t in (4, 5):
                        bank_read(At(W_ATT + 6 * q + t))
                pe.wait_ge(sems["att_pt_a"], after("att_pt_a", q, e))
                pe.wait_ge(sems["att_pt_b"], after("att_pt_b", q, 2 * e + 1))
                for i in range(TT):
                    for b in range(i + 1):
                        col = PT_OFF[b] + (i - b) * P
                        ins = mm(I01[:, i * CH:(i + 1) * CH], PT[:, col:col + P], AV[:, b, e * CH:(e + 1) * CH],
                                 start=b == 0, stop=b == i)
                inc(ins, "att_pv")

            def att_part(q, k):
                n, wn = At(N_ATT + 6 * q), At(W_ATT + 6 * q)
                if k < 12:
                    t, which = k // 3, k % 3
                    if which == 0:
                        bank_free(wn + t)
                    fm_pass(G[:, (wn + t).slot, :], n + t, which)
                else:
                    if k == 12:
                        bank_free(wn + 4)
                        bank_free(wn + 5)
                    tm_tile(n + 4, wn + 4, k - 12)

            hd = HG - 1
            for k in range(16):
                att_part(0, k)
                if k == 2:
                    gla_a(hd)
                if k == 4:
                    gla_u(hd)
                if k == 8:
                    gla_o(hd)
                if k == 13:
                    turn_back(GO, I34, "gla_o_ready", hd, "gla_turned")

            def merge2_part(nt, kind, n, wn):
                output(n, wn, *((UH, UL), (GH, GL), (UH, UL), (AH, AL))[kind])

            def merge2_head(k):
                merge2_part(*MERGE2_HEAD[k], At(N_MERGE2 + k), At(W_MERGE2 + k))

            for q in range(NQ):
                more = q + 1 < NQ
                for e in range(4):
                    att_s(q, e)
                    if more:
                        att_part(q + 1, 4 * e)
                        att_part(q + 1, 4 * e + 1)
                        att_part(q + 1, 4 * e + 2)
                    else:
                        merge2_head(e)
                    att_turn(q, e)
                    if more:
                        att_part(q + 1, 4 * e + 3)
                    att_pv(q, e)
                if not more:
                    merge2_head(4)
                turn_back(AO, I34, "att_o", q, "att_o_turned")

            pe.wait_ge(sems["att_lo"], last("att_lo", NQ - 1))
            for k in range(5, 8):
                merge2_head(k)
            with pe.Fori(0, 2) as i:
                for k in range(12):
                    merge2_part(None, k % 4, At(N_MERGE2 + 8 + k, i, 12), At(W_MERGE2 + 8 + k, i, 12))

            pe.wait_ge(ml_ready, KT)
            for m in range(KT):
                pe.wait_ge(h_updated, 8 + m + 1)
                fm(I01[:, (m % 2) * T:(m % 2 + 1) * T], At(N_OUT + m), MH, ML)
            ffn(1)
            norm_total(3)
            norm_spread(3)

        @block.scalar
        def _(act):
            for name, k in ROUND["scalar"].items():
                act.sem_inc(sems[name], k)
            for bank in range(3):
                act.sem_inc(g_free[bank], 1)
            act.wait_ge(cst_landed, 16)
            A = nc.scalar.activation

            def hi(n):
                if isinstance(n.value, int) and n.value >= N_SLABS:
                    return
                act.wait_ge(slab_landed[n.slot], 16 * n.turn + 16)
                if n.k >= RING:
                    act.wait_ge(slab_done, n.value - RING + 1)
                nc.scalar.copy(WH[:, n.slot, :], RAW[:, n.slot, :]).then_inc(split_hi, 1)

            def raw_hi(m, stage):
                k = (0, 1, None, 2)[stage]
                if k == 0:
                    act.wait_ge(x_landed[m // 2], 16)
                else:
                    act.wait_ge(h_updated, RES0 + 8 * (k - 1) + m + 1)
                A(UH[:, bass.ds(m, 1), :].rearrange("p a t -> p (a t)"), h[:, bass.ds(m, 1), :].rearrange("p a t -> p (a t)"),
                  ACT.Copy, scale=cst[:, bass.ds((C_N1, C_NM, C_N2)[k] + m, 1)]).then_inc(uh_ready, 1)

            def square(m, k, slot, wait=True):
                if wait:
                    act.wait_ge(acc_updated, 8 * k + m + 1)
                    if k:
                        act.wait_ge(h_updated, RES0 + 8 * (k - 1) + m + 1)
                A(sq[:, slot, :], h[:, bass.ds(m, 1), :].rearrange("p a t -> p (a t)"), ACT.Square).then_inc(squared, 1)

            def store():
                for m in range(KT):
                    act.wait_ge(out_ready, m + 1)
                    act.dma_start(out[:, m, :], h[:, m, :]).then_inc(stored, 16)
                act.wait_ge(stored, 16 * KT)

            def ffn(f):
                n0, nd = (N_FFN1, N_DOWN1) if f == 0 else (N_FFN2, N_DOWN2)
                act.preload_act_table_set("silu_and_others")

                def tile(ft, n, t):
                    if isinstance(ft, int):
                        hi(n + 3)
                    act.wait_ge(gate_scaled, GATE0 + FT * f + ft + 1)
                    A(hid[:, t, :], hid[:, t, :], ACT.Silu).then_inc(gate_ready, 1)
                    if not isinstance(ft, int):
                        hi(n + 3)
                    act.wait_ge(hid_ready, HID0 + FT * f + ft + 1)
                    nc.scalar.copy(HH[:, bass.ds(ft, 1), :].rearrange("p a t -> p (a t)"),
                                   hid[:, t, :]).then_inc(hh_ready, 1)
                    hi(n + 4)

                tile(0, At(n0), 0)
                with act.Fori(0, FT // 3) as i:
                    for t in range(3):
                        tile(3 * i + t + 1, At(n0 + 2 * t + 2, i, 6), (t + 1) % 3)

                def down(m, n, t):
                    for c in range(3):
                        hi(n + 3 + c)
                    if f == 0:
                        act.wait_ge(acc_updated, 8 + m + 1)
                        raw_hi(m, 1)
                    square(m, 1 if f == 0 else 3, t, f == 1)

                with act.Fori(0, KT // 2 - 1) as i:
                    for t in range(2):
                        down(2 * i + t, At(nd + 3 * t, i, 6), t)
                for m in (KT - 2, KT - 1):
                    down(m, At(nd + 3 * m), m % 2)

            def dt_exp():
                act.wait_ge(dt_dve, DT_ABS)
                A(dtw[:, 2, :], dtw[:, 1, :], ACT.Exp, scale=-1.0).then_inc(dt_act, 1)
                A(minus_a[:], cst[:, C_ALOG:C_ALOG + HS], ACT.Exp).then_inc(dt_act, 1)

            def decay_exps():
                act.wait_ge(dt_pe, 2)
                flat = SC[:].rearrange("p r h -> p (r h)")
                A(flat[:, 12 * HS:16 * HS], I01[:, T:T + 128], ACT.Exp).then_inc(dt_act, 1)
                A(flat[:, 8 * HS:12 * HS], I01[:, T + 128:T + 256], ACT.Exp).then_inc(dt_act, 1)
                for odd, src in enumerate((I01[:, T + 256:T + 384], I2[:, 0:128])):
                    A(SC[:, 16 + odd:24:2, :], src.rearrange("p (c h) -> p c h", h=HS), ACT.Exp).then_inc(dt_act, 1)

            def conv_begin(p, t, n, wn):
                raw = isinstance(p, int) and t < 2
                if raw:
                    act.wait_ge(g_free[wn.slot], wn.read)
                else:
                    act.wait_ge(slab_done, n.value + 1)
                act.wait_ge(sems["conv_const"], after("conv_const", p))
                act.wait_ge(sems["conv_done"], after("conv_done", p, t - 2))
                inc(A(CV[:, t % 2, :], XT[:, t, :] if raw else G[:, wn.slot, :], ACT.Identity,
                      bias=gconv[:, 5 * t + 4:5 * t + 5], scale=gconv[:, 5 * t + 3:5 * t + 4]), "conv_begun")
                if not raw:
                    hi(n + 3)

            def conv_tanh(p, t, wn):
                if isinstance(p, int) and t < 2:
                    act.wait_ge(raw_taps, t + 1)
                else:
                    act.wait_ge(g_free[wn.slot], wn.read)
                inc(A(TH[:, t % 2, :], CV[:, t % 2, :], ACT.Tanh), "conv_tanh")

            def z_tanh(p, n, wn):
                act.wait_ge(slab_done, n.value + 2)
                act.wait_ge(sems["conv_done"], last("conv_done", p))
                for s in range(2):
                    inc(A(TH[:, s, :], G[:, (wn + s).slot, :], ACT.Tanh, scale=0.5), "z_tanh")
                hi(n + 3)
                hi(n + 4)

            def ssm_copy_exp(g):
                act.wait_ge(sems["xb_turned"], after("xb_turned", g))
                act.wait_ge(sems["ssm_y"], last("ssm_y", g - 1))
                inc(nc.scalar.copy(XD[:].rearrange("p j c -> p (j c)"), I01[:]), "x_copied")
                act.wait_ge(sems["u_done"], last("u_done", g - 1))
                inc(nc.scalar.copy(BK[:].rearrange("p j c -> p (j c)"), I2[:]), "b_copied")
                act.wait_ge(sems["seg_done"], after("seg_done", g))
                inc(A(M[:].rearrange("p j r t -> p (j r t)"), I34[:], ACT.Exp), "decay_exp")

            def squares(src, dst, name, g):
                for j in range(TT):
                    act.wait_ge(sems[name], after(name, g, j - 1))
                    inc(A(dump[:], src(j), ACT.Square, accum_out=dst[:, j:j + 1]), name)

            def ssm_squares(g):
                act.wait_ge(sems["ssm_y"], last("ssm_y", g))
                act.wait_ge(sems["ssm_chain"], last("ssm_chain", g))
                squares(lambda j: Y[:, j, :], ss4, "ssm_squares", g)

            def evict_hi(src, dstH, k0, scale, turned, g, name):
                act.wait_ge(sems[turned], last(turned, g))
                for f in range(2):
                    inc(A(dstH[:, bass.ds(k0 + f, 1), :].rearrange("p a t -> p (a t)"), src[:, f * T:(f + 1) * T],
                          ACT.Copy, scale=scale[f]), name)

            ssm_norm_cols = [ggrp[:, f:f + 1] for f in range(2)]
            gla_norm_cols = [cst[:, C_GN + f:C_GN + f + 1] for f in range(2)]

            def gate_tanh(wn, slot, n, col):
                act.wait_ge(slab_done, n.value + 1)
                A(gate_th[:, slot, :], G[:, wn.slot, :], ACT.Tanh, bias=half_gate_bias[:, bass.ds(col, 1)],
                  scale=0.5).then_inc(g_free[wn.slot], 1)

            hi(At(0))
            for m in range(KT):
                raw_hi(m, 0)
            hi(At(1))
            for m in range(KT):
                square(m, 0, m % 2)
                if m == 1:
                    hi(At(2))
            ffn(0)
            act.preload_act_table_set("exp_and_others")
            hi(At(N_SMALL + 3))
            hi(At(N_SMALL + 4))
            for m in range(KT):
                act.wait_ge(ut_ready, m + 1)
                act.wait_ge(*((raw_read, m + 1) if m < KT - 1 else (slab_done, N_SSM + 2)))
                nc.scalar.copy(UH[:, m, :], ut[:, m % 2, :]).then_inc(uh_ready, 1)
            hi(At(N_SMALL + 5))
            act.wait_ge(half_bias, 1)

            def ssm_proj(p, n, wn, inner):
                for t in range(4):
                    conv_begin(p, t, n + t, wn + t)
                    if t == 0 and inner is not None:
                        ssm_copy_exp(inner)
                    conv_tanh(p, t, wn + t)
                    if inner is None and t == 0:
                        dt_exp()
                    if inner is None and t == 3:
                        decay_exps()
                if inner is not None:
                    ssm_squares(inner)
                z_tanh(p, n + 4, wn + 4)
                if inner is not None:
                    evict_hi(I01, SH, 2 * inner, ssm_norm_cols, "ssm_turned", inner, "ssm_hi")

            ssm_proj(0, At(N_SSM), At(W_SSM), None)
            with act.Fori(0, NG - 1) as i:
                ssm_proj(i + 1, At(N_SSM + 6, i, 6), At(W_SSM + 6, i, 6), i)
            g = NG - 1
            n, wn = At(N_MERGE1), At(W_MERGE1)
            gate_tanh(wn, 0, n, KT)
            hi(n + 3)
            ssm_copy_exp(g)
            hi(n + 4)
            gate_tanh(wn + 2, 1, n + 2, KT + 1)
            hi(n + 5)
            ssm_squares(g)
            evict_hi(I01, SH, 2 * g, ssm_norm_cols, "ssm_turned", g, "ssm_hi")
            for s in (6, 7, 8):
                hi(n + s)

            act.preload_act_table_set("natural_log_exp_and_others")
            for hd in range(HG):
                act.wait_ge(gk_dve, 2 * (hd + 1))
                A(EX[:, hd, :], EX[:, hd, :], ACT.Exp, scale=-1.0).then_inc(gk_act, 1)
                act.wait_ge(gk_act, 2 * hd + 1)
                A(EX[:, hd, :], EX[:, hd, :], ACT.Ln, bias=1.0).then_inc(gk_act, 1)
            act.preload_act_table_set("exp_and_others")

            with act.Fori(0, 2) as i:
                for t in range(3):
                    n, wn = At(N_MERGE1 + 6 + 3 * t, i, 9), At(W_MERGE1 + 4 + 2 * t, i, 6)
                    used = wn + (-3)
                    act.wait_ge(g_free[used.slot], used.read)
                    gate_tanh(wn, (2 + t) % 3, n, KT + 3 * i + t + 2)
                    for s in (3, 4, 5):
                        hi(n + s)

            def gla_exps(p):
                act.wait_ge(sems["gla_t"], last("gla_t", p))
                A(EX[:, 0, :], TB[:, 0, :], ACT.Exp, scale=1 / GATE_NORM)
                A(EX[:, 1, :], TB[:, 0, :], ACT.Exp, scale=-1 / GATE_NORM)
                A(EX[:, 2, :], BB[:, p, :], ACT.Exp, scale=1 / GATE_NORM)
                A(EX[:, 3, :], TB[:, 1, :], ACT.Exp, scale=1 / GATE_NORM)
                act.wait_ge(sems["gla_chain"], last("gla_chain", p - 1))
                b_last = BB[:, p, :].rearrange("p (c t) -> p c t", t=CH)[:, :, CH - 1]
                inc(A(EL[:], b_last, ACT.Exp, scale=1 / GATE_NORM), "gla_exp")

            def gla_proj(p, n, wn, inner):
                act.wait_ge(slab_done, n.value + 1)
                act.wait_ge(sems["gla_qt"], last("gla_qt", p - 1))
                nc.scalar.copy(QR[:], G[:, wn.slot, :]).then_inc(g_free[wn.slot], 1)
                hi(n + 3)
                if inner is not None:
                    act.wait_ge(sems["gla_kt_turned"], after("gla_kt_turned", inner))
                    inc(nc.scalar.copy(KK[:].rearrange("p j c -> p (j c)"), I34[:, 0:T]), "gla_kt_copied")
                gla_exps(p)
                act.wait_ge(slab_done, n.value + 3)
                act.wait_ge(sems["gla_o_done"], last("gla_o_done", p - 1))
                for s in range(2):
                    nc.scalar.copy(GV[:, 2 * s:2 * s + 2, :].rearrange("p j c -> p (j c)"),
                                   G[:, (wn + 1 + s).slot, :]).then_inc(g_free[(wn + 1 + s).slot], 1)
                hi(n + 4)
                hi(n + 5)
                if inner is not None:
                    gla_squares(inner)
                act.wait_ge(slab_done, n.value + 4)
                hi(n + 6)
                act.wait_ge(slab_done, n.value + 6)
                for s in range(2):
                    inc(A(GTH[:, s, :], G[:, (wn + 4 + s).slot, :], ACT.Tanh, scale=0.5), "gla_r_tanh")
                hi(n + 7)
                hi(n + 8)
                if inner is not None:
                    evict_hi(I34, GH, 2 * inner, gla_norm_cols, "gla_turned", inner, "gla_hi")

            def gla_squares(hd):
                act.wait_ge(sems["gla_o_done"], after("gla_o_done", hd))
                squares(lambda j: I01[:, j * 256:(j + 1) * 256], gss4, "gla_squares", hd)

            for p in range(HG):
                gla_proj(p, At(N_GLA + 6 * p), At(W_GLA + 6 * p), p - 1 if p else None)

            def load_bias(hd):
                s = hd % 2
                if hd >= 2:
                    act.wait_ge(sems["att_scored"], 16 * ((hd - 2) // 4 + 1) + 4 * ((hd - 2) % 4) + 4)
                else:
                    act.wait_ge(bias_masked, s + 1)
                act.dma_start(bias[0:CH, s, 0:T - CH], a["rel"][hd, 0:CH, 0:T - CH]).then_inc(bias_landed[s], 16)
                act.dma_start(bias[CH:P, s, :], a["rel"][hd, CH:P, :]).then_inc(bias_landed[s], 16)

            def att_out(q, t, n, wn):
                act.wait_ge(slab_done, n.value + t + 1)
                par, kind, f = q % 2, t % 2, t // 2
                act.wait_ge(sems["att_pv"], last("att_pv", q - 2) if q >= 2 else PER["att_pv"])
                dst = (AQ, AK)[kind][par][:, f, :]
                if kind == 0:
                    ins = nc.scalar.mul(dst, G[:, (wn + t).slot, :], ATT_SCALE)
                else:
                    ins = nc.scalar.copy(dst, G[:, (wn + t).slot, :])
                ins.then_inc(g_free[(wn + t).slot], 1)
                hi(n + t + 3)

            def att_v(q, n, wn):
                act.wait_ge(slab_done, n.value + 6)
                act.wait_ge(sems["att_pv"], last("att_pv", q - 1))
                for s in range(2):
                    nc.scalar.copy(AV[:, 2 * s:2 * s + 2, :].rearrange("p j c -> p (j c)"),
                                   G[:, (wn + 4 + s).slot, :]).then_inc(g_free[(wn + 4 + s).slot], 1)
                hi(n + 7)
                hi(n + 8)

            def att_exp(q, e):
                act.wait_ge(sems["att_neg"], after("att_neg", q, e))
                for i in range(TT):
                    o = P_OFF[i]
                    ins = A(PR[:, o:o + (i + 1) * P], PR[:, o:o + (i + 1) * P], ACT.Exp, bias=ngm[:, i:i + 1],
                            accum_out=rs[:, i:i + 1])
                inc(ins, "att_p")

            def att_pt(q, e):
                act.wait_ge(sems["att_turned"], after("att_turned", q, e))
                act.wait_ge(sems["att_pv"], after("att_pv", q, e - 1))
                inc(nc.scalar.copy(PT[:, 0:T], I34[:, 0:T]), "att_pt_a")

            hd = HG - 1
            n, wn = At(N_ATT), At(W_ATT)
            load_bias(0)
            load_bias(1)
            att_out(0, 0, n, wn)
            act.wait_ge(sems["gla_kt_turned"], after("gla_kt_turned", hd))
            inc(nc.scalar.copy(KK[:].rearrange("p j c -> p (j c)"), I34[:, 0:T]), "gla_kt_copied")
            att_out(0, 1, n, wn)
            att_out(0, 2, n, wn)
            gla_squares(hd)
            att_out(0, 3, n, wn)
            evict_hi(I34, GH, 2 * hd, gla_norm_cols, "gla_turned", hd, "gla_hi")
            att_v(0, n, wn)

            def merge2_part(nt, kind, n, wn):
                if kind in (0, 2):
                    if not isinstance(nt, int) or nt:
                        act.wait_ge(m_final if kind else m_sum, nt)
                    gate_tanh(wn, kind // 2, n, kind * KT + nt)
                hi(n + 3)
                if kind == 3:
                    act.wait_ge(m_final, nt + 1)
                    A(MH[:, bass.ds(nt, 1), :].rearrange("p a t -> p (a t)"),
                      merged[:, bass.ds(nt, 1), :].rearrange("p a t -> p (a t)"), ACT.Copy,
                      scale=0.5).then_inc(mh_ready, 1)

            def merge2_head(k):
                merge2_part(*MERGE2_HEAD[k], At(N_MERGE2 + k), At(W_MERGE2 + k))

            for q in range(NQ):
                n, wn = At(N_ATT + 6 * (q + 1)), At(W_ATT + 6 * (q + 1))
                for e in range(4):
                    att_exp(q, e)
                    if 4 * q + e + 2 < 16:
                        load_bias(4 * q + e + 2)
                    if q + 1 < NQ:
                        att_out(q + 1, e, n, wn)
                    else:
                        merge2_head(e)
                    att_pt(q, e)
                if q + 1 < NQ:
                    att_v(q + 1, n, wn)
                else:
                    merge2_head(4)
                evict_hi(I34, AH, 2 * q, (1.0, 1.0), "att_o_turned", q, "att_hi")

            for k in range(5, 8):
                merge2_head(k)
            with act.Fori(0, 2) as i:
                for k in range(12):
                    merge2_part(3 * i + k // 4 + 2, k % 4, At(N_MERGE2 + 8 + k, i, 12), At(W_MERGE2 + 8 + k, i, 12))
            for m in range(KT):
                hi(At(N_OUT + m + 3))
                raw_hi(m, 3)
                square(m, 2, m % 2)
            ffn(1)
            store()

        @block.vector
        def _(dve):
            for name, k in ROUND["vector"].items():
                dve.sem_inc(sems[name], k)
            dve.sem_inc(hid_ready, HID0)
            dve.sem_inc(gate_scaled, GATE0)
            dve.sem_inc(h_updated, RES0)
            dve.sem_inc(acc_updated, RES0)
            V = nc.vector

            def tile_of(ap, k):
                return ap[:, bass.ds(k, 1), :].rearrange("p a t -> p (a t)")

            def lo(n):
                if isinstance(n.value, int) and n.value >= N_SLABS:
                    return
                dve.wait_ge(split_hi, n.value + 1)
                V.tensor_tensor(WL[:, n.slot, :], RAW[:, n.slot, :], WH[:, n.slot, :].bitcast(F32),
                                ALU.subtract).then_inc(split_lo, 1)

            def accumulate(m, k, slot):
                dve.wait_ge(squared, 8 * k + m + 1)
                dve.wait_ge(acc_updated, RES0 + 8 * k + m)
                V.tensor_tensor(acc[:], acc[:], sq[:, slot, :], ALU.add).then_inc(acc_updated, 1)

            def clear_acc(k):
                V.memset(acc[:], 0.0).then_inc(acc_clear, 1)
                dve.wait_ge(acc_clear, k + 1)

            def raw_lo(m, stage):
                dve.wait_ge(uh_ready, 8 * stage + m + 1)
                col = (C_N1, C_NM, None, C_N2)[stage]
                V.scalar_tensor_tensor(tile_of(UL, m), tile_of(h, m), cst[:, bass.ds(col + m, 1)],
                                       tile_of(UH, m).bitcast(F32), ALU.mult, ALU.subtract).then_inc(ul_ready, 1)

            def norm_rms(k):
                dve.wait_ge(norm_sums, k + 1)
                V.tensor_scalar(var4[:], I2[:, 0:TT], 1.0 / D, EPS, ALU.mult, ALU.add).then_inc(norm_var, 1)
                dve.wait_ge(norm_rstd, k + 1)
                V.tensor_tensor(diag[:], ident[:].unsqueeze(1).to_broadcast([P, TT, P]), bc(rstd4[:], P),
                                ALU.mult).then_inc(norm_diag, 1)

            def take_rms(k):
                dve.wait_ge(norm_bc, k + 1)
                V.tensor_copy(rms[:], I34[:, 0:T]).then_inc(rms_ready, 1)
                dve.wait_ge(rms_ready, k + 1)

            def residual(m, k, n, bank, scale):
                dve.wait_ge(slab_done, n.value + 1)
                V.scalar_tensor_tensor(tile_of(h, m), I01[:, bank * T:(bank + 1) * T], scale, tile_of(h, m),
                                       ALU.mult, ALU.add).then_inc(h_updated, 1)

            def ffn(f):
                n0, nd = (N_FFN1, N_DOWN1) if f == 0 else (N_FFN2, N_DOWN2)

                def tile(ft, n, t):
                    if isinstance(ft, int):
                        norm_rms(2 * f)
                        lo(n + 3)
                        take_rms(2 * f)
                    dve.wait_ge(slab_done, n.value + 1)
                    V.tensor_tensor(hid[:, t, :], G[:, n.slot, :], rms[:], ALU.mult).then_inc(gate_scaled, 1)
                    if not isinstance(ft, int):
                        lo(n + 3)
                    dve.wait_ge(gate_rms, FT * f + ft + 1)
                    dve.wait_ge(slab_done, n.value + 2)
                    V.tensor_tensor(hid[:, t, :], G[:, (n + 1).slot, :], hid[:, t, :],
                                    ALU.mult).then_inc(hid_ready, 1)
                    dve.wait_ge(hh_ready, FT * f + ft + 1)
                    V.tensor_tensor(tile_of(HL, ft), hid[:, t, :], tile_of(HH, ft).bitcast(F32),
                                    ALU.subtract).then_inc(hl_ready, 1)
                    lo(n + 4)

                tile(0, At(n0), 0)
                with dve.Fori(0, FT // 3) as i:
                    for t in range(3):
                        tile(3 * i + t + 1, At(n0 + 2 * t + 2, i, 6), (t + 1) % 3)
                k = 1 if f == 0 else 3
                clear_acc(k)

                def down(m, n, t):
                    for c in range(3):
                        lo(n + 3 + c)
                    residual(m, k, n + 2, t, 0.5)
                    if f == 0:
                        raw_lo(m, 1)
                    accumulate(m, k, t)

                with dve.Fori(0, KT // 2 - 1) as i:
                    for t in range(2):
                        down(2 * i + t, At(nd + 3 * t, i, 6), t)
                for m in (KT - 2, KT - 1):
                    down(m, At(nd + 3 * m), m % 2)

            dt_step = [0]

            def dt_link(ins):
                dt_step[0] += 1
                ins.then_inc(dt_dve, 1)
                dve.wait_ge(dt_dve, dt_step[0])

            r0, r1, r2, r3, r4, r5 = (dtw[:, s, :] for s in range(6))
            dt_rows = SC[:, 4:8, :].rearrange("p j h -> p (j h)")

            def over_tiles(ap):
                return ap.unsqueeze(1).to_broadcast([P, TT, HS])

            def dt_logits():
                dve.wait_ge(dt_pe, 1)
                dt_link(V.tensor_tensor(r0.rearrange("p (j h) -> p j h", h=HS),
                                        I01[:, 0:128].rearrange("p (j h) -> p j h", h=HS),
                                        over_tiles(cst[:, C_DTB:C_DTB + HS]), ALU.add))
                dt_link(V.scalar_tensor_tensor(r1, r0, -1.0, r0, ALU.mult, ALU.max))
                assert dt_step[0] == DT_ABS

            def dt_softplus():
                dve.wait_ge(dt_act, 1)
                dt_link(V.tensor_scalar(r3, r2, 2.0, None, ALU.add))
                dt_link(V.reciprocal(r4, r3))
                dt_link(V.tensor_tensor(r5, r2, r4, ALU.mult))
                dt_link(V.tensor_tensor(r4, r5, r5, ALU.mult))
                dt_link(V.tensor_scalar(r3, r4, 1.0 / 17, None, ALU.mult))
                for odd in (15, 13, 11, 9, 7, 5, 3):
                    dt_link(V.scalar_tensor_tensor(r3, r3, 1.0 / odd, r4, ALU.add, ALU.mult))
                dt_link(V.scalar_tensor_tensor(r3, r3, 1.0, r5, ALU.add, ALU.mult))
                dt_link(V.tensor_scalar(r1, r0, 0.0, None, ALU.max))
                dt_link(V.scalar_tensor_tensor(dt_rows, r3, 2.0, r1, ALU.mult, ALU.add))
                dve.wait_ge(dt_act, 2)
                dt_link(V.scalar_tensor_tensor(SC[:, 0:4, :], SC[:, 4:8, :], -1.0, over_tiles(minus_a[:]),
                                               ALU.mult, ALU.mult))
                assert dt_step[0] == DA_READY, dt_step

            def dt_to_end():
                dve.wait_ge(dt_act, 6)
                te = SC[:, 8:12, :].rearrange("p j h -> p (j h)")
                dt_link(V.tensor_tensor(te, te, dt_rows, ALU.mult))
                dt_link(V.memset(SS[:, 0, :], 0.0))

            def raw_evict(t, n, wn):
                dve.wait_ge(slab_done, n.value + 1)
                V.tensor_tensor(XT[:, t, :], G[:, wn.slot, :], rms[:], ALU.mult).then_inc(g_free[wn.slot], 1)

            def norm_mixer():
                def scaled(m):
                    if m >= 2:
                        dve.wait_ge(ul_ready, 16 + m - 1)
                    V.scalar_tensor_tensor(ut[:, m % 2, :], h[:, m, :], cst[:, C_NM + m:C_NM + m + 1], rms[:],
                                           ALU.mult, ALU.mult).then_inc(ut_ready, 1)

                n, wn = At(N_SSM), At(W_SSM)
                norm_rms(1)
                lo(At(N_SMALL + 3))
                conv_consts(0)
                take_rms(1)
                V.tensor_tensor(LR[:], G[0:16, 0, :], rms[0:16, :], ALU.mult).then_inc(lr_ready, 1)
                V.tensor_tensor(dtv[32:64, :], G[32:64, 0, :], rms[32:64, :], ALU.mult).then_inc(g_free[0], 1)
                scaled(0)
                scaled(1)
                raw_evict(0, n, wn)
                lo(At(N_SMALL + 4))
                for m in range(2, KT):
                    scaled(m)
                raw_evict(1, n + 1, wn + 1)
                lo(At(N_SMALL + 5))

            def conv_consts(p):
                dve.wait_ge(sems["conv_begun"], last("conv_begun", p - 1))
                inc(V.tensor_scalar(gconv[:], cst[:, bass.ds(C_CONV + 20 * p, 20)], 0.5, None, ALU.mult), "conv_const")
                dve.wait_ge(sems["conv_const"], after("conv_const", p))

            def group_consts(g):
                dve.wait_ge(sems["ssm_hi"], last("ssm_hi", g - 1))
                dve.wait_ge(sems["ssm_lo"], last("ssm_lo", g - 1))
                V.tensor_copy(ggrp[:], cst[:, bass.ds(C_GRP + 6 * g, 6)])
                inc(V.tensor_copy(gsc[:], SC[:, :, bass.ds(HPG * g, HPG)]), "group_const")
                dve.wait_ge(sems["group_const"], after("group_const", g))
                dve.wait_ge(sems["intra_done"], last("intra_done", g - 1))
                da = gsc[:, 0:4, :].rearrange("p j r -> p (j r)")
                inc(V.tensor_tensor(M[:].rearrange("p j r t -> p (j r) t"), bc(da, CH),
                                    causal[:].unsqueeze(1).to_broadcast([P, TT * HPG, CH]), ALU.mult), "da_masked")

            def conv_taps(p, t, n, wn):
                raw = isinstance(p, int) and t < 2
                cv, src = CV[:, t % 2, :], XT[:, t, :] if raw else G[:, wn.slot, :]
                dve.wait_ge(sems["conv_begun"], after("conv_begun", p, t))
                for back in (1, 2, 3):
                    ins = V.scalar_tensor_tensor(cv[:, back:T], src[:, 0:T - back],
                                                 gconv[:, 5 * t + 3 - back:5 * t + 4 - back], cv[:, back:T],
                                                 ALU.mult, ALU.add)
                    if back < 3:
                        ins.then_inc(taps, 1)
                        taps_n[0] += 1
                        dve.wait_ge(taps, taps_at(taps_n[0]))
                ins.then_inc(raw_taps if raw else g_free[wn.slot], 1)

            taps_n = [0]
            taps_base = [lambda k: k]

            def taps_at(k):
                return taps_base[0](k)

            def conv_silu(p, t):
                dve.wait_ge(sems["conv_tanh"], after("conv_tanh", p, t))
                if t < 3:
                    dve.wait_ge(sems["cb_done" if t == 2 else "xb_turned"],
                                last("cb_done" if t == 2 else "xb_turned", p - 1))
                else:
                    dve.wait_ge(sems["inter_done"], last("inter_done", p - 1))
                dst = (XT[:, 0, :], XT[:, 1, :], BT[:], CT[:])[t]
                inc(V.scalar_tensor_tensor(dst, TH[:, t % 2, :], 1.0, CV[:, t % 2, :], ALU.add, ALU.mult), "conv_done")

            def z_silu(p, wn):
                for s in range(2):
                    dve.wait_ge(sems["z_tanh"], after("z_tanh", p, s))
                    V.scalar_tensor_tensor(ZS[:, 2 * s:2 * s + 2, :].rearrange("p j c -> p (j c)"), TH[:, s, :], 1.0,
                                           G[:, (wn + s).slot, :], ALU.add,
                                           ALU.mult).then_inc(g_free[(wn + s).slot], 1)

            def rows(k):
                return bc(gsc[:, 4 * k:4 * k + 4, :].rearrange("p j r -> p (j r)"), CH)

            def heads(ap):
                return ap.rearrange("p (q c) -> p q c", c=CH)

            def ssm_x(g):
                dve.wait_ge(sems["x_copied"], after("x_copied", g))
                dve.wait_ge(sems["intra_done"], last("intra_done", g - 1))
                inc(V.tensor_tensor(XDT[:].rearrange("p j (r c) -> p (j r) c", c=CH), heads(XD[:].rearrange("p j c -> p (j c)")), rows(1),
                                    ALU.mult), "xdt_ready")
                dve.wait_ge(sems["u_done"], last("u_done", g - 1))
                inc(V.tensor_tensor(XTE[:].rearrange("p j (r c) -> p (j r) c", c=CH), heads(XD[:].rearrange("p j c -> p (j c)")), rows(2),
                                    ALU.mult), "xte_ready")

            def ssm_m(g):
                dve.wait_ge(sems["cb_done"], after("cb_done", g))
                inc(V.tensor_tensor(CBM[:], I2[:, 0:256].rearrange("p (j t) -> p j t", t=CH),
                                    causal[:].unsqueeze(1).to_broadcast([P, TT, CH]), ALU.mult), "cb_masked")
                dve.wait_ge(sems["cb_masked"], after("cb_masked", g))
                dve.wait_ge(sems["decay_exp"], after("decay_exp", g))
                inc(V.tensor_tensor(M[:], M[:], CBM[:].unsqueeze(2).to_broadcast([P, TT, HPG, CH]), ALU.mult),
                    "m_ready")

            def ssm_chain(g):
                dve.wait_ge(sems["inter_done"], last("inter_done", g - 1))
                dve.wait_ge(sems["ssm_squares"], last("ssm_squares", g - 1))
                k = 0
                for c in range(7):
                    u = update(c)
                    dve.wait_ge(sems["u_done"], after("u_done", g, 0 if c < 4 else 1))
                    if c == 0:
                        inc(V.tensor_copy(SS[:, 1, :], u), "ssm_chain")
                        k += 1
                    else:
                        dve.wait_ge(sems["ssm_chain"], after("ssm_chain", g, k - 1))
                        inc(V.tensor_tensor(heads(ST[:]), heads(SS[:, c, :]), bc(gsc[:, 16 + c, :], CH), ALU.mult),
                            "ssm_chain")
                        k += 1
                        dve.wait_ge(sems["ssm_chain"], after("ssm_chain", g, k - 1))
                        inc(V.tensor_tensor(SS[:, c + 1, :], ST[:], u, ALU.add), "ssm_chain")
                        k += 1
                assert k == PER["ssm_chain"]

            def ssm_y(g):
                dve.wait_ge(sems["inter_done"], after("inter_done", g))
                dve.wait_ge(sems["ssm_turned"], last("ssm_turned", g - 1))
                yf = Y[:].rearrange("p j c -> p (j c)")
                inc(V.tensor_tensor(heads(yf), heads(I34[:]), rows(3), ALU.mult), "ssm_y")
                dve.wait_ge(sems["ssm_y"], after("ssm_y", g, 0))
                dve.wait_ge(sems["intra_done"], after("intra_done", g))
                inc(V.tensor_tensor(yf, yf, I01[:], ALU.add), "ssm_y")
                dve.wait_ge(sems["ssm_y"], after("ssm_y", g, 1))
                dve.wait_ge(sems["xd_ready"], after("xd_ready", g))
                inc(V.tensor_tensor(yf, yf, XD[:].rearrange("p j c -> p (j c)"), ALU.add), "ssm_y")
                dve.wait_ge(sems["ssm_y"], after("ssm_y", g, 2))
                inc(V.tensor_tensor(yf, yf, ZS[:].rearrange("p j c -> p (j c)"), ALU.mult), "ssm_y")

            def ssm_scale(g):
                dve.wait_ge(sems["ssm_squares"], last("ssm_squares", g))
                inc(V.tensor_scalar(var4[:], ss4[:], 1.0 / 256, 4 * EPS, ALU.mult, ALU.add), "ssm_var")
                dve.wait_ge(sems["ssm_rstd"], last("ssm_rstd", g))
                for j in range(TT):
                    inc(V.tensor_scalar(Y[:, j, :], Y[:, j, :], rstd4[:, j:j + 1], None, ALU.mult), "ssm_scaled")

            def evict_lo(src, dH, dL, k0, scale, hi_name, g, name):
                for f in range(2):
                    dve.wait_ge(sems[hi_name], after(hi_name, g, f))
                    inc(V.scalar_tensor_tensor(tile_of(dL, k0 + f), src[:, f * T:(f + 1) * T], scale[f],
                                               tile_of(dH, k0 + f).bitcast(F32), ALU.mult, ALU.subtract), name)

            def take_output(wn, gate_wn, n, slot, nt):
                dve.wait_ge(g_free[gate_wn.slot], gate_wn.read)
                dve.wait_ge(slab_done, n.value + 1)
                dst = gate_th[:, slot, :] if nt is None else tile_of(merged, nt)
                V.scalar_tensor_tensor(dst, gate_th[:, slot, :], 1.0, G[:, wn.slot, :],
                                       ALU.add, ALU.mult).then_inc(g_free[wn.slot], 1)

            def merge2_part(nt, kind, n, wn, gate_wn):
                if kind in (1, 3):
                    take_output(wn, gate_wn, n, kind // 2, None)
                    dve.wait_ge(g_free[wn.slot], wn.read)
                    if kind == 3:
                        dve.wait_ge(m_sum, nt + 1)
                    V.tensor_tensor(tile_of(merged, nt), tile_of(merged, nt), gate_th[:, kind // 2, :],
                                    ALU.add).then_inc(m_final if kind == 3 else m_sum, 1)
                lo(n + 3)
                if kind == 3:
                    dve.wait_ge(mh_ready, nt + 1)
                    V.scalar_tensor_tensor(tile_of(ML, nt), tile_of(merged, nt), 0.5, tile_of(MH, nt).bitcast(F32),
                                           ALU.mult, ALU.subtract).then_inc(ml_ready, 1)

            def merge2_head(k):
                nt, kind = MERGE2_HEAD[k]
                gate = MERGE2_HEAD.index((nt, kind - kind % 2))
                merge2_part(nt, kind, At(N_MERGE2 + k), At(W_MERGE2 + k), At(W_MERGE2 + gate))

            clear_acc(0)
            dve.wait_ge(cst_landed, 16)
            V.tensor_scalar(half_gate_bias[:], cst[:, C_GATE:C_GATE + 3 * KT], 0.5, None,
                            ALU.mult).then_inc(half_bias, 1)
            lo(At(0))
            for m in range(KT):
                raw_lo(m, 0)
            lo(At(1))
            for m in range(KT):
                accumulate(m, 0, m % 2)
                if m == 1:
                    lo(At(2))
            dve.wait_ge(consts, N_CONSTS)
            ffn(0)
            norm_mixer()

            def ssm_proj(p, n, wn, inner):
                if inner is not None:
                    conv_consts(p)
                if inner is not None:
                    group_consts(inner)
                for t in range(4):
                    conv_taps(p, t, n + t, wn + t)
                    if inner is None and t == 0:
                        dt_logits()
                    if inner is not None or t >= 2:
                        lo(n + t + 3)
                    if inner is not None:
                        if t == 0:
                            ssm_x(inner)
                        if t == 1:
                            ssm_m(inner)
                            ssm_chain(inner)
                        if t == 3:
                            ssm_y(inner)
                    conv_silu(p, t)
                    if inner is None and t == 1:
                        dt_softplus()
                if inner is None:
                    dt_to_end()
                else:
                    ssm_scale(inner)
                z_silu(p, wn + 4)
                lo(n + 7)
                lo(n + 8)
                if inner is not None:
                    evict_lo(I01, SH, SL, 2 * inner, ssm_norm_cols, "ssm_hi", inner, "ssm_lo")

            ssm_norm_cols = [ggrp[:, f:f + 1] for f in range(2)]
            gla_norm_cols = [cst[:, C_GN + f:C_GN + f + 1] for f in range(2)]
            ssm_proj(0, At(N_SSM), At(W_SSM), None)
            with dve.Fori(0, NG - 1) as i:
                taps_n[0] = 0
                taps_base[0] = lambda k: 8 * i + 8 + k
                ssm_proj(i + 1, At(N_SSM + 6, i, 6), At(W_SSM + 6, i, 6), i)
            g = NG - 1
            n, wn = At(N_MERGE1), At(W_MERGE1)
            group_consts(g)
            lo(n + 3)
            ssm_x(g)
            ssm_m(g)
            ssm_chain(g)
            lo(n + 4)
            ssm_y(g)
            lo(n + 5)
            ssm_scale(g)
            evict_lo(I01, SH, SL, 2 * g, ssm_norm_cols, "ssm_hi", g, "ssm_lo")
            lo(n + 6)
            take_output(wn + 1, wn, n + 4, 0, 0)
            lo(n + 7)
            take_output(wn + 3, wn + 2, n + 5, 1, 1)
            lo(n + 8)

            dve.wait_ge(gk_pe, 1)
            for hd in range(HG):
                src = (I01[:, 0:T], I01[:, T:], I34[:, 0:T], I34[:, T:])[hd]
                V.tensor_scalar(BB[:, hd, :], src, cst[:, C_GB + hd:C_GB + hd + 1], None, ALU.add).then_inc(gk_dve, 1)
                dve.wait_ge(gk_dve, 2 * hd + 1)
                V.scalar_tensor_tensor(EX[:, hd, :], BB[:, hd, :], -1.0, BB[:, hd, :], ALU.mult,
                                       ALU.max).then_inc(gk_dve, 1)

            with dve.Fori(0, 2) as i:
                for t in range(3):
                    n, wn = At(N_MERGE1 + 6 + 3 * t, i, 9), At(W_MERGE1 + 4 + 2 * t, i, 6)
                    lo(n + 3)
                    lo(n + 4)
                    take_output(wn + 1, wn, n + 2, (2 + t) % 3, 3 * i + t + 2)
                    lo(n + 5)

            k = 2 * HG
            assert k == GK_EVICTED
            dve.wait_ge(gk_pool, 2)
            for hd in range(HG):
                dve.wait_ge(gk_act, 2 * hd + 2)
                V.scalar_tensor_tensor(TB[:, hd % 2, :], BB[:, hd, :], 0.0, EX[:, hd, :], ALU.min,
                                       ALU.subtract).then_inc(gk_dve, 1)
                k += 1
                dve.wait_ge(gk_dve, k)
                V.tensor_tensor_scan(BB[:, hd, :], RM[:], TB[:, hd % 2, :], 0.0, ALU.mult, ALU.add).then_inc(gk_dve, 1)
                k += 1
                dve.wait_ge(gk_dve, k)
            V.memset(GS[:, 0, :], 0.0).then_inc(gk_dve, 1)

            def chunks(ap):
                return ap.rearrange("p (c t) -> p c t", t=CH)

            def gla_proj(p, n, wn, inner):
                dve.wait_ge(sems["gla_exp"], last("gla_exp", p - 1))
                b3 = chunks(BB[:, p, :])
                inc(V.tensor_tensor(chunks(TB[:, 0, :]), b3, bc(b3[:, :, CH // 2], CH), ALU.subtract), "gla_t")
                inc(V.tensor_tensor(chunks(TB[:, 1, :]), bc(b3[:, :, CH - 1], CH), b3, ALU.subtract), "gla_t")
                lo(n + 3)
                if inner is not None:
                    gla_a_chain(inner)
                dve.wait_ge(sems["gla_exp"], after("gla_exp", p))
                dve.wait_ge(g_free[wn.slot], wn.read)
                dve.wait_ge(sems["gla_a_done"], last("gla_a_done", p - 1))
                inc(V.scalar_tensor_tensor(QH[:], QR[:], GLA_SCALE, EX[:, 0, :], ALU.mult, ALU.mult), "gla_qh")
                dve.wait_ge(sems["gla_o_done"], last("gla_o_done", p - 1))
                inc(V.scalar_tensor_tensor(QT[:], QR[:], GLA_SCALE, EX[:, 2, :], ALU.mult, ALU.mult), "gla_qt")
                lo(n + 4)
                lo(n + 5)
                if inner is not None:
                    gla_out(inner)
                dve.wait_ge(slab_done, n.value + 4)
                dve.wait_ge(sems["gla_kt_turned"], last("gla_kt_turned", p - 1))
                inc(V.tensor_tensor(KH[:], G[:, (wn + 3).slot, :], EX[:, 1, :], ALU.mult), "gla_kh")
                V.tensor_tensor(KT_[:], G[:, (wn + 3).slot, :], EX[:, 3, :], ALU.mult).then_inc(g_free[(wn + 3).slot], 1)
                lo(n + 6)
                dve.wait_ge(sems["gla_o_ready"], last("gla_o_ready", p - 1))
                for s in range(2):
                    dve.wait_ge(sems["gla_r_tanh"], after("gla_r_tanh", p, s))
                    V.scalar_tensor_tensor(GR[:, 2 * s:2 * s + 2, :].rearrange("p j c -> p (j c)"), GTH[:, s, :], 1.0,
                                           G[:, (wn + 4 + s).slot, :], ALU.add,
                                           ALU.mult).then_inc(g_free[(wn + 4 + s).slot], 1)
                lo(n + 7)
                lo(n + 8)
                if inner is not None:
                    evict_lo(I34, GH, GL, 2 * inner, gla_norm_cols, "gla_hi", inner, "gla_lo")

            def gla_a_chain(hd):
                dve.wait_ge(sems["gla_a_done"], after("gla_a_done", hd))
                inc(V.tensor_tensor(GA[:], I2[:, 0:256].rearrange("p (j t) -> p j t", t=CH),
                                    causal[:].unsqueeze(1).to_broadcast([P, TT, CH]), ALU.mult), "gla_a_masked")
                for c in range(7):
                    u = update(c)
                    dve.wait_ge(sems["gla_u_done"], after("gla_u_done", hd, 0 if c < 4 else 1))
                    if c:
                        dve.wait_ge(sems["gla_chain"], after("gla_chain", hd, c - 1))
                    inc(V.scalar_tensor_tensor(GS[:, c + 1, :], GS[:, c, :], EL[:, c:c + 1], u, ALU.mult, ALU.add),
                        "gla_chain")

            def gla_out(hd):
                dve.wait_ge(sems["gla_squares"], last("gla_squares", hd))
                inc(V.tensor_scalar(var4[:], gss4[:], 4.0 / 256, 4 * EPS, ALU.mult, ALU.add), "gla_var")
                dve.wait_ge(sems["gla_rstd"], last("gla_rstd", hd))
                dve.wait_ge(sems["gla_turned"], last("gla_turned", hd - 1))
                for j in range(TT):
                    inc(V.scalar_tensor_tensor(GO[:, j, :], I01[:, j * 256:(j + 1) * 256], rstd4[:, j:j + 1],
                                               GR[:, j, :], ALU.mult, ALU.mult), "gla_o_ready")

            for p in range(HG):
                gla_proj(p, At(N_GLA + 6 * p), At(W_GLA + 6 * p), p - 1 if p else None)
            def att_score(q, e):
                hd = 4 * q + e
                s = hd % 2
                dve.wait_ge(sems["att_s"], after("att_s", q, e))
                dve.wait_ge(bias_landed[s], 32 * (hd // 2 + 1))
                dve.wait_ge(bias_masked, s + 1)
                dve.wait_ge(sems["att_turned"], after("att_turned", q, e - 1))
                for k, i in enumerate((3, 2, 0, 1)):
                    src = {3: I01[:, 0:512], 2: I01[:, 512:896], 0: I01[:, 896:1024], 1: I2[:, 0:256]}[i]
                    o, wd = P_OFF[i], (i + 1) * P
                    inc(V.tensor_tensor_reduce(out=PR[:, o:o + wd], in0=src, in1=bias[:, s, T - wd:T], scale=1.0,
                                               scalar=-3.0e38, op0=ALU.add, op1=ALU.max,
                                               accum_out=mx[:, i:i + 1]), "att_scored")
                dve.wait_ge(sems["att_scored"], 16 * (q + 1) + 4 * e + 4)
                dve.wait_ge(sems["att_p"], after("att_p", q, e - 1))
                inc(V.tensor_scalar(ngm[:], mx[:], -1.0, None, ALU.mult), "att_neg")

            def att_rest(q, e):
                dve.wait_ge(sems["att_p"], after("att_p", q, e))
                dve.wait_ge(sems["att_o"], after("att_o", q, e - 1))
                inc(V.reciprocal(rc[:], rs[:]), "att_recip")
                dve.wait_ge(sems["att_turned"], after("att_turned", q, e))
                dve.wait_ge(sems["att_pv"], after("att_pv", q, e - 1))
                inc(V.tensor_copy(PT[:, T:2 * T], I34[:, T:2 * T]), "att_pt_b")
                inc(V.tensor_copy(PT[:, 2 * T:2 * T + 256], I2[:, 256:512]), "att_pt_b")
                dve.wait_ge(sems["att_recip"], after("att_recip", q, e))
                if e == 0:
                    dve.wait_ge(sems["att_o_turned"], last("att_o_turned", q - 1))
                dve.wait_ge(sems["att_pv"], after("att_pv", q, e))
                inc(V.tensor_tensor(AO[:, :, e * CH:(e + 1) * CH],
                                    I01[:, 0:256].rearrange("p (j c) -> p j c", c=CH), bc(rc[:], CH), ALU.mult),
                    "att_o")

            hd = HG - 1
            lo(At(N_ATT + 3))
            gla_a_chain(hd)
            lo(At(N_ATT + 4))
            lo(At(N_ATT + 5))
            gla_out(hd)
            lo(At(N_ATT + 6))
            evict_lo(I34, GH, GL, 2 * hd, gla_norm_cols, "gla_hi", hd, "gla_lo")
            lo(At(N_ATT + 7))
            lo(At(N_ATT + 8))
            for q in range(NQ):
                n = At(N_ATT + 6 * (q + 1))
                for e in range(4):
                    att_score(q, e)
                    if q + 1 < NQ:
                        lo(n + e + 3)
                    else:
                        merge2_head(e)
                    att_rest(q, e)
                if q + 1 < NQ:
                    lo(n + 7)
                    lo(n + 8)
                else:
                    merge2_head(4)
                evict_lo(I34, AH, AL, 2 * q, (1.0, 1.0), "att_hi", q, "att_lo")

            for k in range(5, 8):
                merge2_head(k)
            with dve.Fori(0, 2) as i:
                for k in range(12):
                    wn = At(W_MERGE2 + 8 + k, i, 12)
                    merge2_part(3 * i + k // 4 + 2, k % 4, At(N_MERGE2 + 8 + k, i, 12), wn, wn + (-(k % 2)))
            clear_acc(2)
            for m in range(KT):
                lo(At(N_OUT + m + 3))
                residual(m, 2, At(N_OUT + m), m % 2, 1.0)
                raw_lo(m, 3)
                accumulate(m, 2, m % 2)
            ffn(1)
            norm_rms(3)
            dve.wait_ge(norm_bc, 4)
            for m in range(KT):
                V.scalar_tensor_tensor(h[:, m, :], h[:, m, :], cst[:, C_NF + m:C_NF + m + 1], I34[:, 0:T],
                                       ALU.mult, ALU.mult).then_inc(out_ready, 1)


N_CONSTS = 10
DT_ABS, DA_READY = 2, 18
GK_EVICTED = 2 * HG
P_OFF = {3: 0, 2: 512, 0: 896, 1: 1024}
PT_OFF = {0: 0, 1: 512, 3: 896, 2: 1024}
MAX_REL = 256


def fm_slabs(w):
    k = w.shape[0] // P
    return np.ascontiguousarray(w.reshape(k, P, -1, P).transpose(2, 1, 0, 3)).reshape(-1, P, k * P)


def tm_slabs(w):
    t = w.reshape(2, 4, P, -1, 256).transpose(3, 0, 2, 1, 4)
    return np.ascontiguousarray(t).reshape(-1, P, SLAB)


def down_slabs(w):
    t = fm_slabs(w)
    out = np.zeros((t.shape[0], 3, P, SLAB), np.float32)
    for c, (k0, k1) in enumerate(DOWN_K):
        out[:, c, :, 0:(k1 - k0) * P] = t[:, :, k0 * P:k1 * P]
    return out.reshape(-1, P, SLAB)


def interleave(*parts):
    return np.concatenate(parts, axis=1).reshape(-1, P, SLAB)


def lay_out(i):
    sizes = (512, 512, 1024, 1024, 16, 2048, 4096, 32, 1024, 1024, 1024, 3072)
    ends = np.cumsum(sizes)
    win = i["w_in"][0]
    q, k, v, r, lr, z, xbc, dt, aq, ak, av, gates = (win[:, e - s:e] for s, e in zip(sizes, ends))
    small = np.zeros((D, P), np.float32)
    small[:, 0:16] = lr
    small[:, 32:64] = dt
    gate = fm_slabs(gates).reshape(3, KT, 1, P, SLAB)

    def rounds(s, n):
        return s.reshape(n, -1, P, SLAB)

    xb = fm_slabs(xbc)
    aq_s, ak_s = rounds(fm_slabs(aq), NQ), rounds(fm_slabs(ak), NQ)
    ws = fm_slabs(i["w_branch_ssm"][0]).reshape(KT, P, 2, SLAB).transpose(0, 2, 1, 3)
    merge1 = interleave(gate[1], ws)
    merge1[:6] = merge1[[0, 1, 3, 4, 2, 5]]
    merge2 = interleave(gate[0], rounds(fm_slabs(i["w_branch_gla"][0]), KT), gate[2],
                        rounds(fm_slabs(i["w_branch_attn"][0]), KT))
    merge2[:8] = merge2[[4 * nt + kind for nt, kind in MERGE2_HEAD]]
    stream = [
        interleave(rounds(fm_slabs(i["ffn1_w_gate"][0]), FT), rounds(fm_slabs(i["ffn1_w_up"][0]), FT)),
        down_slabs(i["ffn1_w_down"][0]),
        fm_slabs(small),
        interleave(rounds(xb[0:16], NG), rounds(xb[16:24], NG), rounds(xb[24:32], NG), rounds(tm_slabs(z), NG)),
        merge1,
        interleave(rounds(fm_slabs(q), HG), rounds(tm_slabs(v), HG), rounds(fm_slabs(k), HG), rounds(tm_slabs(r), HG)),
        interleave(aq_s[:, 0:1], ak_s[:, 0:1], aq_s[:, 1:2], ak_s[:, 1:2], rounds(tm_slabs(av), NQ)),
        merge2,
        fm_slabs(i["w_out"][0]),
        interleave(rounds(fm_slabs(i["ffn2_w_gate"][0]), FT), rounds(fm_slabs(i["ffn2_w_up"][0]), FT)),
        down_slabs(i["ffn2_w_down"][0]),
    ]
    slabs = np.concatenate(stream)
    assert slabs.shape[0] == N_SLABS, slabs.shape

    cst = np.zeros((P, NCST), np.float32)

    def cols(at, vec):
        cst[:, at:at + vec.size // P] = vec.reshape(-1, P).T

    cols(C_N1, i["ffn1_norm"][0])
    cols(C_NM, i["mix_norm"][0])
    cols(C_N2, i["ffn2_norm"][0])
    cols(C_NF, i["final_norm"])
    cols(C_GN, i["gla_norm"][0])
    cols(C_GB, i["gla_b_gk"][0])
    cols(C_GATE, i["gate_bias"][0])
    taps = np.concatenate([i["ssm_conv_w"][0], i["ssm_conv_b"][0][None]])
    taps = taps.reshape(5, 32, P).transpose(2, 1, 0)
    sn = i["ssm_norm"][0].reshape(NG, 2, P)
    for g in range(NG):
        for t, tile in enumerate((2 * g, 2 * g + 1, 16 + g, 24 + g)):
            cst[:, C_CONV + 20 * g + 5 * t:C_CONV + 20 * g + 5 * t + 5] = taps[:, tile]
        cst[:, C_GRP + 6 * g:C_GRP + 6 * g + 2] = sn[g].T
        cst[:, C_GRP + 6 * g + 2:C_GRP + 6 * g + 6] = i["ssm_D"][0][None, HPG * g:HPG * g + HPG]
    cst[:, C_ALOG:C_DTB] = i["ssm_A_log"][0][None]
    cst[:, C_DTB:] = i["ssm_dt_bias"][0][None]

    distance = np.arange(P)[:, None] + T - P - np.arange(T)[None, :]
    rel = np.ascontiguousarray(i["attn_rel_bias"][0][np.minimum(distance, MAX_REL) + MAX_REL].transpose(2, 0, 1))
    x = np.ascontiguousarray(i["x"][0].reshape(T, KT, P).transpose(2, 1, 0))
    return {"slabs": slabs, "cst": cst, "rel": rel, "x": x, "wgk": np.ascontiguousarray(i["gla_w_gk"][0])}


def kernel(**inputs):
    from concourse import bacc
    from concourse.bass_utils import run_bass_kernel_spmd

    arrays = lay_out({k: np.asarray(v) for k, v in inputs.items()})
    nc = bacc.Bacc("TRN2", target_bir_lowering=False, num_devices=1, dynamic_dma_scratch_size=1024)
    aps = {n: nc.dram_tensor(f"in_{n}", v.shape, mybir.dt.from_np(v.dtype), kind="ExternalInput").ap()
           for n, v in arrays.items()}
    out = nc.dram_tensor("out_y", (P, KT, T), F32, kind="ExternalOutput").ap()
    build(nc, aps, out)
    r = run_bass_kernel_spmd(nc, [{f"in_{n}": v for n, v in arrays.items()}], core_ids=[0])
    y = r.results[0]["out_y"]
    return np.ascontiguousarray(y.transpose(2, 1, 0)).reshape(1, T, D)
```

```python
from contextlib import ExitStack

import numpy as np
import concourse.bass as bass
from concourse import mybir

F32 = mybir.dt.float32
F32R = mybir.dt.float32r
ALU = mybir.AluOpType
ACT = mybir.ActivationFunctionType

P = 128
T = 512
D = 1024
KT = D // P
FFN = 2816
FT = FFN // P
TT = T // P
CH = 64
NCH = T // CH
HG = 4
NG = 8
HPG = 4
HS = NG * HPG
NQ = 4
EPS = 1e-6
GLA_SCALE = 128 ** -0.5
GATE_NORM = 16.0
ATT_SCALE = 64 ** -0.5
MASKED = -1.0e30
SLAB = 1024
RING = 3
LR_ROWS = 96

N_FFN1 = 0
N_DOWN1 = N_FFN1 + 2 * FT
N_SMALL = N_DOWN1 + 3 * KT
N_SSM = N_SMALL + 1
N_MERGE1 = N_SSM + 6 * NG
N_GLA = N_MERGE1 + 3 * KT
N_ATT = N_GLA + 6 * HG
N_MERGE2 = N_ATT + 6 * NQ
N_OUT = N_MERGE2 + 4 * KT
N_FFN2 = N_OUT + KT
N_DOWN2 = N_FFN2 + 2 * FT
N_SLABS = N_DOWN2 + 3 * KT
DOWN_K = ((0, 8), (8, 15), (15, 22))

W_SSM = 1
W_MERGE1 = W_SSM + 6 * NG
W_GLA = W_MERGE1 + 2 * KT
W_ATT = W_GLA + 6 * HG
W_MERGE2 = W_ATT + 6 * NQ
MERGE2_HEAD = ((0, 0), (0, 1), (0, 2), (1, 0), (1, 1), (1, 2), (0, 3), (1, 3))

C_N1, C_NM, C_N2, C_NF, C_GN, C_GB, C_GATE, C_CONV, C_GRP = 0, 8, 16, 24, 32, 34, 38, 64, 224
C_ALOG = C_GRP + 6 * NG
C_DTB = C_ALOG + HS
NCST = C_DTB + HS


class At:

    def __init__(self, k, i=0, per=0):
        self.k, self.i, self.per = k, i, per

    def __add__(self, d):
        return At(self.k + d, self.i, self.per)

    @property
    def value(self):
        return self.k + self.per * self.i if self.per else self.k

    @property
    def slot(self):
        return self.k % RING

    @property
    def turn(self):
        return self.k // RING + ((self.per // RING) * self.i if self.per else 0)

    @property
    def free(self):
        return self.turn + 1

    @property
    def read(self):
        return self.turn + 2


ROUND = {
    "scalar": {
        "conv_begun": 4, "conv_tanh": 4, "x_copied": 1, "b_copied": 1, "decay_exp": 1, "z_tanh": 2,
        "ssm_squares": 4, "ssm_hi": 2,
        "gla_exp": 1, "gla_kt_copied": 1, "gla_r_tanh": 2, "gla_squares": 4, "gla_hi": 2,
        "att_p": 4, "att_pt_a": 4, "att_hi": 2,
    },
    "vector": {
        "conv_const": 1, "group_const": 1, "group_norm": 1, "da_masked": 1, "xdt_ready": 1, "xte_ready": 1, "cb_masked": 1,
        "m_ready": 1, "conv_done": 4, "ssm_chain": 13, "ssm_y": 4, "ssm_var": 1, "ssm_scaled": 4, "ssm_lo": 2,
        "gla_t": 2, "gla_qh": 1, "gla_qt": 1, "gla_kh": 1, "gla_a_masked": 1, "gla_chain": 7, "gla_var": 1,
        "gla_o_ready": 4, "gla_lo": 2,
        "att_scored": 16, "att_neg": 4, "att_recip": 4, "att_pt_b": 8, "att_o": 4, "att_lo": 2,
    },
    "gpsimd": {"xd_ready": 1, "ssm_rstd": 1, "gla_rstd": 1},
    "tensor": {
        "xb_turned": 1, "seg_done": 1, "cb_done": 1, "u_done": 2, "intra_done": 1, "inter_done": 1,
        "ssm_turned": 1,
        "gla_a_done": 1, "gla_kt_turned": 1, "gla_u_done": 2, "gla_o_done": 1, "gla_turned": 1,
        "att_s": 4, "att_turned": 4, "att_pv": 4, "att_o_turned": 1,
    },
}
PER = {name: k for sems in ROUND.values() for name, k in sems.items()}


def after(name, r, j=0):
    return PER[name] * (r + 1) + j + 1


def last(name, r):
    return PER[name] * (r + 1) + PER[name] if not isinstance(r, int) or r >= 0 else PER[name]


def build(nc, a, out):
    ctx = ExitStack()
    with ctx:
        def sb(name, shape, dt=F32, stack=None):
            return (stack or ctx).enter_context(nc.sbuf_tensor(name, shape, dt))

        h = sb("h", [P, KT, T])
        UH = sb("UH", [P, KT, T], F32R)
        UL = sb("UL", [P, KT, T], F32R)
        RAW = sb("RAW", [P, RING, SLAB])
        WH = sb("WH", [P, RING, SLAB], F32R)
        WL = sb("WL", [P, RING, SLAB], F32R)
        cst = sb("cst", [P, NCST])
        half_gate_bias = sb("half_gate_bias", [P, 3 * KT])
        ident = sb("ident", [P, P])
        ones = sb("ones", [P, P])
        after_s = sb("after_s", [P, P])
        upto_t = sb("upto_t", [P, P])
        causal = sb("causal", [P, CH])
        minus_half = sb("minus_half", [P, TT])
        LR = sb("LR", [LR_ROWS, T], F32R)
        var4 = sb("var4", [P, TT])
        rstd4 = sb("rstd4", [P, TT])
        SC = sb("SC", [P, 24, HS])
        gconv = sb("gconv", [P, 20])
        ggrp = sb("ggrp", [P, 6])
        gsc = sb("gsc", [P, 24, HPG])
        minus_a = sb("minus_a", [P, HS])
        ut = sb("ut", [P, 3, T])
        gate_th = ut
        wgk_raw = ut[0:LR_ROWS, 2, :]
        WGK = sb("WGK", [LR_ROWS, 512], F32R)
        rms = sb("rms", [P, T])

        r = ExitStack()
        acc = sb("acc", [P, T], F32, r)
        acc_pool = sb("acc_pool", [P, T], F32, r)
        sq_pool = sb("sq_pool", [P, T], F32, r)
        sq = sb("sq", [P, 2, T], F32, r)
        diag = sb("diag", [P, TT, P], F32, r)
        HH = sb("HH", [P, FT, T], F32R, r)
        HL = sb("HL", [P, FT, T], F32R, r)
        hid = sb("hid", [P, RING, T], F32, r)
        r.close()

        r = ExitStack()
        SH = sb("SH", [P, 2 * NG, T], F32R, r)
        SL = sb("SL", [P, 2 * NG, T], F32R, r)
        w = ExitStack()
        XT = sb("XT", [P, 2, T], F32, w)
        BT = sb("BT", [P, T], F32, w)
        CT = sb("CT", [P, T], F32, w)
        CV = sb("CV", [P, 2, T], F32, w)
        TH = sb("TH", [P, 2, T], F32, w)
        ZS = sb("ZS", [P, TT, 256], F32, w)
        prep = ExitStack()
        dtv = sb("dtv", [P, T], F32, prep)
        dtw = sb("dtw", [P, 6, P], F32, prep)
        prep.close()
        XDT = sb("XDT", [P, TT, 256], F32, w)
        XTE = sb("XTE", [P, TT, 256], F32, w)
        XD = sb("XD", [P, TT, 256], F32, w)
        BK = sb("BK", [P, TT, P], F32, w)
        M = sb("M", [P, TT, HPG, CH], F32, w)
        CBM = sb("CBM", [P, TT, CH], F32, w)
        SS = sb("SS", [P, NCH, 256], F32, w)
        ST = sb("ST", [P, 256], F32, w)
        Y = sb("Y", [P, TT, 256], F32, w)
        ssm_dump = sb("ssm_dump", [P, 256], F32, w)
        ss4 = sb("ss4", [P, TT], F32, w)
        w.close()
        r.close()

        r = ExitStack()
        GH = sb("GH", [P, KT, T], F32R, r)
        GL = sb("GL", [P, KT, T], F32R, r)
        w = ExitStack()
        KK = sb("KK", [P, TT, P], F32, w)
        GV = sb("GV", [P, TT, 256], F32, w)
        GR = sb("GR", [P, TT, 256], F32, w)
        GTH = sb("GTH", [P, 2, T], F32, w)
        GA = sb("GA", [P, TT, CH], F32, w)
        GS = sb("GS", [P, NCH, 256], F32, w)
        GO = sb("GO", [P, TT, 256], F32, w)
        EL = sb("EL", [P, NCH], F32, w)
        gss4 = sb("gss4", [P, TT], F32, w)
        gla_dump = sb("gla_dump", [P, 256], F32, w)
        w.close()
        AH = sb("AH", [P, KT, T], F32R, r)
        AL = sb("AL", [P, KT, T], F32R, r)
        merged = sb("merged", [P, KT, T], F32, r)
        w = ExitStack()
        BB = sb("BB", [P, HG, T], F32, w)
        EX = sb("EX", [P, 4, T], F32, w)
        TB = sb("TB", [P, 2, T], F32, w)
        RM = sb("RM", [P, T], F32, w)
        QR = sb("QR", [P, T], F32, w)
        QT = sb("QT", [P, T], F32, w)
        QH = sb("QH", [P, T], F32, w)
        KH = sb("KH", [P, T], F32, w)
        KT_ = sb("KT_", [P, T], F32, w)
        w.close()
        w = ExitStack()
        AQ, AK = [None, None], [None, None]
        AQ[0] = sb("AQ0", [P, 2, T], F32, w)
        AK[0] = sb("AK0", [P, 2, T], F32, w)
        AV = sb("AV", [P, TT, 256], F32, w)
        bias = sb("bias", [P, 2, T], F32, w)
        AQ[1] = sb("AQ1", [P, 2, T], F32, w)
        AK[1] = sb("AK1", [P, 2, T], F32, w)
        PR = sb("PR", [P, 1280], F32, w)
        PT = sb("PT", [P, 1280], F32, w)
        AO = sb("AO", [P, TT, 256], F32, w)
        mx = sb("mx", [P, TT], F32, w)
        ngm = sb("ngm", [P, TT], F32, w)
        rs = sb("rs", [P, TT], F32, w)
        rc = sb("rc", [P, TT], F32, w)
        w.close()
        w = ExitStack()
        MH = sb("MH", [P, KT, T], F32R, w)
        ML = sb("ML", [P, KT, T], F32R, w)
        w.close()
        r.close()
        G = ctx.enter_context(nc.psum_tensor("G", [P, 3, T], F32))
        I01 = ctx.enter_context(nc.psum_tensor("I01", [P, 2 * T], F32))
        I2 = ctx.enter_context(nc.psum_tensor("I2", [P, T], F32))
        I34 = ctx.enter_context(nc.psum_tensor("I34", [P, 2 * T], F32))

        sems = {}

        def sem(name):
            sems[name] = ctx.enter_context(nc.semaphore(name))
            return sems[name]

        slab_landed = [sem(f"slab_landed{s}") for s in range(RING)]
        split_hi, split_lo, slab_done = sem("split_hi"), sem("split_lo"), sem("slab_done")
        g_free = [sem(f"g_free{s}") for s in range(3)]
        gate_scaled, gate_ready, gate_rms, hid_ready, hh_ready, hl_ready = (
            sem("gate_scaled"), sem("gate_ready"), sem("gate_rms"), sem("hid_ready"), sem("hh_ready"), sem("hl_ready"))
        h_updated, squared, acc_updated = sem("h_updated"), sem("squared"), sem("acc_updated")
        acc_clear = sem("acc_clear")
        norm_sums, norm_var, norm_rstd, norm_diag, norm_bc = (
            sem("norm_sums"), sem("norm_var"), sem("norm_rstd"), sem("norm_diag"), sem("norm_bc"))
        ut_ready, uh_ready, ul_ready = sem("ut_ready"), sem("uh_ready"), sem("ul_ready")
        rms_ready, raw_read, raw_taps = sem("rms_ready"), sem("raw_read"), sem("raw_taps")
        x_landed = [sem(f"x_landed{s}") for s in range(KT // 2)]
        cst_landed, wgk_landed, wgk_split, lr_split = (
            sem("cst_landed"), sem("wgk_landed"), sem("wgk_split"), sem("lr_split"))
        consts, half_bias, lr_ready = sem("consts"), sem("half_bias"), sem("lr_ready")
        m_sum, m_final, mh_ready, ml_ready = sem("m_sum"), sem("m_final"), sem("mh_ready"), sem("ml_ready")
        out_ready, stored = sem("out_ready"), sem("stored")
        dt_act, dt_dve, dt_pe, dt_pool = sem("dt_act"), sem("dt_dve"), sem("dt_pe"), sem("dt_pool")
        gk_act, gk_dve, gk_pe, gk_pool = sem("gk_act"), sem("gk_dve"), sem("gk_pe"), sem("gk_pool")
        bias_landed = [sem(f"bias_landed{s}") for s in range(2)]
        bias_masked = sem("bias_masked")
        taps, pool_squared = sem("taps"), sem("pool_squared")
        for group in ROUND.values():
            for name in group:
                sem(name)

        def inc(ins, name):
            return ins.then_inc(sems[name], 1)

        HID0, GATE0, RES0 = 2, 1, 2

        def update(c):
            bank, k = c % 2, c // 2 % 2
            return (I01, I34)[c // 4][:, bank * T + k * 256:bank * T + (k + 1) * 256]

        def bc(ap, n):
            return ap.unsqueeze(len(ap.shape)).to_broadcast(list(ap.shape) + [n])

        def over_tiles(ap):
            return ap.unsqueeze(1).to_broadcast([P, TT, HS])

        block = ctx.enter_context(nc.Block())

        @block.sync
        def _(sp):
            slabs = a["slabs"]

            def load(n):
                sp.dma_start(RAW[:, n.slot:n.slot + 1, :],
                             slabs[bass.ds(n.value, 1)].rearrange("s p c -> p s c")
                             ).then_inc(slab_landed[n.slot], 16)

            load(At(0))
            sp.dma_start(cst[:], a["cst"]).then_inc(cst_landed, 16)
            for s in range(KT // 2):
                sp.dma_start(h[:, 2 * s:2 * s + 2, :], a["x"][:, 2 * s:2 * s + 2, :]).then_inc(x_landed[s], 16)
            load(At(1))
            load(At(2))
            sp.wait_ge(consts, N_CONSTS)
            for k in range(3):
                sp.dma_start(wgk_raw[32 * k:32 * k + 16, :], a["wgk"]).then_inc(wgk_landed, 16)
            with sp.Fori(1, N_SLABS // RING) as i:
                for j in range(RING):
                    n = At(j, i, RING)
                    sp.wait_ge(split_lo, n.value - (RING - 1))
                    load(n)
            for n in range(N_SLABS // RING * RING, N_SLABS):
                sp.wait_ge(split_lo, n - (RING - 1))
                load(At(n))

        @block.gpsimd
        def _(pool):
            for name, k in ROUND["gpsimd"].items():
                pool.sem_inc(sems[name], k)
            step = [0]

            def link(ins):
                step[0] += 1
                ins.then_inc(consts, 1)
                pool.wait_ge(consts, step[0])

            link(nc.gpsimd.memset(ones[:], 1.0))
            link(nc.gpsimd.memset(minus_half[:], -0.5))
            link(nc.gpsimd.memset(wgk_raw, 0.0))
            link(nc.gpsimd.memset(ident[:], 0.0))
            link(nc.gpsimd.affine_select(out=ident[:], in_=ident[:], compare_op=ALU.not_equal, fill=1.0, base=0,
                                         pattern=[[-1, P]], channel_multiplier=1))
            link(nc.gpsimd.affine_select(out=after_s[:], in_=ones[:], compare_op=ALU.is_gt, fill=0.0, base=0,
                                         pattern=[[-1, P]], channel_multiplier=1))
            link(nc.gpsimd.memset(after_s[CH:P, 0:CH], 0.0))
            link(nc.gpsimd.affine_select(out=upto_t[:], in_=ones[:], compare_op=ALU.is_ge, fill=0.0, base=0,
                                         pattern=[[1, P]], channel_multiplier=-1))
            link(nc.gpsimd.memset(upto_t[0:CH, CH:P], 0.0))
            link(nc.gpsimd.tensor_copy(causal[0:CH, :], upto_t[0:CH, 0:CH]))
            link(nc.gpsimd.tensor_copy(causal[CH:P, :], upto_t[CH:P, CH:P]))
            assert step[0] == N_CONSTS

            def norm(k):
                pool.wait_ge(norm_var, k + 1)
                nc.gpsimd.tensor_tensor(rstd4[:], var4[:], minus_half[:], ALU.pow).then_inc(norm_rstd, 1)

            def ssm(g):
                pool.wait_ge(sems["xte_ready"], after("xte_ready", g))
                pool.wait_ge(sems["group_norm"], after("group_norm", g))
                d = ggrp[:, 2:6].unsqueeze(1).unsqueeze(3).to_broadcast([P, TT, HPG, CH])
                x4 = XD[:].rearrange("p j (r c) -> p j r c", r=HPG)
                inc(nc.gpsimd.tensor_tensor(x4, x4, d, ALU.mult), "xd_ready")
                pool.wait_ge(sems["ssm_var"], after("ssm_var", g))
                inc(nc.gpsimd.tensor_tensor(rstd4[:], var4[:], minus_half[:], ALU.pow), "ssm_rstd")

            def gla(hd):
                pool.wait_ge(sems["gla_var"], after("gla_var", hd))
                inc(nc.gpsimd.tensor_tensor(rstd4[:], var4[:], minus_half[:], ALU.pow), "gla_rstd")

            def ffn(f):
                def tile(ft, t):
                    pool.wait_ge(gate_ready, FT * f + ft + 1)
                    nc.gpsimd.tensor_tensor(hid[:, t, :], hid[:, t, :], rms[:], ALU.mult).then_inc(gate_rms, 1)

                tile(0, 0)
                with pool.Fori(0, FT // 3) as i:
                    for t in range(3):
                        tile(3 * i + t + 1, (t + 1) % 3)

            def dt_softplus():
                step = [0]

                def link(ins):
                    step[0] += 1
                    ins.then_inc(dt_pool, 1)
                    pool.wait_ge(dt_pool, step[0])

                g = nc.gpsimd
                v, low, e, s, z2, z = (dtw[:, k, :] for k in range(6))
                dt = SC[:, 4:8, :].rearrange("p j h -> p (j h)")
                pool.wait_ge(dt_act, 1)
                pool.wait_ge(dt_dve, 4)
                link(g.tensor_tensor(z, e, z, ALU.mult))
                link(g.tensor_tensor(z2, z, z, ALU.mult))
                link(g.tensor_scalar(s, z2, 1.0 / 17, 1.0 / 15, ALU.mult, ALU.add))
                for odd in (13, 11, 9, 7, 5, 3):
                    link(g.tensor_tensor(s, s, z2, ALU.mult))
                    link(g.tensor_scalar(s, s, 1.0 / odd, None, ALU.add))
                link(g.tensor_tensor(s, s, z2, ALU.mult))
                link(g.tensor_scalar(s, s, 2.0, 2.0, ALU.mult, ALU.add))
                link(g.tensor_tensor(s, s, z, ALU.mult))
                link(g.tensor_scalar(low, v, 0.0, None, ALU.max))
                link(g.tensor_tensor(dt, s, low, ALU.add))
                pool.wait_ge(dt_act, 2)
                link(g.tensor_scalar(s, dt, -1.0, None, ALU.mult))
                link(g.tensor_tensor(SC[:, 0:4, :], s.rearrange("p (j h) -> p j h", h=HS), over_tiles(minus_a[:]),
                                     ALU.mult))
                assert step[0] == DA_READY, step

            for m in range(POOL_SQUARES):
                pool.wait_ge(x_landed[m // 2], 16)
                if m:
                    pool.wait_ge(pool_squared, 2 * m - 1)
                dst = sq_pool if m else acc_pool
                nc.gpsimd.tensor_tensor(dst[:], h[:, m, :], h[:, m, :], ALU.mult).then_inc(pool_squared, 1)
                if m:
                    pool.wait_ge(pool_squared, 2 * m)
                    nc.gpsimd.tensor_tensor(acc_pool[:], acc_pool[:], sq_pool[:], ALU.add).then_inc(pool_squared, 1)
            norm(0)
            pool.wait_ge(wgk_landed, 3 * 16)
            nc.gpsimd.tensor_copy(WGK[:], wgk_raw).then_inc(wgk_split, 1)
            pool.wait_ge(wgk_split, 1)
            nc.gpsimd.tensor_tensor(WGK[32:64, :], wgk_raw[32:64, :], WGK[32:64, :].bitcast(F32),
                                    ALU.subtract).then_inc(wgk_split, 1)
            pool.wait_ge(wgk_split, 2)
            ffn(0)
            norm(1)
            for m in range(KT):
                pool.wait_ge(uh_ready, 16 + m + 1)
                nc.gpsimd.tensor_tensor(UL[:, m, :], ut[:, m % 3, :], UH[:, m, :].bitcast(F32),
                                        ALU.subtract).then_inc(ul_ready, 1)
            dt_softplus()
            with pool.Fori(0, NG) as i:
                ssm(i)
            pool.wait_ge(sems["ssm_lo"], last("ssm_lo", NG - 1))
            nc.gpsimd.memset(RM[:], 1.0).then_inc(gk_pool, 1)
            pool.wait_ge(gk_pool, 1)
            nc.gpsimd.memset(RM[:].rearrange("p (c t) -> p c t", t=CH)[:, :, 0:1], 0.0).then_inc(gk_pool, 1)
            for hd in range(HG - 1):
                gla(hd)
            k_last = At(W_GLA + 6 * (HG - 1) + 3)
            pool.wait_ge(g_free[k_last.slot], k_last.read)
            for s in range(2):
                nc.gpsimd.memset(bias[0:CH, s, T - CH:T], MASKED).then_inc(bias_masked, 1)
            gla(HG - 1)
            norm(2)
            ffn(1)
            norm(3)

        @block.tensor
        def _(pe):
            for name, k in ROUND["tensor"].items():
                pe.sem_inc(sems[name], k)
            mm = nc.tensor.matmul

            def need_slab(n):
                pe.wait_ge(split_lo, n.value + 1)

            def blocks(dst, n, k0, k1, RH, RL, begin, end):
                ins = None
                for which, (W, R) in enumerate(((WH, RH), (WH, RL), (WL, RH))):
                    for k in range(k0, k1):
                        ins = mm(dst, W[:, n.slot, (k - k0) * P:(k - k0 + 1) * P], R[:, k, :],
                                      start=begin and which == 0 and k == k0,
                                      stop=end and which == 2 and k == k1 - 1)
                return ins

            def fm(dst, n, RH, RL):
                need_slab(n)
                blocks(dst, n, 0, KT, RH, RL, True, True).then_inc(slab_done, 1)

            def fm_piece(dst, n, RH, RL, piece):
                if piece == 0:
                    need_slab(n)
                which, k0 = piece // 2, piece % 2 * 4
                W, R = ((WH, RH), (WH, RL), (WL, RH))[which]
                for k in range(k0, k0 + 4):
                    ins = mm(dst, W[:, n.slot, k * P:(k + 1) * P], R[:, k, :], start=piece == 0 and k == 0,
                             stop=piece == 5 and k == KT - 1)
                if piece == 5:
                    ins.then_inc(slab_done, 1)

            def fm_fresh(dst, n, stage, source=(UH, UL, uh_ready, ul_ready)):
                RH, RL, hi_ready, lo_ready = source
                need_slab(n)
                for k in range(KT):
                    pe.wait_ge(hi_ready, 8 * stage + k + 1)
                    mm(dst, WH[:, n.slot, k * P:(k + 1) * P], RH[:, k, :], start=k == 0, stop=False)
                    mm(dst, WL[:, n.slot, k * P:(k + 1) * P], RH[:, k, :], start=False, stop=False)
                    pe.wait_ge(lo_ready, 8 * stage + k + 1)
                    ins = mm(dst, WH[:, n.slot, k * P:(k + 1) * P], RL[:, k, :], start=False, stop=k == KT - 1)
                ins.then_inc(slab_done, 1)

            def fm_by_tile(dst, n):
                need_slab(n)
                for k in range(KT):
                    for which, (W, R) in enumerate(((WH, UH), (WH, UL), (WL, UH))):
                        ins = mm(dst, W[:, n.slot, k * P:(k + 1) * P], R[:, k, :],
                                 start=which == 0 and k == 0, stop=which == 2 and k == KT - 1)
                    ins.then_inc(raw_read if k < KT - 1 else slab_done, 1)

            def tm_tile(n, wn, j, thirds=range(3)):
                if j == 0 and thirds[0] == 0:
                    need_slab(n)
                    need_slab(n + 1)
                dst = G[:, (wn + j // 2).slot, (j % 2) * 256:(j % 2 + 1) * 256]
                for which in thirds:
                    U, W = ((UH, WH), (UL, WH), (UH, WL))[which]
                    for k in range(KT):
                        ins = mm(dst, U[:, k, j * P:(j + 1) * P],
                                 W[:, (n + k // 4).slot, (k % 4) * 256:(k % 4 + 1) * 256],
                                 start=which == 0 and k == 0, stop=which == 2 and k == KT - 1)
                if j == TT - 1 and which == 2:
                    ins.then_inc(slab_done, 2)

            def bank_free(wn):
                pe.wait_ge(g_free[wn.slot], wn.free)

            def bank_read(wn):
                pe.wait_ge(g_free[wn.slot], wn.read)

            def norm_total(k):
                pe.wait_ge(acc_updated, RES0 + 8 * k + 8)
                if k == 0:
                    pe.wait_ge(consts, N_CONSTS)
                    pe.wait_ge(pool_squared, 2 * POOL_SQUARES - 1)
                for j in range(TT):
                    if k == 0:
                        mm(I2[:, j:j + 1], acc_pool[:, j * P:(j + 1) * P], ones[:, 0:1], start=True, stop=False)
                    ins = mm(I2[:, j:j + 1], acc[:, j * P:(j + 1) * P], ones[:, 0:1], start=k > 0, stop=True)
                ins.then_inc(norm_sums, 1)

            def norm_spread(k):
                pe.wait_ge(norm_diag, k + 1)
                mm(I34[:, 0:T], ones[:], diag[:].rearrange("p j t -> p (j t)"), start=True,
                   stop=True).then_inc(norm_bc, 1)

            def ffn(f):
                n0, nd = (N_FFN1, N_DOWN1) if f == 0 else (N_FFN2, N_DOWN2)

                def tile(ft, n):
                    pe.wait_ge(hid_ready, FT * f + ft + 1)
                    fm(G[:, n.slot, :], n, UH, UL)
                    pe.wait_ge(gate_scaled, FT * f + ft + 1)
                    fm(G[:, (n + 1).slot, :], n + 1, UH, UL)

                n = At(n0)
                pe.wait_ge(hid_ready, FT * f + 1)
                fm_fresh(G[:, n.slot, :], n, 3 * f)
                pe.wait_ge(gate_scaled, FT * f + 1)
                for piece in range(6):
                    fm_piece(G[:, (n + 1).slot, :], n + 1, UH, UL, piece)
                    if piece == (3, 1)[f]:
                        norm_total(2 * f)
                norm_spread(2 * f)
                with pe.Fori(0, FT // 3) as i:
                    for t in range(3):
                        tile(3 * i + t + 1, At(n0 + 2 * t + 2, i, 6))

                with pe.Fori(0, KT // 2) as i:
                    for t in range(2):
                        pe.wait_ge(h_updated, 8 * (0, 2)[f] + 2 * i + t + 1)
                        for c, (k0, k1) in enumerate(DOWN_K):
                            n = At(nd + 3 * t + c, i, 6)
                            need_slab(n)
                            pe.wait_ge(hl_ready, FT * f + k1)
                            blocks(I01[:, t * T:(t + 1) * T], n, k0, k1, HH, HL, c == 0,
                                   c == 2).then_inc(slab_done, 1)

            def half(c):
                return slice(CH * (c % 2), CH * (c % 2) + CH)

            def dt_turn():
                bank_read(At(0))
                for j in range(TT):
                    ins = nc.tensor.transpose(I01[:, j * 32:(j + 1) * 32], dtv[LR_ROWS:P, j * P:(j + 1) * P],
                                              ident[LR_ROWS:P, LR_ROWS:P])
                ins.then_inc(dt_pe, 1)

            def dt_sums():
                pe.wait_ge(dt_pool, DA_READY)
                da = SC[:, 0:4, :].rearrange("p j h -> p (j h)")
                mm(I01[:, T:T + 128], upto_t[:], da, start=True, stop=True)
                mm(I01[:, T + 128:T + 256], after_s[:], da, start=True, stop=True)
                for c in range(NCH):
                    dst = I2[:, 32 * (c // 2):32 * (c // 2) + 32] if c % 2 else \
                        I01[:, T + 256 + 16 * c:T + 288 + 16 * c]
                    ins = mm(dst, ones[half(c), :], SC[half(c), c // 2, :], start=True, stop=True)
                ins.then_inc(dt_pe, 1)

            def ssm_turn(g):
                pe.wait_ge(sems["conv_done"], last("conv_done", g))
                pe.wait_ge(sems["ssm_lo"], last("ssm_lo", g - 1))
                pe.wait_ge(sems["cb_masked"], last("cb_masked", g - 1))
                for j in range(TT):
                    for f in range(2):
                        nc.tensor.transpose(I01[:, j * 256 + f * P:j * 256 + (f + 1) * P],
                                            XT[:, f, j * P:(j + 1) * P], ident[:])
                for j in range(TT):
                    ins = nc.tensor.transpose(I2[:, j * P:(j + 1) * P], BT[:, j * P:(j + 1) * P], ident[:])
                inc(ins, "xb_turned")
                pe.wait_ge(sems["da_masked"], last("da_masked", g))
                pe.wait_ge(sems["ssm_y"], after("ssm_y", g - 1, 0))
                rhs = M[:].rearrange("p j r t -> p (j r t)")
                for s in range(2):
                    ins = mm(I34[:, s * T:(s + 1) * T], after_s[:], rhs[:, s * T:(s + 1) * T], start=True, stop=True)
                inc(ins, "seg_done")

            def ssm_cb_u(g):
                pe.wait_ge(sems["b_copied"], after("b_copied", g))
                for c in range(NCH):
                    ins = mm(I2[half(c), (c // 2) * CH:(c // 2 + 1) * CH], BT[:, c * CH:(c + 1) * CH],
                             CT[:, c * CH:(c + 1) * CH], start=True, stop=True)
                inc(ins, "cb_done")
                pe.wait_ge(sems["xte_ready"], after("xte_ready", g))
                pe.wait_ge(sems["x_copied"], after("x_copied", g))
                for c in range(4):
                    ins = mm(update(c), BK[half(c), c // 2, :], XTE[half(c), c // 2, :],
                             start=True, stop=True)
                inc(ins, "u_done")
                pe.wait_ge(sems["decay_exp"], after("decay_exp", g))
                for c in range(4, 7):
                    ins = mm(update(c), BK[half(c), c // 2, :], XTE[half(c), c // 2, :],
                             start=True, stop=True)
                inc(ins, "u_done")

            def ssm_intra():
                for c in range(NCH):
                    j, s = c // 2, half(c)
                    for rr in range(HPG):
                        ins = mm(I01[s, j * 256 + rr * CH:j * 256 + (rr + 1) * CH], M[s, j, rr, :],
                                 XDT[s, j, rr * CH:(rr + 1) * CH], start=True, stop=True)
                inc(ins, "intra_done")

            def ssm_inter(g):
                pe.wait_ge(sems["m_ready"], after("m_ready", g))
                pe.wait_ge(sems["ssm_chain"], last("ssm_chain", g))
                for c in range(NCH):
                    ins = mm(I34[half(c), (c // 2) * 256:(c // 2 + 1) * 256], CT[:, c * CH:(c + 1) * CH],
                             SS[:, c, :], start=True, stop=True)
                inc(ins, "inter_done")

            def turn_back(src, dst, ready, g, done):
                pe.wait_ge(sems[ready], last(ready, g))
                for f in range(2):
                    for j in range(TT):
                        ins = nc.tensor.transpose(dst[:, f * T + j * P:f * T + (j + 1) * P],
                                                  src[:, j, f * P:(f + 1) * P], ident[:])
                inc(ins, done)

            def project(n, wn, kinds, between):
                t = u = 0
                for kind in kinds:
                    if kind == "fm":
                        bank_free(wn + t)
                        fm(G[:, (wn + t).slot, :], n + t, UH, UL)
                        between.get(u, lambda: None)()
                        t, u = t + 1, u + 1
                    else:
                        bank_free(wn + t)
                        bank_free(wn + t + 1)
                        for j in range(TT):
                            tm_tile(n + t, wn + t, j)
                            between.get(u + j, lambda: None)()
                        t, u = t + 2, u + 4

            def output(n, wn, RH, RL):
                bank_free(wn)
                fm(G[:, wn.slot, :], n, RH, RL)

            def output_half(n, wn, half_no):
                if half_no == 0:
                    bank_free(wn)
                need_slab(n)
                blocks(G[:, wn.slot, :], n, half_no * KT, half_no * KT + KT, SH, SL, half_no == 0,
                       half_no == 1).then_inc(slab_done, 1)

            def output_part(n, wn, k0, k1, RH, RL, begin, end, block0=0):
                for which, (W, R) in enumerate(((WH, RH), (WH, RL), (WL, RH))):
                    for k in range(k0, k1):
                        b = block0 + k - k0
                        ins = mm(G[:, wn.slot, :], W[:, n.slot, b * P:(b + 1) * P], R[:, k, :],
                                 start=begin and which == 0 and k == k0, stop=end and which == 2 and k == k1 - 1)
                if end:
                    ins.then_inc(slab_done, 1)

            ffn(0)

            fm_fresh(G[:, 0, :], At(N_SMALL), 1)
            norm_total(1)
            n, wn = At(N_SSM), At(W_SSM)
            bank_free(wn)
            fm(G[:, wn.slot, :], n, UH, UL)
            norm_spread(1)
            bank_free(wn + 1)
            fm_by_tile(G[:, (wn + 1).slot, :], n + 1)
            dt_turn()
            bank_free(wn + 2)
            fm_fresh(G[:, (wn + 2).slot, :], n + 2, 2)
            bank_free(wn + 3)
            fm(G[:, (wn + 3).slot, :], n + 3, UH, UL)
            bank_free(wn + 4)
            bank_free(wn + 5)
            for j in range(TT):
                tm_tile(n + 4, wn + 4, j)
                if j == 2:
                    dt_sums()
            pe.wait_ge(dt_act, 6)

            SSM_KINDS = ("fm", "fm", "fm", "fm", "tm")
            with pe.Fori(0, NG - 1) as i:
                project(At(N_SSM + 6, i, 6), At(W_SSM + 6, i, 6), SSM_KINDS, {
                    0: lambda: ssm_turn(i), 1: lambda: ssm_cb_u(i), 3: lambda: (ssm_inter(i), ssm_intra()),
                    7: lambda: turn_back(Y, I01, "ssm_scaled", i, "ssm_turned")})
            g = NG - 1
            n, wn = At(N_MERGE1), At(W_MERGE1)
            output(n, wn, UH, UL)
            ssm_turn(g)
            ssm_cb_u(g)
            output_half(n + 1, wn + 1, 0)
            ssm_inter(g)
            ssm_intra()
            output(n + 2, wn + 2, UH, UL)
            output_half(n + 3, wn + 3, 0)
            turn_back(Y, I01, "ssm_scaled", g, "ssm_turned")
            need_slab(n + 4)
            output_part(n + 4, wn + 1, KT, 2 * KT - 2, SH, SL, False, False)

            pe.wait_ge(sems["ssm_lo"], last("ssm_lo", NG - 1))
            pe.wait_ge(lr_ready, 1)
            pe.wait_ge(wgk_split, 2)
            for hd in range(HG):
                dst = (I01[:, 0:T], I01[:, T:], I34[:, 0:T], I34[:, T:])[hd]
                ins = mm(dst, WGK[:, hd * P:(hd + 1) * P], LR[:], start=True, stop=True)
            ins.then_inc(gk_pe, 1)

            output_part(n + 4, wn + 1, 2 * KT - 2, 2 * KT, SH, SL, False, True, KT - 2)
            output_half(n + 5, wn + 3, 1)
            with pe.Fori(0, 2) as i:
                for t in range(3):
                    n, wn = At(N_MERGE1 + 6 + 3 * t, i, 9), At(W_MERGE1 + 4 + 2 * t, i, 6)
                    output(n, wn, UH, UL)
                    output_half(n + 1, wn + 1, 0)
                    output_half(n + 2, wn + 1, 1)

            def gla_a(hd):
                pe.wait_ge(sems["gla_qh"], after("gla_qh", hd))
                bank_read(At(W_GLA + 6 * hd + 3))
                for c in range(NCH):
                    ins = mm(I2[half(c), (c // 2) * CH:(c // 2 + 1) * CH], KH[:, c * CH:(c + 1) * CH],
                             QH[:, c * CH:(c + 1) * CH], start=True, stop=True)
                inc(ins, "gla_a_done")
                pe.wait_ge(sems["gla_lo"], last("gla_lo", hd - 1))
                for j in range(TT):
                    ins = nc.tensor.transpose(I34[:, j * P:(j + 1) * P], KT_[:, j * P:(j + 1) * P], ident[:])
                inc(ins, "gla_kt_turned")

            def gla_u(hd):
                pe.wait_ge(sems["gla_kt_copied"], after("gla_kt_copied", hd))
                for s in range(2):
                    bank_read(At(W_GLA + 6 * hd + 1 + s))
                pe.wait_ge(sems["gla_o_ready"], last("gla_o_ready", hd - 1))
                for c in range(4):
                    ins = mm(update(c), KK[half(c), c // 2, :], GV[half(c), c // 2, :],
                             start=True, stop=True)
                inc(ins, "gla_u_done")
                for c in range(4, 7):
                    ins = mm(update(c), KK[half(c), c // 2, :], GV[half(c), c // 2, :],
                             start=True, stop=True)
                inc(ins, "gla_u_done")

            def gla_o(hd):
                pe.wait_ge(sems["gla_a_masked"], after("gla_a_masked", hd))
                pe.wait_ge(sems["gla_chain"], last("gla_chain", hd))
                pe.wait_ge(sems["gla_qt"], after("gla_qt", hd))
                for c in range(NCH):
                    j, s = c // 2, half(c)
                    dst = I01[s, j * 256:(j + 1) * 256]
                    mm(dst, GA[s, j, :], GV[s, j, :], start=True, stop=False)
                    ins = mm(dst, QT[:, c * CH:(c + 1) * CH], GS[:, c, :], start=False, stop=True)
                inc(ins, "gla_o_done")

            GLA_KINDS = ("fm", "tm", "fm", "tm")
            project(At(N_GLA), At(W_GLA), GLA_KINDS, {})
            pe.wait_ge(gk_dve, GK_EVICTED)
            for hd in range(HG - 1):
                project(At(N_GLA + 6 * (hd + 1)), At(W_GLA + 6 * (hd + 1)), GLA_KINDS, {
                    0: lambda: gla_a(hd), 1: lambda: gla_u(hd), 4: lambda: gla_o(hd),
                    8: lambda: turn_back(GO, I34, "gla_o_ready", hd, "gla_turned")})

            def att_s(q, e):
                f, s, par = e // 2, slice(CH * (e % 2), CH * (e % 2) + CH), q % 2
                if e == 0:
                    for t in range(4):
                        bank_read(At(W_ATT + 6 * q + t))
                    if q == 0:
                        pe.wait_ge(sems["gla_lo"], last("gla_lo", HG - 1))
                pe.wait_ge(sems["att_o"], after("att_o", q, e - 1))
                for i in (3, 2, 0, 1):
                    dst = {3: I01[:, 0:512], 2: I01[:, 512:896], 0: I01[:, 896:1024], 1: I2[:, 0:256]}[i]
                    ins = mm(dst, AQ[par][s, f, i * P:(i + 1) * P], AK[par][s, f, 0:(i + 1) * P],
                             start=True, stop=True)
                inc(ins, "att_s")

            def att_turn(q, e):
                pe.wait_ge(sems["att_p"], after("att_p", q, e))
                if q == 0 and e == 0:
                    pass
                elif e == 0:
                    pe.wait_ge(sems["att_lo"], last("att_lo", q - 1))
                else:
                    pe.wait_ge(sems["att_pt_b"], after("att_pt_b", q, 2 * (e - 1) + 1))
                    pe.wait_ge(sems["att_pt_a"], after("att_pt_a", q, e - 1))
                for i in range(TT):
                    for b in range(i + 1):
                        col = PT_OFF[b] + (i - b) * P
                        dst = I34[:, col:col + P] if b != 2 else I2[:, 256 + (i - b) * P:256 + (i - b + 1) * P]
                        ins = nc.tensor.transpose(dst, PR[:, P_OFF[i] + b * P:P_OFF[i] + (b + 1) * P], ident[:])
                inc(ins, "att_turned")

            def att_pv(q, e):
                if e == 0:
                    for t in (4, 5):
                        bank_read(At(W_ATT + 6 * q + t))
                pe.wait_ge(sems["att_pt_a"], after("att_pt_a", q, e))
                pe.wait_ge(sems["att_pt_b"], after("att_pt_b", q, 2 * e + 1))
                for i in range(TT):
                    for b in range(i + 1):
                        col = PT_OFF[b] + (i - b) * P
                        ins = mm(I01[:, i * CH:(i + 1) * CH], PT[:, col:col + P], AV[:, b, e * CH:(e + 1) * CH],
                                 start=b == 0, stop=b == i)
                inc(ins, "att_pv")

            PIECES = 36

            def att_pieces(q, begin, end):
                for k in range(begin, end):
                    if q == NQ:
                        merge2_piece(k)
                    elif k < 24:
                        n, wn = At(N_ATT + 6 * q + k // 6), At(W_ATT + 6 * q + k // 6)
                        if k % 6 == 0:
                            bank_free(wn)
                        fm_piece(G[:, wn.slot, :], n, UH, UL, k % 6)
                    else:
                        n, wn = At(N_ATT + 6 * q + 4), At(W_ATT + 6 * q + 4)
                        if k == 24:
                            bank_free(wn)
                            bank_free(wn + 1)
                        j, third = divmod(k - 24, 3)
                        tm_tile(n, wn, j, (third,))

            hd = HG - 1
            for begin, end, then in (
                    (0, 6, lambda: gla_a(hd)), (6, 10, lambda: gla_u(hd)), (10, 18, lambda: gla_o(hd)),
                    (18, 28, lambda: turn_back(GO, I34, "gla_o_ready", hd, "gla_turned"))):
                att_pieces(0, begin, end)
                then()
            att_pieces(0, 28, PIECES)

            BRANCH = ((UH, UL), (GH, GL), (UH, UL), (AH, AL))

            def merge2_part(kind, n, wn):
                output(n, wn, *BRANCH[kind])

            def merge2_piece(k):
                kind, n, wn = MERGE2_HEAD[k // 6][1], At(N_MERGE2 + k // 6), At(W_MERGE2 + k // 6)
                if k % 6 == 0:
                    bank_free(wn)
                fm_piece(G[:, wn.slot, :], n, *BRANCH[kind], k % 6)

            for q in range(NQ):
                for e in range(4):
                    att_s(q, e)
                    att_pieces(q + 1, 9 * e, 9 * e + 6)
                    att_turn(q, e)
                    att_pieces(q + 1, 9 * e + 6, 9 * e + 8)
                    att_pv(q, e)
                    att_pieces(q + 1, 9 * e + 8, 9 * e + 9)
                turn_back(AO, I34, "att_o", q, "att_o_turned")

            n, wn = At(N_MERGE2 + 6), At(W_MERGE2 + 6)
            bank_free(wn)
            need_slab(n)
            output_part(n, wn, 0, KT - 2, AH, AL, True, False)
            pe.wait_ge(sems["att_lo"], last("att_lo", NQ - 1))
            output_part(n, wn, KT - 2, KT, AH, AL, False, True, KT - 2)
            merge2_part(MERGE2_HEAD[7][1], n + 1, wn + 1)
            with pe.Fori(0, 2) as i:
                for k in range(12):
                    merge2_part(k % 4, At(N_MERGE2 + 8 + k, i, 12), At(W_MERGE2 + 8 + k, i, 12))

            fm_fresh(I01[:, 0:T], At(N_OUT), 0, (MH, ML, mh_ready, ml_ready))
            for m in range(1, KT):
                pe.wait_ge(h_updated, 8 + m + 1)
                fm(I01[:, (m % 2) * T:(m % 2 + 1) * T], At(N_OUT + m), MH, ML)
            ffn(1)
            norm_total(3)
            norm_spread(3)

        @block.scalar
        def _(act):
            for name, k in ROUND["scalar"].items():
                act.sem_inc(sems[name], k)
            act.sem_inc(squared, POOL_SQUARES)
            for bank in range(3):
                act.sem_inc(g_free[bank], 1)
            act.preload_act_table_set("silu_and_others")
            A = nc.scalar.activation

            def hi(n):
                if isinstance(n.value, int) and n.value >= N_SLABS:
                    return
                act.wait_ge(slab_landed[n.slot], 16 * n.turn + 16)
                if n.k >= RING:
                    act.wait_ge(slab_done, n.value - RING + 1)
                nc.scalar.copy(WH[:, n.slot, :], RAW[:, n.slot, :]).then_inc(split_hi, 1)

            def raw_hi(m, stage):
                k = (0, 1, None, 2)[stage]
                if k == 0:
                    act.wait_ge(x_landed[m // 2], 16)
                else:
                    act.wait_ge(h_updated, RES0 + 8 * (k - 1) + m + 1)
                A(UH[:, bass.ds(m, 1), :].rearrange("p a t -> p (a t)"), h[:, bass.ds(m, 1), :].rearrange("p a t -> p (a t)"),
                  ACT.Copy, scale=cst[:, bass.ds((C_N1, C_NM, C_N2)[k] + m, 1)]).then_inc(uh_ready, 1)

            def square(m, k, slot, wait=True):
                if wait:
                    act.wait_ge(acc_updated, 8 * k + m + 1)
                    if k:
                        act.wait_ge(h_updated, RES0 + 8 * (k - 1) + m + 1)
                A(sq[:, slot, :], h[:, bass.ds(m, 1), :].rearrange("p a t -> p (a t)"), ACT.Square).then_inc(squared, 1)

            def store():
                for m in range(KT):
                    act.wait_ge(out_ready, m + 1)
                    act.dma_start(out[:, m, :], h[:, m, :]).then_inc(stored, 16)
                act.wait_ge(stored, 16 * KT)

            def ffn(f):
                n0, nd = (N_FFN1, N_DOWN1) if f == 0 else (N_FFN2, N_DOWN2)
                act.preload_act_table_set("silu_and_others")

                def tile(ft, n, t):
                    if isinstance(ft, int):
                        hi(n + 3)
                    act.wait_ge(gate_scaled, GATE0 + FT * f + ft + 1)
                    A(hid[:, t, :], hid[:, t, :], ACT.Silu).then_inc(gate_ready, 1)
                    if not isinstance(ft, int):
                        hi(n + 3)
                    act.wait_ge(hid_ready, HID0 + FT * f + ft + 1)
                    nc.scalar.copy(HH[:, bass.ds(ft, 1), :].rearrange("p a t -> p (a t)"),
                                   hid[:, t, :]).then_inc(hh_ready, 1)
                    hi(n + 4)

                tile(0, At(n0), 0)
                with act.Fori(0, FT // 3) as i:
                    for t in range(3):
                        tile(3 * i + t + 1, At(n0 + 2 * t + 2, i, 6), (t + 1) % 3)

                def down(m, n, t):
                    hi(n + 3)
                    hi(n + 4)
                    if f == 0:
                        act.wait_ge(acc_updated, 8 + m + 1)
                        raw_hi(m, 1)
                    hi(n + 5)
                    square(m, 1 if f == 0 else 3, t, f == 1)

                with act.Fori(0, KT // 2 - 1) as i:
                    for t in range(2):
                        down(2 * i + t, At(nd + 3 * t, i, 6), t)
                for m in (KT - 2, KT - 1):
                    down(m, At(nd + 3 * m), m % 2)

            def dt_exp():
                act.wait_ge(dt_dve, DT_ABS)
                A(dtw[:, 2, :], dtw[:, 1, :], ACT.Exp, scale=-1.0).then_inc(dt_act, 1)
                A(minus_a[:], cst[:, C_ALOG:C_ALOG + HS], ACT.Exp).then_inc(dt_act, 1)

            def decay_exps():
                act.wait_ge(dt_pe, 2)
                flat = SC[:].rearrange("p r h -> p (r h)")
                A(flat[:, 12 * HS:16 * HS], I01[:, T:T + 128], ACT.Exp).then_inc(dt_act, 1)
                A(flat[:, 8 * HS:12 * HS], I01[:, T + 128:T + 256], ACT.Exp).then_inc(dt_act, 1)
                for odd, src in enumerate((I01[:, T + 256:T + 384], I2[:, 0:128])):
                    A(SC[:, 16 + odd:24:2, :], src.rearrange("p (c h) -> p c h", h=HS), ACT.Exp).then_inc(dt_act, 1)

            def conv_begin(p, t, n, wn):
                raw = isinstance(p, int) and t < 2
                if raw:
                    act.wait_ge(g_free[wn.slot], wn.read)
                else:
                    act.wait_ge(slab_done, n.value + 1)
                act.wait_ge(sems["conv_const"], after("conv_const", p))
                act.wait_ge(sems["conv_done"], after("conv_done", p, t - 2))
                inc(A(CV[:, t % 2, :], XT[:, t, :] if raw else G[:, wn.slot, :], ACT.Identity,
                      bias=gconv[:, 5 * t + 4:5 * t + 5], scale=gconv[:, 5 * t + 3:5 * t + 4]), "conv_begun")
                if not raw:
                    hi(n + 3)

            def conv_tanh(p, t, wn):
                if isinstance(p, int) and t < 2:
                    act.wait_ge(raw_taps, t + 1)
                else:
                    act.wait_ge(g_free[wn.slot], wn.read)
                inc(A(TH[:, t % 2, :], CV[:, t % 2, :], ACT.Tanh), "conv_tanh")

            def z_tanh(p, n, wn):
                act.wait_ge(slab_done, n.value + 2)
                act.wait_ge(sems["conv_done"], last("conv_done", p))
                for s in range(2):
                    inc(A(TH[:, s, :], G[:, (wn + s).slot, :], ACT.Tanh, scale=0.5), "z_tanh")
                hi(n + 3)

            def ssm_copy_exp(g):
                act.wait_ge(sems["xb_turned"], after("xb_turned", g))
                act.wait_ge(sems["ssm_y"], last("ssm_y", g - 1))
                inc(nc.scalar.copy(XD[:].rearrange("p j c -> p (j c)"), I01[:]), "x_copied")
                act.wait_ge(sems["u_done"], last("u_done", g - 1))
                inc(nc.scalar.copy(BK[:].rearrange("p j c -> p (j c)"), I2[:]), "b_copied")
                act.wait_ge(sems["seg_done"], after("seg_done", g))
                inc(A(M[:].rearrange("p j r t -> p (j r t)"), I34[:], ACT.Exp), "decay_exp")

            def squares(src, dump, dst, name, g):
                for j in range(TT):
                    act.wait_ge(sems[name], after(name, g, j - 1))
                    inc(A(dump[:], src(j), ACT.Square, accum_out=dst[:, j:j + 1]), name)

            def ssm_squares(g):
                act.wait_ge(sems["ssm_y"], last("ssm_y", g))
                act.wait_ge(sems["ssm_chain"], last("ssm_chain", g))
                squares(lambda j: Y[:, j, :], ssm_dump, ss4, "ssm_squares", g)

            def evict_hi(src, dstH, k0, scale, turned, g, name):
                act.wait_ge(sems[turned], last(turned, g))
                for f in range(2):
                    inc(A(dstH[:, bass.ds(k0 + f, 1), :].rearrange("p a t -> p (a t)"), src[:, f * T:(f + 1) * T],
                          ACT.Copy, scale=scale[f]), name)

            ssm_norm_cols = [ggrp[:, f:f + 1] for f in range(2)]
            gla_norm_cols = [cst[:, C_GN + f:C_GN + f + 1] for f in range(2)]

            def gate_tanh(wn, slot, n, col):
                act.wait_ge(slab_done, n.value + 1)
                A(gate_th[:, slot, :], G[:, wn.slot, :], ACT.Tanh, bias=half_gate_bias[:, bass.ds(col, 1)],
                  scale=0.5).then_inc(g_free[wn.slot], 1)

            hi(At(0))
            act.wait_ge(cst_landed, 16)
            for m in range(KT):
                raw_hi(m, 0)
            hi(At(1))
            for m in range(POOL_SQUARES, KT):
                square(m, 0, m % 2)
            hi(At(2))
            ffn(0)
            act.preload_act_table_set("exp_and_others")
            hi(At(N_SMALL + 3))
            hi(At(N_SMALL + 4))
            for m in range(KT):
                if m == 2:
                    conv_begin(0, 0, At(N_SSM), At(W_SSM))
                act.wait_ge(ut_ready, m + 1)
                act.wait_ge(*((raw_read, m + 1) if m < KT - 1 else (slab_done, N_SSM + 2)))
                nc.scalar.copy(UH[:, m, :], ut[:, m % 3, :]).then_inc(uh_ready, 1)
            hi(At(N_SMALL + 5))
            act.wait_ge(half_bias, 1)

            def ssm_first():
                n, wn = At(N_SSM), At(W_SSM)
                dt_exp()
                conv_tanh(0, 0, wn)
                conv_begin(0, 1, n + 1, wn + 1)
                conv_begin(0, 2, n + 2, wn + 2)
                conv_tanh(0, 1, wn + 1)
                conv_tanh(0, 2, wn + 2)
                nc.scalar.copy(LR[:], dtv[0:LR_ROWS, :]).then_inc(lr_split, 1)
                conv_begin(0, 3, n + 3, wn + 3)
                conv_tanh(0, 3, wn + 3)
                decay_exps()
                z_tanh(0, n + 4, wn + 4)
                hi(n + 8)

            def ssm_round(p, n, wn, inner):
                for t in range(4):
                    conv_begin(p, t, n + t, wn + t)
                    if t == 0:
                        ssm_copy_exp(inner)
                    conv_tanh(p, t, wn + t)
                ssm_squares(inner)
                z_tanh(p, n + 4, wn + 4)
                evict_hi(I01, SH, 2 * inner, ssm_norm_cols, "ssm_turned", inner, "ssm_hi")
                hi(n + 8)

            ssm_first()
            with act.Fori(0, NG - 1) as i:
                ssm_round(i + 1, At(N_SSM + 6, i, 6), At(W_SSM + 6, i, 6), i)
            g = NG - 1
            n, wn = At(N_MERGE1), At(W_MERGE1)
            gate_tanh(wn, 0, n, KT)
            hi(n + 3)
            ssm_copy_exp(g)
            hi(n + 4)
            gate_tanh(wn + 2, 1, n + 2, KT + 1)
            hi(n + 5)
            ssm_squares(g)
            evict_hi(I01, SH, 2 * g, ssm_norm_cols, "ssm_turned", g, "ssm_hi")
            for s in (6, 7, 8):
                hi(n + s)

            act.preload_act_table_set("natural_log_exp_and_others")
            for hd in range(HG):
                act.wait_ge(gk_dve, 2 * (hd + 1))
                A(EX[:, hd, :], EX[:, hd, :], ACT.Exp, scale=-1.0).then_inc(gk_act, 1)
                act.wait_ge(gk_act, 2 * hd + 1)
                A(EX[:, hd, :], EX[:, hd, :], ACT.Ln, bias=1.0).then_inc(gk_act, 1)
            act.preload_act_table_set("exp_and_others")

            with act.Fori(0, 2) as i:
                for t in range(3):
                    n, wn = At(N_MERGE1 + 6 + 3 * t, i, 9), At(W_MERGE1 + 4 + 2 * t, i, 6)
                    used = wn + (-3)
                    act.wait_ge(g_free[used.slot], used.read)
                    gate_tanh(wn, (2 + t) % 3, n, KT + 3 * i + t + 2)
                    for s in (3, 4, 5):
                        hi(n + s)

            def gla_exps(p):
                act.wait_ge(sems["gla_t"], last("gla_t", p))
                A(EX[:, 0, :], TB[:, 0, :], ACT.Exp, scale=1 / GATE_NORM)
                A(EX[:, 1, :], TB[:, 0, :], ACT.Exp, scale=-1 / GATE_NORM)
                A(EX[:, 2, :], BB[:, p, :], ACT.Exp, scale=1 / GATE_NORM)
                A(EX[:, 3, :], TB[:, 1, :], ACT.Exp, scale=1 / GATE_NORM)
                act.wait_ge(sems["gla_chain"], last("gla_chain", p - 1))
                b_last = BB[:, p, :].rearrange("p (c t) -> p c t", t=CH)[:, :, CH - 1]
                inc(A(EL[:], b_last, ACT.Exp, scale=1 / GATE_NORM), "gla_exp")

            def gla_proj(p, n, wn, inner):
                act.wait_ge(slab_done, n.value + 1)
                act.wait_ge(sems["gla_qt"], last("gla_qt", p - 1))
                nc.scalar.copy(QR[:], G[:, wn.slot, :]).then_inc(g_free[wn.slot], 1)
                hi(n + 3)
                if inner is not None:
                    act.wait_ge(sems["gla_kt_turned"], after("gla_kt_turned", inner))
                    inc(nc.scalar.copy(KK[:].rearrange("p j c -> p (j c)"), I34[:, 0:T]), "gla_kt_copied")
                gla_exps(p)
                act.wait_ge(slab_done, n.value + 3)
                act.wait_ge(sems["gla_o_done"], last("gla_o_done", p - 1))
                for s in range(2):
                    nc.scalar.copy(GV[:, 2 * s:2 * s + 2, :].rearrange("p j c -> p (j c)"),
                                   G[:, (wn + 1 + s).slot, :]).then_inc(g_free[(wn + 1 + s).slot], 1)
                hi(n + 4)
                hi(n + 5)
                if inner is not None:
                    gla_squares(inner)
                act.wait_ge(slab_done, n.value + 4)
                hi(n + 6)
                act.wait_ge(slab_done, n.value + 6)
                for s in range(2):
                    inc(A(GTH[:, s, :], G[:, (wn + 4 + s).slot, :], ACT.Tanh, scale=0.5), "gla_r_tanh")
                hi(n + 7)
                hi(n + 8)
                if inner is not None:
                    evict_hi(I34, GH, 2 * inner, gla_norm_cols, "gla_turned", inner, "gla_hi")

            def gla_squares(hd):
                act.wait_ge(sems["gla_o_done"], after("gla_o_done", hd))
                squares(lambda j: I01[:, j * 256:(j + 1) * 256], gla_dump, gss4, "gla_squares", hd)

            for p in range(HG):
                gla_proj(p, At(N_GLA + 6 * p), At(W_GLA + 6 * p), p - 1 if p else None)

            def load_bias(hd):
                s = hd % 2
                if hd >= 2:
                    act.wait_ge(sems["att_scored"], 16 * ((hd - 2) // 4 + 1) + 4 * ((hd - 2) % 4) + 4)
                else:
                    act.wait_ge(bias_masked, s + 1)
                act.dma_start(bias[0:CH, s, 0:T - CH], a["rel"][hd, 0:CH, 0:T - CH]).then_inc(bias_landed[s], 16)
                act.dma_start(bias[CH:P, s, :], a["rel"][hd, CH:P, :]).then_inc(bias_landed[s], 16)

            def att_out(q, t, n, wn):
                act.wait_ge(slab_done, n.value + t + 1)
                par, kind, f = q % 2, t % 2, t // 2
                act.wait_ge(sems["att_pv"], last("att_pv", q - 2) if q >= 2 else PER["att_pv"])
                dst = (AQ, AK)[kind][par][:, f, :]
                if kind == 0:
                    ins = nc.scalar.mul(dst, G[:, (wn + t).slot, :], ATT_SCALE)
                else:
                    ins = nc.scalar.copy(dst, G[:, (wn + t).slot, :])
                ins.then_inc(g_free[(wn + t).slot], 1)

            def att_v(q, n, wn):
                act.wait_ge(slab_done, n.value + 6)
                act.wait_ge(sems["att_pv"], last("att_pv", q - 1))
                for s in range(2):
                    nc.scalar.copy(AV[:, 2 * s:2 * s + 2, :].rearrange("p j c -> p (j c)"),
                                   G[:, (wn + 4 + s).slot, :]).then_inc(g_free[(wn + 4 + s).slot], 1)
                hi(n + 7)
                hi(n + 8)

            def att_exp(q, e):
                act.wait_ge(sems["att_neg"], after("att_neg", q, e))
                for i in range(TT):
                    o = P_OFF[i]
                    ins = A(PR[:, o:o + (i + 1) * P], PR[:, o:o + (i + 1) * P], ACT.Exp, bias=ngm[:, i:i + 1],
                            accum_out=rs[:, i:i + 1])
                inc(ins, "att_p")

            def att_pt(q, e):
                act.wait_ge(sems["att_turned"], after("att_turned", q, e))
                act.wait_ge(sems["att_pv"], after("att_pv", q, e - 1))
                inc(nc.scalar.copy(PT[:, 0:T], I34[:, 0:T]), "att_pt_a")

            hd = HG - 1
            n, wn = At(N_ATT), At(W_ATT)
            load_bias(0)
            load_bias(1)
            att_out(0, 0, n, wn)
            act.wait_ge(sems["gla_kt_turned"], after("gla_kt_turned", hd))
            inc(nc.scalar.copy(KK[:].rearrange("p j c -> p (j c)"), I34[:, 0:T]), "gla_kt_copied")
            hi(n + 3)
            att_out(0, 1, n, wn)
            hi(n + 4)
            att_out(0, 2, n, wn)
            hi(n + 5)
            gla_squares(hd)
            att_out(0, 3, n, wn)
            hi(n + 6)
            evict_hi(I34, GH, 2 * hd, gla_norm_cols, "gla_turned", hd, "gla_hi")
            att_v(0, n, wn)

            def merge2_part(nt, kind, n, wn, ahead=True):
                if kind in (0, 2):
                    if not isinstance(nt, int) or nt:
                        act.wait_ge(m_final if kind else m_sum, nt)
                    gate_tanh(wn, kind // 2, n, kind * KT + nt)
                if kind == 3:
                    act.wait_ge(m_final, nt + 1)
                    A(MH[:, bass.ds(nt, 1), :].rearrange("p a t -> p (a t)"),
                      merged[:, bass.ds(nt, 1), :].rearrange("p a t -> p (a t)"), ACT.Copy,
                      scale=0.5).then_inc(mh_ready, 1)
                if ahead:
                    hi(n + 3)

            for q in range(NQ):
                n, wn = At(N_ATT + 6 * (q + 1)), At(W_ATT + 6 * (q + 1))
                for e in range(4):
                    att_exp(q, e)
                    if 4 * q + e + 2 < 16:
                        load_bias(4 * q + e + 2)
                    if q + 1 < NQ:
                        att_out(q + 1, e, n, wn)
                        if e == 2:
                            hi(n + 5)
                    att_pt(q, e)
                    if q + 1 < NQ:
                        if e != 2:
                            hi(n + e + 3)
                    else:
                        merge2_part(*MERGE2_HEAD[e], At(N_MERGE2 + e), At(W_MERGE2 + e))
                if q + 1 < NQ:
                    att_v(q + 1, n, wn)
                else:
                    merge2_part(*MERGE2_HEAD[4], At(N_MERGE2 + 4), At(W_MERGE2 + 4))
                evict_hi(I34, AH, 2 * q, (1.0, 1.0), "att_o_turned", q, "att_hi")

            hi(At(N_MERGE2 + 8))
            merge2_part(*MERGE2_HEAD[6], At(N_MERGE2 + 6), None)
            merge2_part(*MERGE2_HEAD[5], At(N_MERGE2 + 5), At(W_MERGE2 + 5), False)
            merge2_part(*MERGE2_HEAD[7], At(N_MERGE2 + 7), None)
            with act.Fori(0, 2) as i:
                for k in range(12):
                    merge2_part(3 * i + k // 4 + 2, k % 4, At(N_MERGE2 + 8 + k, i, 12), At(W_MERGE2 + 8 + k, i, 12))
            for m in range(KT):
                raw_hi(m, 3)
                hi(At(N_OUT + m + 3))
                square(m, 2, m % 2)
            ffn(1)
            store()

        @block.vector
        def _(dve):
            for name, k in ROUND["vector"].items():
                dve.sem_inc(sems[name], k)
            dve.sem_inc(hid_ready, HID0)
            dve.sem_inc(gate_scaled, GATE0)
            dve.sem_inc(h_updated, RES0)
            dve.sem_inc(acc_updated, RES0 + POOL_SQUARES)
            V = nc.vector

            def tile_of(ap, k):
                return ap[:, bass.ds(k, 1), :].rearrange("p a t -> p (a t)")

            def lo(n):
                if isinstance(n.value, int) and n.value >= N_SLABS:
                    return
                dve.wait_ge(split_hi, n.value + 1)
                V.tensor_tensor(WL[:, n.slot, :], RAW[:, n.slot, :], WH[:, n.slot, :].bitcast(F32),
                                ALU.subtract).then_inc(split_lo, 1)

            def accumulate(m, k, slot):
                dve.wait_ge(squared, 8 * k + m + 1)
                dve.wait_ge(acc_updated, RES0 + 8 * k + m)
                V.tensor_tensor(acc[:], acc[:], sq[:, slot, :], ALU.add).then_inc(acc_updated, 1)

            def clear_acc(k):
                V.memset(acc[:], 0.0).then_inc(acc_clear, 1)
                dve.wait_ge(acc_clear, k + 1)

            def raw_lo(m, stage):
                dve.wait_ge(uh_ready, 8 * stage + m + 1)
                col = (C_N1, C_NM, None, C_N2)[stage]
                V.scalar_tensor_tensor(tile_of(UL, m), tile_of(h, m), cst[:, bass.ds(col + m, 1)],
                                       tile_of(UH, m).bitcast(F32), ALU.mult, ALU.subtract).then_inc(ul_ready, 1)

            def norm_rms(k):
                dve.wait_ge(norm_sums, k + 1)
                V.tensor_scalar(var4[:], I2[:, 0:TT], 1.0 / D, EPS, ALU.mult, ALU.add).then_inc(norm_var, 1)
                dve.wait_ge(norm_rstd, k + 1)
                V.tensor_tensor(diag[:], ident[:].unsqueeze(1).to_broadcast([P, TT, P]), bc(rstd4[:], P),
                                ALU.mult).then_inc(norm_diag, 1)

            def take_rms(k):
                dve.wait_ge(norm_bc, k + 1)
                V.tensor_copy(rms[:], I34[:, 0:T]).then_inc(rms_ready, 1)
                dve.wait_ge(rms_ready, k + 1)

            def residual(m, k, n, bank, scale):
                dve.wait_ge(slab_done, n.value + 1)
                V.scalar_tensor_tensor(tile_of(h, m), I01[:, bank * T:(bank + 1) * T], scale, tile_of(h, m),
                                       ALU.mult, ALU.add).then_inc(h_updated, 1)

            def ffn(f):
                n0, nd = (N_FFN1, N_DOWN1) if f == 0 else (N_FFN2, N_DOWN2)

                def tile(ft, n, t):
                    if isinstance(ft, int):
                        norm_rms(2 * f)
                        lo(n + 3)
                        take_rms(2 * f)
                    dve.wait_ge(slab_done, n.value + 1)
                    V.tensor_tensor(hid[:, t, :], G[:, n.slot, :], rms[:], ALU.mult).then_inc(gate_scaled, 1)
                    if not isinstance(ft, int):
                        lo(n + 3)
                    dve.wait_ge(gate_rms, FT * f + ft + 1)
                    dve.wait_ge(slab_done, n.value + 2)
                    V.tensor_tensor(hid[:, t, :], G[:, (n + 1).slot, :], hid[:, t, :],
                                    ALU.mult).then_inc(hid_ready, 1)
                    dve.wait_ge(hh_ready, FT * f + ft + 1)
                    V.tensor_tensor(tile_of(HL, ft), hid[:, t, :], tile_of(HH, ft).bitcast(F32),
                                    ALU.subtract).then_inc(hl_ready, 1)
                    lo(n + 4)

                tile(0, At(n0), 0)
                with dve.Fori(0, FT // 3) as i:
                    for t in range(3):
                        tile(3 * i + t + 1, At(n0 + 2 * t + 2, i, 6), (t + 1) % 3)
                k = 1 if f == 0 else 3
                clear_acc(k)

                def down(m, n, t):
                    lo(n + 3)
                    lo(n + 4)
                    residual(m, k, n + 2, t, 0.5)
                    if f == 0:
                        raw_lo(m, 1)
                    lo(n + 5)
                    accumulate(m, k, t)

                with dve.Fori(0, KT // 2 - 1) as i:
                    for t in range(2):
                        down(2 * i + t, At(nd + 3 * t, i, 6), t)
                for m in (KT - 2, KT - 1):
                    down(m, At(nd + 3 * m), m % 2)

            def dt_logits():
                v, size = dtw[:, 0, :], dtw[:, 1, :]
                dve.wait_ge(dt_pe, 1)
                V.tensor_tensor(v.rearrange("p (j h) -> p j h", h=HS),
                                I01[:, 0:128].rearrange("p (j h) -> p j h", h=HS),
                                over_tiles(cst[:, C_DTB:C_DTB + HS]), ALU.add).then_inc(dt_dve, 1)
                dve.wait_ge(dt_dve, 1)
                V.scalar_tensor_tensor(size, v, -1.0, v, ALU.mult, ALU.max).then_inc(dt_dve, 1)

            def dt_reciprocal():
                dve.wait_ge(dt_act, 1)
                V.tensor_scalar(dtw[:, 3, :], dtw[:, 2, :], 2.0, None, ALU.add).then_inc(dt_dve, 1)
                dve.wait_ge(dt_dve, 3)
                V.reciprocal(dtw[:, 5, :], dtw[:, 3, :]).then_inc(dt_dve, 1)

            def dt_to_end():
                dve.wait_ge(dt_act, 6)
                te = SC[:, 8:12, :].rearrange("p j h -> p (j h)")
                V.tensor_tensor(te, te, SC[:, 4:8, :].rearrange("p j h -> p (j h)"), ALU.mult).then_inc(dt_dve, 1)
                V.memset(SS[:, 0, :], 0.0).then_inc(dt_dve, 1)
                dve.wait_ge(dt_dve, 6)

            def raw_evict(t, n, wn):
                dve.wait_ge(slab_done, n.value + 1)
                V.tensor_tensor(XT[:, t, :], G[:, wn.slot, :], rms[:], ALU.mult).then_inc(g_free[wn.slot], 1)

            def norm_mixer():
                def scaled(m):
                    if m >= 3:
                        dve.wait_ge(ul_ready, 16 + m - 2)
                    V.scalar_tensor_tensor(ut[:, m % 3, :], h[:, m, :], cst[:, C_NM + m:C_NM + m + 1], rms[:],
                                           ALU.mult, ALU.mult).then_inc(ut_ready, 1)

                n, wn = At(N_SSM), At(W_SSM)
                norm_rms(1)
                lo(At(N_SMALL + 3))
                conv_consts(0)
                take_rms(1)
                V.tensor_tensor(dtv[:], G[:, 0, :], rms[:], ALU.mult).then_inc(g_free[0], 1)
                scaled(0)
                scaled(1)
                raw_evict(0, n, wn)
                lo(At(N_SMALL + 4))
                for m in range(2, KT):
                    scaled(m)
                    if m < 5:
                        conv_taps(0, 0, n, wn, (m - 1,))
                raw_evict(1, n + 1, wn + 1)
                lo(At(N_SMALL + 5))

            def conv_consts(p):
                dve.wait_ge(sems["conv_begun"], last("conv_begun", p - 1))
                inc(V.tensor_scalar(gconv[:], cst[:, bass.ds(C_CONV + 20 * p, 20)], 0.5, None, ALU.mult), "conv_const")
                dve.wait_ge(sems["conv_const"], after("conv_const", p))

            def group_scalars(g):
                inc(V.tensor_copy(gsc[:], SC[:, :, bass.ds(HPG * g, HPG)]), "group_const")
                dve.wait_ge(sems["group_const"], after("group_const", g))
                dve.wait_ge(sems["intra_done"], last("intra_done", g - 1))
                da = gsc[:, 0:4, :].rearrange("p j r -> p (j r)")
                inc(V.tensor_tensor(M[:].rearrange("p j r t -> p (j r) t"), bc(da, CH),
                                    causal[:].unsqueeze(1).to_broadcast([P, TT * HPG, CH]), ALU.mult), "da_masked")

            def group_norm(g):
                dve.wait_ge(sems["ssm_hi"], last("ssm_hi", g - 1))
                dve.wait_ge(sems["ssm_lo"], last("ssm_lo", g - 1))
                inc(V.tensor_copy(ggrp[:], cst[:, bass.ds(C_GRP + 6 * g, 6)]), "group_norm")

            taps_n = [0]
            taps_base = [0]

            def conv_taps(p, t, n, wn, taps_back=(1, 2, 3)):
                raw = isinstance(p, int) and t < 2
                cv, src = CV[:, t % 2, :], XT[:, t, :] if raw else G[:, wn.slot, :]
                dve.wait_ge(sems["conv_begun"], after("conv_begun", p, t))
                for back in taps_back:
                    ins = V.scalar_tensor_tensor(cv[:, back:T], src[:, 0:T - back],
                                                 gconv[:, 5 * t + 3 - back:5 * t + 4 - back], cv[:, back:T],
                                                 ALU.mult, ALU.add)
                    if back < 3:
                        ins.then_inc(taps, 1)
                        taps_n[0] += 1
                        dve.wait_ge(taps, taps_base[0] + taps_n[0])
                if back == 3:
                    ins.then_inc(raw_taps if raw else g_free[wn.slot], 1)

            def conv_silu(p, t):
                dve.wait_ge(sems["conv_tanh"], after("conv_tanh", p, t))
                if t < 3:
                    dve.wait_ge(sems["cb_done" if t == 2 else "xb_turned"],
                                last("cb_done" if t == 2 else "xb_turned", p - 1))
                else:
                    dve.wait_ge(sems["inter_done"], last("inter_done", p - 1))
                dst = (XT[:, 0, :], XT[:, 1, :], BT[:], CT[:])[t]
                inc(V.scalar_tensor_tensor(dst, TH[:, t % 2, :], 1.0, CV[:, t % 2, :], ALU.add, ALU.mult), "conv_done")

            def z_silu(p, wn):
                for s in range(2):
                    dve.wait_ge(sems["z_tanh"], after("z_tanh", p, s))
                    V.scalar_tensor_tensor(ZS[:, 2 * s:2 * s + 2, :].rearrange("p j c -> p (j c)"), TH[:, s, :], 1.0,
                                           G[:, (wn + s).slot, :], ALU.add,
                                           ALU.mult).then_inc(g_free[(wn + s).slot], 1)

            def rows(k):
                return bc(gsc[:, 4 * k:4 * k + 4, :].rearrange("p j r -> p (j r)"), CH)

            def heads(ap):
                return ap.rearrange("p (q c) -> p q c", c=CH)

            def ssm_x(g):
                dve.wait_ge(sems["x_copied"], after("x_copied", g))
                dve.wait_ge(sems["intra_done"], last("intra_done", g - 1))
                inc(V.tensor_tensor(XDT[:].rearrange("p j (r c) -> p (j r) c", c=CH), heads(XD[:].rearrange("p j c -> p (j c)")), rows(1),
                                    ALU.mult), "xdt_ready")
                inc(V.tensor_tensor(XTE[:].rearrange("p j (r c) -> p (j r) c", c=CH), heads(XD[:].rearrange("p j c -> p (j c)")), rows(2),
                                    ALU.mult), "xte_ready")

            def ssm_m(g):
                dve.wait_ge(sems["cb_done"], after("cb_done", g))
                inc(V.tensor_tensor(CBM[:], I2[:, 0:256].rearrange("p (j t) -> p j t", t=CH),
                                    causal[:].unsqueeze(1).to_broadcast([P, TT, CH]), ALU.mult), "cb_masked")
                dve.wait_ge(sems["cb_masked"], after("cb_masked", g))
                dve.wait_ge(sems["decay_exp"], after("decay_exp", g))
                inc(V.tensor_tensor(M[:], M[:], CBM[:].unsqueeze(2).to_broadcast([P, TT, HPG, CH]), ALU.mult),
                    "m_ready")

            def ssm_chain(g):
                dve.wait_ge(sems["inter_done"], last("inter_done", g - 1))
                dve.wait_ge(sems["ssm_squares"], last("ssm_squares", g - 1))
                k = 0
                for c in range(7):
                    u = update(c)
                    dve.wait_ge(sems["u_done"], after("u_done", g, 0 if c < 4 else 1))
                    if c == 0:
                        inc(V.tensor_copy(SS[:, 1, :], u), "ssm_chain")
                        k += 1
                    else:
                        dve.wait_ge(sems["ssm_chain"], after("ssm_chain", g, k - 1))
                        inc(V.tensor_tensor(heads(ST[:]), heads(SS[:, c, :]), bc(gsc[:, 16 + c, :], CH), ALU.mult),
                            "ssm_chain")
                        k += 1
                        dve.wait_ge(sems["ssm_chain"], after("ssm_chain", g, k - 1))
                        inc(V.tensor_tensor(SS[:, c + 1, :], ST[:], u, ALU.add), "ssm_chain")
                        k += 1
                assert k == PER["ssm_chain"]

            def ssm_y(g):
                dve.wait_ge(sems["inter_done"], after("inter_done", g))
                dve.wait_ge(sems["ssm_turned"], last("ssm_turned", g - 1))
                yf = Y[:].rearrange("p j c -> p (j c)")
                inc(V.tensor_tensor(heads(yf), heads(I34[:]), rows(3), ALU.mult), "ssm_y")
                dve.wait_ge(sems["ssm_y"], after("ssm_y", g, 0))
                dve.wait_ge(sems["intra_done"], after("intra_done", g))
                inc(V.tensor_tensor(yf, yf, I01[:], ALU.add), "ssm_y")
                dve.wait_ge(sems["ssm_y"], after("ssm_y", g, 1))
                dve.wait_ge(sems["xd_ready"], after("xd_ready", g))
                inc(V.tensor_tensor(yf, yf, XD[:].rearrange("p j c -> p (j c)"), ALU.add), "ssm_y")
                dve.wait_ge(sems["ssm_y"], after("ssm_y", g, 2))
                inc(V.tensor_tensor(yf, yf, ZS[:].rearrange("p j c -> p (j c)"), ALU.mult), "ssm_y")

            def ssm_scale(g):
                dve.wait_ge(sems["ssm_squares"], last("ssm_squares", g))
                inc(V.tensor_scalar(var4[:], ss4[:], 1.0 / 256, 4 * EPS, ALU.mult, ALU.add), "ssm_var")
                dve.wait_ge(sems["ssm_rstd"], last("ssm_rstd", g))
                for j in range(TT):
                    inc(V.tensor_scalar(Y[:, j, :], Y[:, j, :], rstd4[:, j:j + 1], None, ALU.mult), "ssm_scaled")

            def evict_lo(src, dH, dL, k0, scale, hi_name, g, name):
                for f in range(2):
                    dve.wait_ge(sems[hi_name], after(hi_name, g, f))
                    inc(V.scalar_tensor_tensor(tile_of(dL, k0 + f), src[:, f * T:(f + 1) * T], scale[f],
                                               tile_of(dH, k0 + f).bitcast(F32), ALU.mult, ALU.subtract), name)

            def take_output(wn, gate_wn, n, slot, nt):
                dve.wait_ge(g_free[gate_wn.slot], gate_wn.read)
                dve.wait_ge(slab_done, n.value + 1)
                dst = gate_th[:, slot, :] if nt is None else tile_of(merged, nt)
                V.scalar_tensor_tensor(dst, gate_th[:, slot, :], 1.0, G[:, wn.slot, :],
                                       ALU.add, ALU.mult).then_inc(g_free[wn.slot], 1)

            def merge2_part(nt, kind, n, wn, gate_wn):
                if kind in (1, 3):
                    take_output(wn, gate_wn, n, kind // 2, None)
                    dve.wait_ge(g_free[wn.slot], wn.read)
                    if kind == 3:
                        dve.wait_ge(m_sum, nt + 1)
                    V.tensor_tensor(tile_of(merged, nt), tile_of(merged, nt), gate_th[:, kind // 2, :],
                                    ALU.add).then_inc(m_final if kind == 3 else m_sum, 1)
                if kind == 3:
                    dve.wait_ge(mh_ready, nt + 1)
                    V.scalar_tensor_tensor(tile_of(ML, nt), tile_of(merged, nt), 0.5, tile_of(MH, nt).bitcast(F32),
                                           ALU.mult, ALU.subtract).then_inc(ml_ready, 1)
                lo(n + 3)

            def merge2_head(k):
                nt, kind = MERGE2_HEAD[k]
                gate = MERGE2_HEAD.index((nt, kind - kind % 2))
                merge2_part(nt, kind, At(N_MERGE2 + k), At(W_MERGE2 + k), At(W_MERGE2 + gate))

            clear_acc(0)
            dve.wait_ge(cst_landed, 16)
            V.tensor_scalar(half_gate_bias[:], cst[:, C_GATE:C_GATE + 3 * KT], 0.5, None,
                            ALU.mult).then_inc(half_bias, 1)
            lo(At(0))
            for m in range(KT):
                raw_lo(m, 0)
            lo(At(1))
            for m in range(POOL_SQUARES, KT):
                accumulate(m, 0, m % 2)
            lo(At(2))
            dve.wait_ge(consts, N_CONSTS)
            ffn(0)
            norm_mixer()

            def ssm_first():
                n, wn = At(N_SSM), At(W_SSM)
                dt_logits()
                conv_silu(0, 0)
                conv_taps(0, 1, n + 1, wn + 1)
                dt_reciprocal()
                conv_taps(0, 2, n + 2, wn + 2)
                lo(n + 5)
                conv_silu(0, 1)
                conv_silu(0, 2)
                conv_taps(0, 3, n + 3, wn + 3)
                lo(n + 6)
                conv_silu(0, 3)
                dve.wait_ge(lr_split, 1)
                V.tensor_tensor(LR[64:LR_ROWS, :], dtv[64:LR_ROWS, :], LR[64:LR_ROWS, :].bitcast(F32),
                                ALU.subtract).then_inc(lr_ready, 1)
                dt_to_end()
                group_scalars(0)
                z_silu(0, wn + 4)
                lo(n + 7)
                lo(n + 8)

            def ssm_round(p, n, wn, inner):
                conv_consts(p)
                group_norm(inner)
                for t in range(4):
                    conv_taps(p, t, n + t, wn + t)
                    lo(n + t + 3)
                    if t == 0:
                        ssm_x(inner)
                    if t == 1:
                        ssm_m(inner)
                        ssm_chain(inner)
                    if t == 3:
                        ssm_y(inner)
                    conv_silu(p, t)
                ssm_scale(inner)
                z_silu(p, wn + 4)
                lo(n + 7)
                evict_lo(I01, SH, SL, 2 * inner, ssm_norm_cols, "ssm_hi", inner, "ssm_lo")
                group_scalars(p)
                lo(n + 8)

            ssm_norm_cols = [ggrp[:, f:f + 1] for f in range(2)]
            gla_norm_cols = [cst[:, C_GN + f:C_GN + f + 1] for f in range(2)]
            ssm_first()
            with dve.Fori(0, NG - 1) as i:
                taps_n[0] = 0
                taps_base[0] = 8 * i + 8
                ssm_round(i + 1, At(N_SSM + 6, i, 6), At(W_SSM + 6, i, 6), i)
            g = NG - 1
            n, wn = At(N_MERGE1), At(W_MERGE1)
            group_norm(g)
            lo(n + 3)
            ssm_x(g)
            ssm_m(g)
            ssm_chain(g)
            lo(n + 4)
            ssm_y(g)
            lo(n + 5)
            ssm_scale(g)
            evict_lo(I01, SH, SL, 2 * g, ssm_norm_cols, "ssm_hi", g, "ssm_lo")
            lo(n + 6)
            take_output(wn + 1, wn, n + 4, 0, 0)
            lo(n + 7)
            take_output(wn + 3, wn + 2, n + 5, 1, 1)
            lo(n + 8)

            dve.wait_ge(gk_pe, 1)
            for hd in range(HG):
                src = (I01[:, 0:T], I01[:, T:], I34[:, 0:T], I34[:, T:])[hd]
                V.tensor_scalar(BB[:, hd, :], src, cst[:, C_GB + hd:C_GB + hd + 1], None, ALU.add).then_inc(gk_dve, 1)
                dve.wait_ge(gk_dve, 2 * hd + 1)
                V.scalar_tensor_tensor(EX[:, hd, :], BB[:, hd, :], -1.0, BB[:, hd, :], ALU.mult,
                                       ALU.max).then_inc(gk_dve, 1)

            with dve.Fori(0, 2) as i:
                for t in range(3):
                    n, wn = At(N_MERGE1 + 6 + 3 * t, i, 9), At(W_MERGE1 + 4 + 2 * t, i, 6)
                    lo(n + 3)
                    lo(n + 4)
                    take_output(wn + 1, wn, n + 2, (2 + t) % 3, 3 * i + t + 2)
                    lo(n + 5)

            k = 2 * HG
            assert k == GK_EVICTED
            dve.wait_ge(gk_pool, 2)
            for hd in range(HG):
                dve.wait_ge(gk_act, 2 * hd + 2)
                V.scalar_tensor_tensor(TB[:, hd % 2, :], BB[:, hd, :], 0.0, EX[:, hd, :], ALU.min,
                                       ALU.subtract).then_inc(gk_dve, 1)
                k += 1
                dve.wait_ge(gk_dve, k)
                V.tensor_tensor_scan(BB[:, hd, :], RM[:], TB[:, hd % 2, :], 0.0, ALU.mult, ALU.add).then_inc(gk_dve, 1)
                k += 1
                dve.wait_ge(gk_dve, k)
            V.memset(GS[:, 0, :], 0.0).then_inc(gk_dve, 1)

            def chunks(ap):
                return ap.rearrange("p (c t) -> p c t", t=CH)

            def gla_proj(p, n, wn, inner):
                dve.wait_ge(sems["gla_exp"], last("gla_exp", p - 1))
                b3 = chunks(BB[:, p, :])
                inc(V.tensor_tensor(chunks(TB[:, 0, :]), b3, bc(b3[:, :, CH // 2], CH), ALU.subtract), "gla_t")
                inc(V.tensor_tensor(chunks(TB[:, 1, :]), bc(b3[:, :, CH - 1], CH), b3, ALU.subtract), "gla_t")
                lo(n + 3)
                if inner is not None:
                    gla_a_chain(inner)
                dve.wait_ge(sems["gla_exp"], after("gla_exp", p))
                dve.wait_ge(g_free[wn.slot], wn.read)
                dve.wait_ge(sems["gla_a_done"], last("gla_a_done", p - 1))
                inc(V.scalar_tensor_tensor(QH[:], QR[:], GLA_SCALE, EX[:, 0, :], ALU.mult, ALU.mult), "gla_qh")
                dve.wait_ge(sems["gla_o_done"], last("gla_o_done", p - 1))
                inc(V.scalar_tensor_tensor(QT[:], QR[:], GLA_SCALE, EX[:, 2, :], ALU.mult, ALU.mult), "gla_qt")
                lo(n + 4)
                lo(n + 5)
                if inner is not None:
                    gla_out(inner)
                dve.wait_ge(slab_done, n.value + 4)
                dve.wait_ge(sems["gla_kt_turned"], last("gla_kt_turned", p - 1))
                inc(V.tensor_tensor(KH[:], G[:, (wn + 3).slot, :], EX[:, 1, :], ALU.mult), "gla_kh")
                V.tensor_tensor(KT_[:], G[:, (wn + 3).slot, :], EX[:, 3, :], ALU.mult).then_inc(g_free[(wn + 3).slot], 1)
                lo(n + 6)
                dve.wait_ge(sems["gla_o_ready"], last("gla_o_ready", p - 1))
                for s in range(2):
                    dve.wait_ge(sems["gla_r_tanh"], after("gla_r_tanh", p, s))
                    V.scalar_tensor_tensor(GR[:, 2 * s:2 * s + 2, :].rearrange("p j c -> p (j c)"), GTH[:, s, :], 1.0,
                                           G[:, (wn + 4 + s).slot, :], ALU.add,
                                           ALU.mult).then_inc(g_free[(wn + 4 + s).slot], 1)
                lo(n + 7)
                lo(n + 8)
                if inner is not None:
                    evict_lo(I34, GH, GL, 2 * inner, gla_norm_cols, "gla_hi", inner, "gla_lo")

            def gla_a_chain(hd):
                dve.wait_ge(sems["gla_a_done"], after("gla_a_done", hd))
                inc(V.tensor_tensor(GA[:], I2[:, 0:256].rearrange("p (j t) -> p j t", t=CH),
                                    causal[:].unsqueeze(1).to_broadcast([P, TT, CH]), ALU.mult), "gla_a_masked")
                for c in range(7):
                    u = update(c)
                    dve.wait_ge(sems["gla_u_done"], after("gla_u_done", hd, 0 if c < 4 else 1))
                    if c:
                        dve.wait_ge(sems["gla_chain"], after("gla_chain", hd, c - 1))
                    inc(V.scalar_tensor_tensor(GS[:, c + 1, :], GS[:, c, :], EL[:, c:c + 1], u, ALU.mult, ALU.add),
                        "gla_chain")

            def gla_out(hd):
                dve.wait_ge(sems["gla_squares"], last("gla_squares", hd))
                inc(V.tensor_scalar(var4[:], gss4[:], 4.0 / 256, 4 * EPS, ALU.mult, ALU.add), "gla_var")
                dve.wait_ge(sems["gla_rstd"], last("gla_rstd", hd))
                dve.wait_ge(sems["gla_turned"], last("gla_turned", hd - 1))
                for j in range(TT):
                    inc(V.scalar_tensor_tensor(GO[:, j, :], I01[:, j * 256:(j + 1) * 256], rstd4[:, j:j + 1],
                                               GR[:, j, :], ALU.mult, ALU.mult), "gla_o_ready")

            for p in range(HG):
                gla_proj(p, At(N_GLA + 6 * p), At(W_GLA + 6 * p), p - 1 if p else None)
            def att_score(q, e):
                hd = 4 * q + e
                s = hd % 2
                dve.wait_ge(sems["att_s"], after("att_s", q, e))
                dve.wait_ge(bias_landed[s], 32 * (hd // 2 + 1))
                dve.wait_ge(bias_masked, s + 1)
                dve.wait_ge(sems["att_turned"], after("att_turned", q, e - 1))
                for k, i in enumerate((3, 2, 0, 1)):
                    src = {3: I01[:, 0:512], 2: I01[:, 512:896], 0: I01[:, 896:1024], 1: I2[:, 0:256]}[i]
                    o, wd = P_OFF[i], (i + 1) * P
                    inc(V.tensor_tensor_reduce(out=PR[:, o:o + wd], in0=src, in1=bias[:, s, T - wd:T], scale=1.0,
                                               scalar=-3.0e38, op0=ALU.add, op1=ALU.max,
                                               accum_out=mx[:, i:i + 1]), "att_scored")
                dve.wait_ge(sems["att_scored"], 16 * (q + 1) + 4 * e + 4)
                dve.wait_ge(sems["att_p"], after("att_p", q, e - 1))
                inc(V.tensor_scalar(ngm[:], mx[:], -1.0, None, ALU.mult), "att_neg")

            def att_pt(q, e):
                dve.wait_ge(sems["att_p"], after("att_p", q, e))
                dve.wait_ge(sems["att_o"], after("att_o", q, e - 1))
                inc(V.reciprocal(rc[:], rs[:]), "att_recip")
                dve.wait_ge(sems["att_turned"], after("att_turned", q, e))
                dve.wait_ge(sems["att_pv"], after("att_pv", q, e - 1))
                inc(V.tensor_copy(PT[:, T:2 * T], I34[:, T:2 * T]), "att_pt_b")
                inc(V.tensor_copy(PT[:, 2 * T:2 * T + 256], I2[:, 256:512]), "att_pt_b")

            def att_out(q, e):
                dve.wait_ge(sems["att_recip"], after("att_recip", q, e))
                if e == 0:
                    dve.wait_ge(sems["att_o_turned"], last("att_o_turned", q - 1))
                dve.wait_ge(sems["att_pv"], after("att_pv", q, e))
                inc(V.tensor_tensor(AO[:, :, e * CH:(e + 1) * CH],
                                    I01[:, 0:256].rearrange("p (j c) -> p j c", c=CH), bc(rc[:], CH), ALU.mult),
                    "att_o")

            hd = HG - 1
            lo(At(N_ATT + 3))
            gla_a_chain(hd)
            lo(At(N_ATT + 4))
            lo(At(N_ATT + 5))
            gla_out(hd)
            lo(At(N_ATT + 6))
            evict_lo(I34, GH, GL, 2 * hd, gla_norm_cols, "gla_hi", hd, "gla_lo")
            lo(At(N_ATT + 7))
            lo(At(N_ATT + 8))
            for q in range(NQ):
                n = At(N_ATT + 6 * (q + 1))
                for e in range(4):
                    att_score(q, e)
                    if q and e == 0:
                        evict_lo(I34, AH, AL, 2 * q - 2, (1.0, 1.0), "att_hi", q - 1, "att_lo")
                    if q + 1 < NQ and e == 2:
                        lo(n + 5)
                    att_pt(q, e)
                    if q + 1 < NQ:
                        if e != 2:
                            lo(n + e + 3)
                    else:
                        merge2_head(e)
                    att_out(q, e)
                if q + 1 < NQ:
                    lo(n + 7)
                    lo(n + 8)
                else:
                    merge2_head(4)
            evict_lo(I34, AH, AL, 2 * NQ - 2, (1.0, 1.0), "att_hi", NQ - 1, "att_lo")

            for k in range(5, 8):
                merge2_head(k)
            with dve.Fori(0, 2) as i:
                for k in range(12):
                    wn = At(W_MERGE2 + 8 + k, i, 12)
                    merge2_part(3 * i + k // 4 + 2, k % 4, At(N_MERGE2 + 8 + k, i, 12), wn, wn + (-(k % 2)))
            clear_acc(2)
            for m in range(KT):
                residual(m, 2, At(N_OUT + m), m % 2, 1.0)
                raw_lo(m, 3)
                lo(At(N_OUT + m + 3))
                accumulate(m, 2, m % 2)
            ffn(1)
            norm_rms(3)
            dve.wait_ge(norm_bc, 4)
            for m in range(KT):
                V.scalar_tensor_tensor(h[:, m, :], h[:, m, :], cst[:, C_NF + m:C_NF + m + 1], I34[:, 0:T],
                                       ALU.mult, ALU.mult).then_inc(out_ready, 1)


N_CONSTS = 11
DT_ABS, DA_READY = 2, 22
POOL_SQUARES = 4
GK_EVICTED = 2 * HG
P_OFF = {3: 0, 2: 512, 0: 896, 1: 1024}
PT_OFF = {0: 0, 1: 512, 3: 896, 2: 1024}
MAX_REL = 256


def fm_slabs(w):
    k = w.shape[0] // P
    return np.ascontiguousarray(w.reshape(k, P, -1, P).transpose(2, 1, 0, 3)).reshape(-1, P, k * P)


def tm_slabs(w):
    t = w.reshape(2, 4, P, -1, 256).transpose(3, 0, 2, 1, 4)
    return np.ascontiguousarray(t).reshape(-1, P, SLAB)


def down_slabs(w):
    t = fm_slabs(w)
    out = np.zeros((t.shape[0], 3, P, SLAB), np.float32)
    for c, (k0, k1) in enumerate(DOWN_K):
        out[:, c, :, 0:(k1 - k0) * P] = t[:, :, k0 * P:k1 * P]
    return out.reshape(-1, P, SLAB)


def interleave(*parts):
    return np.concatenate(parts, axis=1).reshape(-1, P, SLAB)


def lay_out(i):
    sizes = (512, 512, 1024, 1024, 16, 2048, 4096, 32, 1024, 1024, 1024, 3072)
    ends = np.cumsum(sizes)
    win = i["w_in"][0]
    q, k, v, r, lr, z, xbc, dt, aq, ak, av, gates = (win[:, e - s:e] for s, e in zip(sizes, ends))
    small = np.zeros((D, P), np.float32)
    for at in (0, 32, 64):
        small[:, at:at + 16] = lr
    small[:, LR_ROWS:P] = dt
    gate = fm_slabs(gates).reshape(3, KT, 1, P, SLAB)

    def rounds(s, n):
        return s.reshape(n, -1, P, SLAB)

    xb = fm_slabs(xbc)
    aq_s, ak_s = rounds(fm_slabs(aq), NQ), rounds(fm_slabs(ak), NQ)
    ws = fm_slabs(i["w_branch_ssm"][0]).reshape(KT, P, 2, SLAB).transpose(0, 2, 1, 3)
    merge1 = interleave(gate[1], ws)
    merge1[:6] = merge1[[0, 1, 3, 4, 2, 5]]
    merge2 = interleave(gate[0], rounds(fm_slabs(i["w_branch_gla"][0]), KT), gate[2],
                        rounds(fm_slabs(i["w_branch_attn"][0]), KT))
    merge2[:8] = merge2[[4 * nt + kind for nt, kind in MERGE2_HEAD]]
    stream = [
        interleave(rounds(fm_slabs(i["ffn1_w_gate"][0]), FT), rounds(fm_slabs(i["ffn1_w_up"][0]), FT)),
        down_slabs(i["ffn1_w_down"][0]),
        fm_slabs(small),
        interleave(rounds(xb[0:16], NG), rounds(xb[16:24], NG), rounds(xb[24:32], NG), rounds(tm_slabs(z), NG)),
        merge1,
        interleave(rounds(fm_slabs(q), HG), rounds(tm_slabs(v), HG), rounds(fm_slabs(k), HG), rounds(tm_slabs(r), HG)),
        interleave(aq_s[:, 0:1], ak_s[:, 0:1], aq_s[:, 1:2], ak_s[:, 1:2], rounds(tm_slabs(av), NQ)),
        merge2,
        fm_slabs(i["w_out"][0]),
        interleave(rounds(fm_slabs(i["ffn2_w_gate"][0]), FT), rounds(fm_slabs(i["ffn2_w_up"][0]), FT)),
        down_slabs(i["ffn2_w_down"][0]),
    ]
    slabs = np.concatenate(stream)
    assert slabs.shape[0] == N_SLABS, slabs.shape

    cst = np.zeros((P, NCST), np.float32)

    def cols(at, vec):
        cst[:, at:at + vec.size // P] = vec.reshape(-1, P).T

    cols(C_N1, i["ffn1_norm"][0])
    cols(C_NM, i["mix_norm"][0])
    cols(C_N2, i["ffn2_norm"][0])
    cols(C_NF, i["final_norm"])
    cols(C_GN, i["gla_norm"][0])
    cols(C_GB, i["gla_b_gk"][0])
    cols(C_GATE, i["gate_bias"][0])
    taps = np.concatenate([i["ssm_conv_w"][0], i["ssm_conv_b"][0][None]])
    taps = taps.reshape(5, 32, P).transpose(2, 1, 0)
    sn = i["ssm_norm"][0].reshape(NG, 2, P)
    for g in range(NG):
        for t, tile in enumerate((2 * g, 2 * g + 1, 16 + g, 24 + g)):
            cst[:, C_CONV + 20 * g + 5 * t:C_CONV + 20 * g + 5 * t + 5] = taps[:, tile]
        cst[:, C_GRP + 6 * g:C_GRP + 6 * g + 2] = sn[g].T
        cst[:, C_GRP + 6 * g + 2:C_GRP + 6 * g + 6] = i["ssm_D"][0][None, HPG * g:HPG * g + HPG]
    cst[:, C_ALOG:C_DTB] = i["ssm_A_log"][0][None]
    cst[:, C_DTB:] = i["ssm_dt_bias"][0][None]

    distance = np.arange(P)[:, None] + T - P - np.arange(T)[None, :]
    rel = np.ascontiguousarray(i["attn_rel_bias"][0][np.minimum(distance, MAX_REL) + MAX_REL].transpose(2, 0, 1))
    x = np.ascontiguousarray(i["x"][0].reshape(T, KT, P).transpose(2, 1, 0))
    return {"slabs": slabs, "cst": cst, "rel": rel, "x": x, "wgk": np.ascontiguousarray(i["gla_w_gk"][0])}


def kernel(**inputs):
    from concourse import bacc
    from concourse.bass_utils import run_bass_kernel_spmd

    arrays = lay_out({k: np.asarray(v) for k, v in inputs.items()})
    nc = bacc.Bacc("TRN2", target_bir_lowering=False, num_devices=1, dynamic_dma_scratch_size=1024)
    aps = {n: nc.dram_tensor(f"in_{n}", v.shape, mybir.dt.from_np(v.dtype), kind="ExternalInput").ap()
           for n, v in arrays.items()}
    out = nc.dram_tensor("out_y", (P, KT, T), F32, kind="ExternalOutput").ap()
    build(nc, aps, out)
    r = run_bass_kernel_spmd(nc, [{f"in_{n}": v for n, v in arrays.items()}], core_ids=[0])
    y = r.results[0]["out_y"]
    return np.ascontiguousarray(y.transpose(2, 1, 0)).reshape(1, T, D)
```
